# Optimizing a Trainium2 kernel written in Bass

```python
import jax, jax.numpy as jnp
from jax import lax
import numpy as np

D_MODEL = 1024
BATCH = 1
SEQ = 512
DEPTH = 1

W_BRANCH = D_MODEL
N_BRANCH = 3
POOL_WINDOWS = (2, 4, 8, 16)
N_POOL_GROUPS = len(POOL_WINDOWS)
POOL_GROUP = W_BRANCH // N_POOL_GROUPS
SHORT_CONV = 3
CONFORMER_CONV = 31
LN_EPS = 1e-5
ALPHA = (2 * DEPTH) ** 0.25
BETA = (8 * DEPTH) ** -0.25

SPLIT_SIZES = (
    W_BRANCH, W_BRANCH,
    W_BRANCH, W_BRANCH, W_BRANCH, W_BRANCH,
    W_BRANCH, W_BRANCH, W_BRANCH,
    N_BRANCH * D_MODEL,
)
IN_COLS = int(sum(SPLIT_SIZES))
SPLIT_IDX = [int(v) for v in np.cumsum(SPLIT_SIZES)[:-1]]


def layer_norm(x, g=None, b=None):
    x32 = x.astype(jnp.float32)
    mu = jnp.mean(x32, axis=-1, keepdims=True)
    var = jnp.mean(jnp.square(x32 - mu), axis=-1, keepdims=True)
    y = (x32 - mu) * lax.rsqrt(var + LN_EPS)
    if g is not None:
        y = y * g.astype(jnp.float32) + b.astype(jnp.float32)
    return y.astype(x.dtype)

def causal_dwconv(u, w, b):
    K, C = w.shape
    y = lax.conv_general_dilated(
        u, w[:, None, :].astype(u.dtype), window_strides=(1,),
        padding=[(K - 1, 0)], dimension_numbers=("NWC", "WIO", "NWC"),
        feature_group_count=C)
    return y + b

def causal_multiscale_pool(v):
    bsz, slen, _ = v.shape
    vg = v.reshape(bsz, slen, N_POOL_GROUPS, POOL_GROUP).astype(jnp.float32)
    cs = jnp.cumsum(vg, axis=1)
    t = jnp.arange(1, slen + 1, dtype=jnp.float32)
    outs = []
    for g, w in enumerate(POOL_WINDOWS):
        c_g = cs[:, :, g]
        lagged = jnp.pad(c_g, ((0, 0), (w, 0), (0, 0)))[:, :slen]
        cnt = jnp.minimum(t, float(w))[None, :, None]
        outs.append((c_g - lagged) / cnt)
    pooled = jnp.stack(outs, axis=2)
    return (pooled - vg).astype(v.dtype)

def hybrid_layer(x, c_act, w_ada, b_ada, w_in, b_in, pool_w, pool_scale, sc_w, sc_b,
                 cf_w, cf_b, cf_ln_g, cf_ln_b, w_branch, w_out, ln_g, ln_b):
    bsz, slen, _ = x.shape
    mod = (c_act @ w_ada + b_ada)[:, None, :]
    shift, scale, gate = jnp.split(mod, 3, axis=-1)
    u = layer_norm(x) * (1 + scale) + shift
    proj = u @ w_in + b_in
    a_v, a_g, b_b, b_c, b_h, b_g, c_a, c_b, c_g, merge = jnp.split(proj, SPLIT_IDX, axis=-1)

    pooled = causal_multiscale_pool(a_v)
    y_a = jnp.einsum("bsgi,gio->bsgo", pooled, pool_w).reshape(bsz, slen, W_BRANCH)
    y_a = y_a * pool_scale * jax.nn.silu(a_g)

    y_b = b_b * causal_dwconv(b_c * b_h, sc_w, sc_b) * jax.nn.silu(b_g)

    h_c = causal_dwconv(c_a * jax.nn.sigmoid(c_b), cf_w, cf_b)
    y_c = jax.nn.silu(layer_norm(h_c, cf_ln_g, cf_ln_b)) * jax.nn.silu(c_g)

    g_m = jax.nn.sigmoid(merge).reshape(bsz, slen, N_BRANCH, D_MODEL)
    m = (g_m[:, :, 0] * (y_a @ w_branch[0])
         + g_m[:, :, 1] * (y_b @ w_branch[1])
         + g_m[:, :, 2] * (y_c @ w_branch[2]))
    out = m @ w_out
    return layer_norm(ALPHA * x + gate * out, ln_g, ln_b)

def first_inputs(seed: int = 0) -> dict:
    key = jax.random.key(seed)
    ks = jax.random.split(key, 20)
    L, D, W = DEPTH, D_MODEL, W_BRANCH
    n = lambda k, shp, s: jax.random.normal(k, shp, jnp.float32) * s
    return {
        "x": n(ks[0], (BATCH, SEQ, D), 1.0),
        "c": n(ks[1], (BATCH, D), 1.0),
        "w_ada": n(ks[2], (L, D, 3 * D), 0.5 * D ** -0.5),
        "b_ada": n(ks[3], (L, 3 * D), 0.02),
        "w_in": n(ks[4], (L, D, IN_COLS), D ** -0.5),
        "b_in": n(ks[5], (L, IN_COLS), 0.02),
        "pool_w": n(ks[6], (L, N_POOL_GROUPS, POOL_GROUP, POOL_GROUP), POOL_GROUP ** -0.5),
        "pool_scale": 1.0 + n(ks[7], (L, W), 0.1),
        "sc_w": n(ks[8], (L, SHORT_CONV, W), SHORT_CONV ** -0.5),
        "sc_b": n(ks[9], (L, W), 0.02),
        "cf_w": n(ks[10], (L, CONFORMER_CONV, W), CONFORMER_CONV ** -0.5),
        "cf_b": n(ks[11], (L, W), 0.02),
        "cf_ln_g": 1.0 + n(ks[12], (L, W), 0.05),
        "cf_ln_b": n(ks[13], (L, W), 0.02),
        "w_branch": n(ks[14], (L, N_BRANCH, W, D), BETA * W ** -0.5),
        "w_out": n(ks[15], (L, D, D), BETA * D ** -0.5),
        "ln_g": 1.0 + n(ks[16], (L, D), 0.05),
        "ln_b": n(ks[17], (L, D), 0.02),
    }

def first_block(x, c, w_ada, b_ada, w_in, b_in, pool_w, pool_scale, sc_w, sc_b,
              cf_w, cf_b, cf_ln_g, cf_ln_b, w_branch, w_out, ln_g, ln_b):
    c_act = jax.nn.silu(c)
    for l in range(DEPTH):
        x = hybrid_layer(x, c_act, w_ada[l], b_ada[l], w_in[l], b_in[l], pool_w[l],
                         pool_scale[l], sc_w[l], sc_b[l], cf_w[l], cf_b[l],
                         cf_ln_g[l], cf_ln_b[l], w_branch[l], w_out[l], ln_g[l], ln_b[l])
    return x


DEPTH_2 = 2

N_MIXERS = 2
PLE_DIM = 256
D_FF = 4 * D_MODEL
EPS = 1e-6

HG_KDIM = 128
HG_HEADS = D_MODEL // HG_KDIM
HG_VDIM = D_MODEL // HG_HEADS
HG_QK = HG_HEADS * HG_KDIM
HG_V = HG_HEADS * HG_VDIM
HG_CHUNK = 64
N_HGRN = (DEPTH_2 + 1) // 2

MLA_HEADS = 16
MLA_Q_RANK = 384
MLA_KV_RANK = 256
MLA_NOPE = 128
MLA_ROPE = 64
MLA_V = 128
ROPE_BASE = 10000.0
Q_BLOCK = 128
N_MLA = DEPTH_2 // 2


def rms_norm(x, gain):
    xf = x.astype(jnp.float32)
    y = xf * lax.rsqrt(jnp.mean(xf * xf, axis=-1, keepdims=True) + EPS)
    return (y * gain.astype(jnp.float32)).astype(x.dtype)

def gla_chunk_scan(q, k, v, g):
    b, h, s, dk = q.shape
    dv = v.shape[-1]
    nc = s // HG_CHUNK

    def to_chunks(t):
        return jnp.moveaxis(t.reshape(b, h, nc, HG_CHUNK, t.shape[-1]), 2, 0)

    qc, kc, vc, gc = to_chunks(q), to_chunks(k), to_chunks(v), to_chunks(g)
    mask = jnp.tril(jnp.ones((HG_CHUNK, HG_CHUNK), dtype=bool))

    def step(state, inp):
        qi, ki, vi, gi = inp
        G = jnp.cumsum(gi.astype(jnp.float32), axis=-2)
        G_last = G[..., -1:, :]
        q_dec = qi * jnp.exp(G)
        k_inv = ki * jnp.exp(-G)
        k_end = ki * jnp.exp(G_last - G)
        attn = jnp.where(mask, jnp.einsum('bhik,bhjk->bhij', q_dec, k_inv), 0.0)
        o = (jnp.einsum('bhij,bhjv->bhiv', attn, vi)
             + jnp.einsum('bhik,bhkv->bhiv', q_dec, state))
        new_state = (jnp.exp(G_last[..., 0, :])[..., None] * state
                     + jnp.einsum('bhjk,bhjv->bhkv', k_end, vi))
        return new_state, o

    state0 = jnp.zeros((b, h, dk, dv), jnp.float32)
    _, o = lax.scan(step, state0, (qc, kc, vc, gc))
    return jnp.moveaxis(o, 0, 2).reshape(b, h, s, dv).astype(v.dtype)

def hgrn2_mixer(x, w_in, o_norm, w_out, lb):
    b, s, _ = x.shape
    proj = x @ w_in
    q, f_fw, f_bw, inp, gate = jnp.split(
        proj, [HG_QK, 2 * HG_QK, 3 * HG_QK, 3 * HG_QK + HG_V], axis=-1)

    def heads(t):
        return jnp.transpose(t.reshape(b, s, HG_HEADS, -1), (0, 2, 1, 3))

    q = heads(q) * (HG_KDIM ** -0.5)
    v = heads(inp)
    lbh = lb.astype(jnp.float32).reshape(HG_HEADS, 1, HG_KDIM)

    def gates(f_logit):
        f = lbh + (1.0 - lbh) * jax.nn.sigmoid(heads(f_logit).astype(jnp.float32))
        return 1.0 - f, jnp.log(f)

    k_f, g_f = gates(f_fw)
    k_b, g_b = gates(f_bw)
    flip = lambda t: jnp.flip(t, axis=2)
    o_f = gla_chunk_scan(q, k_f, v, g_f)
    o_b = flip(gla_chunk_scan(flip(q), flip(k_b), flip(v), flip(g_b)))
    o = rms_norm(o_f + o_b, o_norm[:, None, :])
    o = jnp.transpose(o, (0, 2, 1, 3)).reshape(b, s, HG_V)
    return (o * jax.nn.silu(gate)) @ w_out

def rope_angles(positions, dim):
    inv = 1.0 / (ROPE_BASE ** (jnp.arange(0, dim, 2, dtype=jnp.float32) / dim))
    ang = positions.astype(jnp.float32)[..., None] * inv
    return jnp.cos(ang), jnp.sin(ang)

def apply_rope(t, cos, sin):
    t1, t2 = jnp.split(t, 2, axis=-1)
    cos = cos.astype(t.dtype)
    sin = sin.astype(t.dtype)
    return jnp.concatenate([t1 * cos - t2 * sin, t1 * sin + t2 * cos], axis=-1)

def mla_mixer(x, positions, w_in, q_norm, w_uq, kv_norm, w_ukv, w_o):
    b, s, _ = x.shape
    proj = x @ w_in
    cq, ckv, k_rope = jnp.split(proj, [MLA_Q_RANK, MLA_Q_RANK + MLA_KV_RANK], axis=-1)
    cq = rms_norm(cq, q_norm)
    ckv = rms_norm(ckv, kv_norm)
    q = (cq @ w_uq).reshape(b, s, MLA_HEADS, MLA_NOPE + MLA_ROPE)
    q_nope, q_rope = q[..., :MLA_NOPE], q[..., MLA_NOPE:]
    cos, sin = rope_angles(positions, MLA_ROPE)
    q_rope = apply_rope(q_rope, cos[:, :, None, :], sin[:, :, None, :])
    k_rope = apply_rope(k_rope, cos, sin)
    w_ukv_h = w_ukv.reshape(MLA_KV_RANK, MLA_HEADS, MLA_NOPE + MLA_V)
    w_uk, w_uv = w_ukv_h[..., :MLA_NOPE], w_ukv_h[..., MLA_NOPE:]
    q_lat = jnp.einsum('bshn,chn->bshc', q_nope, w_uk)
    scale = (MLA_NOPE + MLA_ROPE) ** -0.5
    nb = s // Q_BLOCK

    def blockify(t):
        return jnp.moveaxis(t.reshape(b, nb, Q_BLOCK, *t.shape[2:]), 1, 0)

    def attend(blk):
        ql, qr = blk
        scores = (jnp.einsum('bqhc,bkc->bhqk', ql, ckv)
                  + jnp.einsum('bqhr,bkr->bhqk', qr, k_rope)) * scale
        probs = jax.nn.softmax(scores.astype(jnp.float32), axis=-1).astype(ckv.dtype)
        return jnp.einsum('bhqk,bkc->bqhc', probs, ckv)

    o_lat = lax.map(attend, (blockify(q_lat), blockify(q_rope)))
    o_lat = jnp.moveaxis(o_lat, 0, 1).reshape(b, s, MLA_HEADS, MLA_KV_RANK)
    o = jnp.einsum('bshc,chv->bshv', o_lat, w_uv).reshape(b, s, MLA_HEADS * MLA_V)
    return o @ w_o

def squared_relu_mlp(x, w1, w2):
    return jnp.square(jax.nn.relu(x @ w1)) @ w2

def second_inputs(seed: int = 0) -> dict:
    key = jax.random.key(seed)
    ks = jax.random.split(key, 32)
    f32 = jnp.float32

    def nrm(k, shape, fan_in):
        return jax.random.normal(k, shape, f32) * (fan_in ** -0.5)

    def gain(k, shape):
        return 1.0 + 0.05 * jax.random.normal(k, shape, f32)

    x = jax.random.normal(ks[0], (BATCH, SEQ, D_MODEL), f32)
    p = jax.random.normal(ks[1], (DEPTH_2, BATCH, SEQ, PLE_DIM), f32)
    positions = (jnp.arange(SEQ, dtype=jnp.int32)[None, :]
                 + jax.random.randint(ks[2], (BATCH, 1), 0, SEQ, dtype=jnp.int32))
    return {
        "x": x,
        "p": p,
        "positions": positions,
        "pre_mix_norm": gain(ks[3], (DEPTH_2, D_MODEL)),
        "post_mix_norm": gain(ks[4], (DEPTH_2, D_MODEL)),
        "pre_mlp_norm": gain(ks[5], (DEPTH_2, D_MODEL)),
        "post_mlp_norm": gain(ks[6], (DEPTH_2, D_MODEL)),
        "w_mlp_in": nrm(ks[7], (DEPTH_2, D_MODEL, D_FF), D_MODEL),
        "w_mlp_out": nrm(ks[8], (DEPTH_2, D_FF, D_MODEL), D_FF),
        "w_ple_proj": nrm(ks[9], (DEPTH_2, PLE_DIM, D_MODEL), PLE_DIM),
        "w_ple_gate": nrm(ks[10], (DEPTH_2, D_MODEL, D_MODEL), D_MODEL),
        "ple_norm": gain(ks[11], (DEPTH_2, D_MODEL)),
        "hg_lb_logits": 0.1 * jax.random.normal(ks[12], (DEPTH_2 + 1, HG_QK), f32),
        "hg_w_in": nrm(ks[13], (N_HGRN, D_MODEL, 3 * HG_QK + 2 * HG_V), D_MODEL),
        "hg_o_norm": gain(ks[14], (N_HGRN, HG_HEADS, HG_VDIM)),
        "hg_w_out": nrm(ks[15], (N_HGRN, HG_V, D_MODEL), HG_V),
        "mla_w_in": nrm(ks[16], (N_MLA, D_MODEL, MLA_Q_RANK + MLA_KV_RANK + MLA_ROPE), D_MODEL),
        "mla_q_norm": gain(ks[17], (N_MLA, MLA_Q_RANK)),
        "mla_w_uq": nrm(ks[18], (N_MLA, MLA_Q_RANK, MLA_HEADS * (MLA_NOPE + MLA_ROPE)), MLA_Q_RANK),
        "mla_kv_norm": gain(ks[19], (N_MLA, MLA_KV_RANK)),
        "mla_w_ukv": nrm(ks[20], (N_MLA, MLA_KV_RANK, MLA_HEADS * (MLA_NOPE + MLA_V)), MLA_KV_RANK),
        "mla_w_o": nrm(ks[21], (N_MLA, MLA_HEADS * MLA_V, D_MODEL), MLA_HEADS * MLA_V),
    }

def second_block(x, p, positions, pre_mix_norm, post_mix_norm, pre_mlp_norm, post_mlp_norm,
              w_mlp_in, w_mlp_out, w_ple_proj, w_ple_gate, ple_norm,
              hg_lb_logits, hg_w_in, hg_o_norm, hg_w_out,
              mla_w_in, mla_q_norm, mla_w_uq, mla_kv_norm, mla_w_ukv, mla_w_o):
    lb_all = jnp.cumsum(jax.nn.softmax(hg_lb_logits.astype(jnp.float32), axis=0), axis=0)
    h = x
    for i in range(DEPTH_2):
        a = rms_norm(h, pre_mix_norm[i])
        j = i // N_MIXERS
        if i % N_MIXERS == 0:
            m = hgrn2_mixer(a, hg_w_in[j], hg_o_norm[j], hg_w_out[j], lb_all[i])
        else:
            m = mla_mixer(a, positions, mla_w_in[j], mla_q_norm[j], mla_w_uq[j],
                          mla_kv_norm[j], mla_w_ukv[j], mla_w_o[j])
        h = h + rms_norm(m, post_mix_norm[i])
        f = squared_relu_mlp(rms_norm(h, pre_mlp_norm[i]), w_mlp_in[i], w_mlp_out[i])
        h = h + rms_norm(f, post_mlp_norm[i])
        e = p[i].astype(h.dtype) @ w_ple_proj[i]
        g = jax.nn.sigmoid(h @ w_ple_gate[i])
        h = h + rms_norm(g * e, ple_norm[i])
    return h


def setup_inputs(seed=0):
    out = dict(first_inputs(seed))
    for name, value in second_inputs(seed + 1).items():
        if name != "x":
            out[name + "_2"] = value
    return out


def reference(
    x, c, w_ada, b_ada, w_in, b_in, pool_w, pool_scale, sc_w, sc_b, cf_w, cf_b, cf_ln_g,
    cf_ln_b, w_branch, w_out, ln_g, ln_b, p_2, positions_2, pre_mix_norm_2, post_mix_norm_2,
    pre_mlp_norm_2, post_mlp_norm_2, w_mlp_in_2, w_mlp_out_2, w_ple_proj_2, w_ple_gate_2,
    ple_norm_2, hg_lb_logits_2, hg_w_in_2, hg_o_norm_2, hg_w_out_2, mla_w_in_2, mla_q_norm_2,
    mla_w_uq_2, mla_kv_norm_2, mla_w_ukv_2, mla_w_o_2,
):
    x = first_block(
        x, c, w_ada, b_ada, w_in, b_in, pool_w, pool_scale, sc_w, sc_b, cf_w, cf_b, cf_ln_g,
        cf_ln_b, w_branch, w_out, ln_g, ln_b,
    )
    return second_block(
        x, p_2, positions_2, pre_mix_norm_2, post_mix_norm_2, pre_mlp_norm_2, post_mlp_norm_2,
        w_mlp_in_2, w_mlp_out_2, w_ple_proj_2, w_ple_gate_2, ple_norm_2, hg_lb_logits_2,
        hg_w_in_2, hg_o_norm_2, hg_w_out_2, mla_w_in_2, mla_q_norm_2, mla_w_uq_2, mla_kv_norm_2,
        mla_w_ukv_2, mla_w_o_2,
    )


_drawn_inputs = setup_inputs


def setup_inputs(seed=0):
    import zlib

    import numpy as np

    out = dict(_drawn_inputs(seed))
    spreads = {}
    factors = {'b_ada': 7.716,
     'b_in': 8.0,
     'pool_scale': 8.0,
     'sc_b': 22.93,
     'cf_b': 8.0,
     'cf_ln_g': 8.0,
     'cf_ln_b': 34.198,
     'mla_q_norm_2': 5.513}
    for name, (base, spread) in spreads.items():
        noise = np.random.default_rng([zlib.crc32(name.encode()), seed]).standard_normal(out[name].shape)
        drawn = base * np.exp(spread * noise) if base else spread * noise
        out[name] = __import__('jax').numpy.asarray(drawn.astype(out[name].dtype))
    for name, factor in factors.items():
        out[name] = (out[name] * factor).astype(out[name].dtype)
    return out
```

```python
from contextlib import ExitStack

import numpy as np

import concourse.bass as bass
from concourse import mybir

F32 = mybir.dt.float32
F32R = mybir.dt.float32r
I32 = mybir.dt.int32
ALU = mybir.AluOpType
ACT = mybir.ActivationFunctionType
AX_X = mybir.AxisListType.X

P = 128
T = 512
D = 1024
NB = D // P
RING = 4
UNIT = 8 * P
TAPS = 31
POOLS = (2, 4, 8, 16)
ALPHA = 2.0 ** 0.25
LN_EPS = 1e-5
RMS_EPS = 1e-6
CH = 64
NCH = T // CH
HEADS = 8
MH = 16
MLA_SCALE = float(128 + 64) ** -0.5
TWO_PI = 6.283185307179586
PI_LO = 3.1415925

PARAMS = (("b_ada", 24), ("b_in", 96), ("pool_scale", 8), ("sc_w", 24), ("sc_b", 8), ("cf_w", 8 * TAPS),
          ("cf_b", 8), ("cf_ln_g", 8), ("cf_ln_b", 8), ("ln_g", 8), ("ln_b", 8), ("pre_mix", 16),
          ("post_mix", 16), ("pre_mlp", 16), ("post_mlp", 16), ("ple_norm", 16), ("hg_lb", 24),
          ("o_norm", 8), ("q_norm", 3), ("kv_norm", 2), ("inv_freq", 1), ("rope_sign", 1), ("c", 8), ("inv_count", 64))
COL = {}
_at = 0
for _name, _n in PARAMS:
    COL[_name] = _at
    _at += _n
NCOL = _at

BRANCH_UNITS = (7, 6, 3, 4, 5, 2, 1, 8)
BRANCH_ACT = {0: (7, ACT.Sigmoid), 2: (3, ACT.Identity), 4: (5, ACT.Sigmoid), 6: (1, ACT.Sigmoid), 7: (8, ACT.Sigmoid)}

STREAM = (("ada", 16), ("proj", 64), ("avp", 10), ("merge0", 16), ("merge1", 16), ("merge2", 16), ("adag", 8),
          ("wout", 8), ("hg", 32), ("hggate", 8), ("hgout", 8), ("mlp0", 64), ("plee0", 2), ("pleg0", 8),
          ("mlain", 7), ("heads0", 16), ("wo0", 8), ("heads1", 16), ("wo1", 8), ("mlp1", 64),
          ("plee1", 2), ("pleg1", 8))
U0 = {}
_at = 0
for _name, _n in STREAM:
    U0[_name] = _at
    _at += _n
UNITS = _at

PAIR = 21
SPLITS = (("u", 8, 1), ("yb", 8, 1), ("ya", 16, 1), ("yc", 8, 1), ("m", 8, 1), ("mix0", 8, 0), ("o", 8, 1),
          ("mlp0", 8, 0), ("p0", 2, 0), ("f0", 32, 0), ("ple0", 8, 0), ("mix1", 8, 0), ("cqkv", 5, 1), ("kr", 1, 1),
          ("ckt", 2, 0), ("pairs0", 4 * PAIR, 0.5), ("pairs1", 4 * PAIR, 0.5), ("mlp1", 8, 0), ("p1", 2, 0),
          ("f1", 32, 0), ("ple1", 8, 0))
K0, V0 = {}, {}
_at = _val = 0
for _name, _n, _has in SPLITS:
    K0[_name], V0[_name] = _at, _val
    _at += _n
    _val += {1: _n, 0: 0, 0.5: 4}[_has]

NORMS = (("ln_in", 8), ("ln_c", 8), ("ln_out", 8), ("mix0", 8), ("o", 8), ("post_mix0", 8), ("mlp0", 8),
         ("post_mlp0", 8), ("post_ple0", 8), ("mix1", 8), ("cqkv", 5), ("post_mix1", 8), ("mlp1", 8),
         ("post_mlp1", 8), ("post_ple1", 8))
Q0, R0 = {}, {}
_at = _i = 0
for _name, _n in NORMS:
    Q0[_name], R0[_name] = _at, _i
    _at += _n
    _i += 1


A0 = {"proj": 1, "merge0": 1 + 5 * NB, "yc": 1 + 6 * NB, "merge1": 1 + 7 * NB, "merge2": 1 + 8 * NB}
STD0 = {n: i for i, n in enumerate(("ln_in", "ln_c", "ln_out", "mix0", "post_mix0", "mlp0", "post_mlp0", "post_ple0",
                                    "mix1", "cqkv", "cqkv_second", "post_mix1", "mlp1", "post_mlp1", "post_ple1"))}
ROUNDER = 12582912.0
TWO_PI_PARTS = (6.28125, 0.0019350051879882812, 3.0199159819567e-07)


class Steps:

    def __init__(self, eng, sem):
        self.eng, self.sem, self.base, self.n = eng, sem, 0, 0

    def did(self, ins):
        ins.then_inc(self.sem, 1)
        self.n += 1

    def wait(self):
        self.eng.wait_ge(self.sem, self.base + self.n)

    def loop(self, rounds, per):
        return _Loop(self, rounds, per)


class _Loop:
    def __init__(self, steps, rounds, per):
        self.steps, self.rounds, self.per = steps, rounds, per

    def __enter__(self):
        k = self.steps
        self.before = k.base + k.n
        self.fori = k.eng.Fori(0, self.rounds)
        r = self.fori.__enter__()
        k.base, k.n = r * self.per + self.before, 0
        return r

    def __exit__(self, *exc):
        k = self.steps
        assert exc[0] or k.n == self.per, f"the loop signals {k.n} times a round, not {self.per}"
        k.base, k.n = self.before + self.rounds * self.per, 0
        return self.fori.__exit__(*exc)


def blk(buf, j):
    if isinstance(j, int):
        return buf[:, j, :]
    return buf[:, bass.ds(j, 1), :].rearrange("p a n -> p (a n)")


def cut(t, i):
    return t[:, i * P:(i + 1) * P]


def build(nc, ins, out):
    ctx = ExitStack()
    with ctx:
        def sb(name, shape, dt=F32, stack=ctx):
            return stack.enter_context(nc.sbuf_tensor(name, shape, dt))

        def sem(name):
            return ctx.enter_context(nc.semaphore(name))

        stage = sb("stage", [P, RING, UNIT])
        w_hi = sb("w_hi", [P, RING, UNIT], F32R)
        w_lo = sb("w_lo", [P, RING, UNIT], F32R)
        x_hi = sb("x_hi", [P, NB, T], F32R)
        x_lo = sb("x_lo", [P, NB, T], F32R)
        hres = sb("hres", [P, NB, T])
        acc = sb("acc", [P, NB, T])
        prm = sb("prm", [P, NCOL])
        ones = sb("ones", [P, P])
        ident = sb("ident", [P, P])
        mod = sb("mod", [P, 24])
        c_hi = sb("c_hi", [P, NB, 2], F32R)
        c_lo = sb("c_lo", [P, NB, 2], F32R)
        mean = sb("mean", [P, T])
        std = sb("std", [P, T])
        rstd_pre = sb("rstd_pre", [P, T])
        rstd_post = sb("rstd_post", [P, T])
        sq = sb("sq", [P, 2, T])
        tmp = sb("tmp", [P, 2, T])
        sig = sb("sig", [P, 2, T])
        consts = sb("consts", [P, 2])
        lbt = sb("lbt", [P, 40])
        small = sb("small", [P, 8])
        with ExitStack() as own:
            ya_hi = sb("ya_hi", [P, NB, T], F32R, own)
            ya_lo = sb("ya_lo", [P, NB, T], F32R, own)
            yb_hi = sb("yb_hi", [P, NB, T], F32R, own)
            yb_lo = sb("yb_lo", [P, NB, T], F32R, own)
            gate_c = sb("gate_c", [P, NB, T], F32, own)
            zpad = sb("zpad", [P, TAPS - 1 + T], F32, own)
            qpad = sb("qpad", [P, 2 + T], F32, own)
        with ExitStack() as own:
            y_hi = sb("y_hi", [P, NB, T], F32R, own)
            y_lo = sb("y_lo", [P, NB, T], F32R, own)
            with ExitStack() as own2:
                p_in = sb("p_in", [P, 2, T], F32, own2)
                p_hi = sb("p_hi", [P, 2, T], F32R, own2)
                p_lo = sb("p_lo", [P, 2, T], F32R, own2)
                e_buf = sb("e_buf", [P, NB, T], F32, own2)
            with ExitStack() as own2:
                hq = sb("hq", [P, T], F32, own2)
                hvT = sb("hvT", [P, T], F32, own2)
                hf = sb("hf", [P, 2, T], F32, own2)
                hk = sb("hk", [P, 2, T], F32, own2)
                hg = sb("hg", [P, 2, T], F32, own2)
                hG = sb("hG", [P, 2, T], F32, own2)
                hE = sb("hE", [P, 2, T], F32, own2)
                hI = sb("hI", [P, 2, T], F32, own2)
                v_tok = sb("v_tok", [P, T], F32, own2)
                k_tok = sb("k_tok", [P, 2, T], F32, own2)
                attn = sb("attn", [P, 2, T], F32, own2)
                state = sb("state", [P, 2, NCH, P], F32, own2)
                mask = sb("mask", [P, 2, T], I32, own2)
                reset = sb("reset", [P, T], F32, own2)
        with ExitStack() as own:
            ckv_hi = sb("ckv_hi", [P, 2, T], F32R, own)
            ckv_lo = sb("ckv_lo", [P, 2, T], F32R, own)
            ckt_hi = sb("ckt_hi", [P, 4, 2 * P], F32R, own)
            ckt_lo = sb("ckt_lo", [P, 4, 2 * P], F32R, own)
            kr_hi = sb("kr_hi", [P, T], F32R, own)
            kr_lo = sb("kr_lo", [P, T], F32R, own)
            cq_hi = sb("cq_hi", [P, 3, T], F32R, own)
            cq_lo = sb("cq_lo", [P, 3, T], F32R, own)
            qn_hi = sb("qn_hi", [P, 2, T], F32R, own)
            qn_lo = sb("qn_lo", [P, 2, T], F32R, own)
            ql_hi = sb("ql_hi", [P, 4, T], F32R, own)
            ql_lo = sb("ql_lo", [P, 4, T], F32R, own)
            qr_hi = sb("qr_hi", [P, T], F32R, own)
            qr_lo = sb("qr_lo", [P, T], F32R, own)
            pt_hi = sb("pt_hi", [P, 4, T], F32R, own)
            pt_lo = sb("pt_lo", [P, 4, T], F32R, own)
            ol_hi = sb("ol_hi", [P, 2, T], F32R, own)
            ol_lo = sb("ol_lo", [P, 2, T], F32R, own)
            pos_i = sb("pos_i", [P, T], I32, own)
        probs = sq
        cos, sin = mean, rstd_post

        bank = [ctx.enter_context(nc.psum_tensor(f"bank{i}", [P, T], F32)) for i in range(8)]

        loaded = [sem(f"unit_loaded{i}") for i in range(RING)]
        rounded = sem("unit_rounded")
        split = sem("unit_split")
        mm_done = sem("unit_multiplied")
        freed = sem("bank_freed")

        consts_in = sem("consts_in")
        x_in = sem("x_in")
        consts_set = sem("consts_set")
        out_sent = sem("out_sent")

        def prm_col(name, j=0):
            if isinstance(j, int):
                return prm[:, COL[name] + j:COL[name] + j + 1]
            return prm[:, bass.ds(j + COL[name], 1)]

        sq_ready = sem("square_ready")
        sq_used = sem("square_summed")
        std_ready = sem("std_ready")
        rstd_ready = sem("rstd_ready")
        sum_done = sem("sum_done")
        mean_ready = sem("mean_ready")
        centred = sem("centred")

        block = ctx.enter_context(nc.Block())

        c_ready = sem("c_ready")
        act_done = sem("branch_act_done")
        hc_ready = sem("conv_ready")
        pool_mm = sem("pool_multiplied")
        r_ready = sem("row_ready")
        val_ready = sem("value_ready")
        hi_ready = sem("hi_ready")
        lo_ready = sem("lo_ready")
        h_ready = sem("h_ready")
        ln_ready = sem("ln_ready")
        step = sem("dve_step")
        lb_exp = sem("lb_exp")
        lb_in = sem("lb_in")

        gla_in = sem("gla_consts_in")
        gla_act = sem("gla_act")
        gla_dve = sem("gla_dve")
        decayed = sem("decayed")
        kend_ready = sem("kend_ready")
        masked = sem("masked")
        states_done = sem("states_done")
        attn_mm = sem("attn_mm")
        v_turned = sem("v_turned")
        k_turned = sem("k_turned")
        kv_mm = sem("kv_mm")
        o_mm = sem("o_mm")
        o_read = sem("o_read")
        tok_copied = sem("tok_copied")
        o_rstd = sem("o_rstd")
        o_normed = sem("o_normed")
        gate_sig = sem("gate_sig")

        squared = sem("squared")
        p_arrived = sem("p_arrived")
        e_mm = sem("e_mm")
        ple_sig = sem("ple_sig")

        pos_in = sem("pos_in")
        trig_arg = sem("trig_arg")
        trig = sem("trig")
        cq_std = sem("cq_std")
        ckt_mm = sem("ckt_mm")
        q_mm = sem("q_mm")
        sc_mm = sem("score_mm")
        mx_ready = sem("max_ready")
        exp_done = sem("exp_done")
        p_ready = sem("prob_ready")
        pt_mm = sem("prob_turned")
        pv_mm = sem("pv_mm")
        uv_mm = sem("uv_mm")

        @block.sync
        def _(sp):
            units = ins["weights"]

            def load(u, s, src):
                sp.dma_start(stage[:, s, :], src).then_inc(loaded[s], 16)

            for s in range(RING):
                load(s, s, units[s])
            with sp.Fori(1, UNITS // RING) as r:
                for s in range(RING):
                    sp.wait_ge(split, r * RING + (s - RING + 1))
                    load(0, s, units[bass.ds(r * RING + s, 1)].rearrange("a p n -> p (a n)"))
            for u in range(UNITS // RING * RING, UNITS):
                sp.wait_ge(split, u - RING + 1)
                load(u, u % RING, units[u])
            for j in range(NB):
                sp.wait_ge(h_ready, 8 * 6 + j + 1)
                sp.dma_start(out[j], hres[:, j, :]).then_inc(out_sent, 16)
            sp.wait_ge(out_sent, 16 * NB)

        @block.gpsimd
        def _(pool):
            def lo(u, s):
                pool.wait_ge(rounded, u + 1)
                nc.gpsimd.tensor_tensor(w_lo[:, s, :], stage[:, s, :], w_hi[:, s, :].bitcast(F32),
                                        ALU.subtract).then_inc(split, 1)

            with pool.Fori(0, UNITS // RING) as r:
                for s in range(RING):
                    lo(r * RING + s, s)
            for u in range(UNITS // RING * RING, UNITS):
                lo(u, u % RING)

        @block.tensor
        def _(pe):
            def mm3(o, wh, wl, xh, xl, start, stop):
                nc.tensor.matmul(o, wh, xh, start=start, stop=False)
                nc.tensor.matmul(o, wh, xl, start=False, stop=False)
                return nc.tensor.matmul(o, wl, xh, start=False, stop=stop)

            def unit(u, s, xh, xl, n=T):
                pe.wait_ge(split, u + 1)
                if not isinstance(u, int) or u >= RING:
                    pe.wait_ge(freed, u - (RING - 1))
                for k in range(8):
                    last = mm3(bank[s][:, 0:n], cut(w_hi[:, s, :], k), cut(w_lo[:, s, :], k),
                               xh[:, k, :], xl[:, k, :], k == 0, k == 7)
                last.then_inc(mm_done, 1)

            def units(name, n, xs, first=0, group=RING):
                with pe.Fori(first // group, (first + n) // group) as r:
                    for i in range(group):
                        unit(r * group + (U0[name] + i), (U0[name] + i) % RING, *xs[i % len(xs)])

            def sum_features(src, ready, base):
                for k in range(NB):
                    pe.wait_ge(ready, base(k))
                    last = nc.tensor.matmul(bank[6][:, :], ones[:, :], src[:, k, :], start=k == 0, stop=k == NB - 1)
                last.then_inc(sum_done, 1)

            def sum_squares(name, n=NB, b=7, first=0, size=None):
                for k in range(n):
                    pe.wait_ge(sq_ready, Q0[name] + first + k + 1)
                    nc.tensor.matmul(bank[b][:, :], ones[:, :], sq[:, (first + k) % 2, :],
                                     start=k == 0, stop=k == n - 1).then_inc(sq_used, 1)

            def operand(name, n):
                pe.wait_ge(lo_ready, K0[name] + n)

            pe.wait_ge(consts_set, 1)
            pe.wait_ge(x_in, 16)
            sum_features(hres, x_in, lambda k: 16)
            pe.wait_ge(c_ready, 1)
            for u in range(RING):
                unit(u, u, c_hi, c_lo, 2)
            sum_squares("ln_in")
            with pe.Fori(1, 4) as r:
                for i in range(RING):
                    unit(r * RING + i, i, c_hi, c_lo, 2)
            operand("u", 8)
            units("proj", 64, [(x_hi, x_lo)])
            for half in range(2):
                a0 = U0["avp"] + 5 * half
                for i in range(4):
                    unit(a0 + i, (a0 + i) % RING, x_hi, x_lo)
                s = (a0 + 4) % RING
                pe.wait_ge(split, a0 + 5)
                for g in (2 * half, 2 * half + 1):
                    operand("ya", 8 * half + 2 * (g % 2) + 2)
                    if half:
                        operand("ya", 8)
                    for m in range(2):
                        o = bank[4 + 2 * (g % 2) + m][:, :]
                        for k in range(2):
                            i = 4 * (g % 2) + 2 * k + m
                            last = mm3(o, cut(w_hi[:, s, :], i), cut(w_lo[:, s, :], i),
                                       ya_hi[:, 2 * g + k, :], ya_lo[:, 2 * g + k, :], k == 0, k == 1)
                    last.then_inc(mm_done if g % 2 else pool_mm, 1)
            operand("ya", 16)
            sum_features(hres, hc_ready, lambda k: k + 2)
            units("merge0", 16, [(x_hi, x_lo), (ya_hi, ya_lo)])
            sum_squares("ln_c")
            units("merge1", 16, [(x_hi, x_lo), (yb_hi, yb_lo)])
            operand("yc", 8)
            units("merge2", 16, [(x_hi, x_lo), (ya_hi, ya_lo)])
            with pe.Fori(0, 2) as r:
                for i in range(RING):
                    unit(r * RING + (U0["adag"] + i), (U0["adag"] + i) % RING, c_hi, c_lo, 2)
            operand("m", 8)
            units("wout", 8, [(yb_hi, yb_lo)])
            sum_features(hres, r_ready, lambda k: k + 1)
            sum_squares("ln_out")
            sum_squares("mix0")

            operand("mix0", 8)

            def head_units(h):
                for i in range(4):
                    unit(h * 4 + (U0["hg"] + i), (U0["hg"] + i) % RING, x_hi, x_lo)

            def pairs(t, p):
                return t[:, p * P:(p + 1) * P]

            def gla(c):
                pe.wait_ge(decayed, c * 2 - 1)
                for p in range(4):
                    last = nc.tensor.matmul(pairs(bank[7], p), pairs(hI[:, 0, :], p), pairs(hf[:, 0, :], p),
                                            start=True, stop=True)
                last.then_inc(attn_mm, 1)
                pe.wait_ge(freed, c * 4 + U0["hg"])
                pe.wait_ge(o_read, c)
                for p in range(4):
                    last = nc.tensor.transpose(pairs(bank[4], p), pairs(hvT[:, :], p), ident[:, :])
                last.then_inc(v_turned, 1)
                pe.wait_ge(kend_ready, c * 2 - 1)
                for p in range(4):
                    last = nc.tensor.transpose(pairs(bank[5], p), pairs(hg[:, 0, :], p), ident[:, :])
                last.then_inc(k_turned, 1)
                pe.wait_ge(decayed, c * 2)
                for p in range(4):
                    last = nc.tensor.matmul(pairs(bank[6], p), pairs(hI[:, 1, :], p), pairs(hf[:, 1, :], p),
                                            start=True, stop=True)
                last.then_inc(attn_mm, 1)
                pe.wait_ge(kend_ready, c * 2)
                pe.wait_ge(masked, c * 2 - 1)
                for p in range(4):
                    last = nc.tensor.transpose(pairs(bank[7], p), pairs(hg[:, 1, :], p), ident[:, :])
                last.then_inc(k_turned, 1)

                def chunk_kv(d, n):
                    half, p = 64 * (n % 2), n // 2
                    return nc.tensor.matmul(pairs(bank[4 + 2 * d + n % 2], n // 2),
                                            k_tok[half:half + CH, d, p * P:(p + 1) * P],
                                            v_tok[half:half + CH, p * P:(p + 1) * P], start=True, stop=True)

                pe.wait_ge(tok_copied, c * 3 - 1)
                for n in range(NCH - 1):
                    last = chunk_kv(0, n)
                last.then_inc(kv_mm, 1)
                pe.wait_ge(tok_copied, c * 3)
                pe.wait_ge(masked, c * 2)
                for n in range(NCH - 1, 0, -1):
                    last = chunk_kv(1, n)
                last.then_inc(kv_mm, 1)
                pe.wait_ge(states_done, c * 2 - 1)
                for d in range(2):
                    if d:
                        pe.wait_ge(states_done, c * 2)
                    for p in range(4):
                        nc.tensor.matmul(pairs(bank[4], p), pairs(v_tok[:, :], p), pairs(attn[:, d, :], p),
                                         start=d == 0 and p == 0, stop=False, skip_group_check=True)
                    for n in range(1 - d, NCH - d):
                        last = nc.tensor.matmul(bank[4][:, n * CH:(n + 1) * CH], state[:, d, n, :],
                                                hf[:, d, n * CH:(n + 1) * CH], start=False,
                                                stop=d == 1 and n == NCH - 2, skip_group_check=True)
                last.then_inc(o_mm, 1)

            head_units(0)
            with pe.Fori(1, HEADS) as h:
                head_units(h)
                gla(h)
            gla(HEADS)
            for h in range(HEADS):
                pe.wait_ge(sq_ready, Q0["o"] + h + 1)
                if h >= 2:
                    pe.wait_ge(o_rstd, h - 1)
                nc.tensor.matmul(bank[6 + h % 2][:, :], ones[:, :], sq[:, h % 2, :],
                                 start=True, stop=True).then_inc(sq_used, 1)
            units("hggate", 8, [(x_hi, x_lo)])
            operand("o", 8)
            units("hgout", 8, [(y_hi, y_lo)])

            def mlp(i):
                sum_squares(f"post_mix{i}")
                sum_squares(f"mlp{i}")
                operand(f"mlp{i}", 8)
                name = f"mlp{i}"
                with pe.Fori(0, 4) as q:
                    for half in range(2):
                        for s in range(4):
                            v = 4 * half + s
                            unit(q * 16 + (U0[name] + v), (U0[name] + v) % RING, x_hi, x_lo)
                    pe.wait_ge(lo_ready, q * 8 + (K0[f"f{i}"] + 8))
                    for half in range(2):
                        for s in range(4):
                            v = 8 + 4 * half + s
                            unit(q * 16 + (U0[name] + v), (U0[name] + v) % RING, y_hi, y_lo)

            def ple(i):
                operand(f"p{i}", 2)
                for e in range(2):
                    u = U0[f"plee{i}"] + e
                    pe.wait_ge(split, u + 1)
                    if e:
                        pe.wait_ge(freed, u)
                    for o in range(4):
                        for k in range(2):
                            w = 2 * o + k
                            last = mm3(bank[4 + o][:, :], cut(w_hi[:, u % RING, :], w), cut(w_lo[:, u % RING, :], w),
                                       p_hi[:, k, :], p_lo[:, k, :], k == 0, k == 1)
                    last.then_inc(mm_done, 1)
                pe.wait_ge(freed, U0[f"plee{i}"] + 2)
                sum_squares(f"post_mlp{i}")
                operand(f"ple{i}", 8)
                units(f"pleg{i}", 8, [(x_hi, x_lo)])
                sum_squares(f"post_ple{i}")

            mlp(0)
            ple(0)

            sum_squares("mix1")
            operand("mix1", 8)
            for i in range(7):
                unit(U0["mlain"] + i, (U0["mlain"] + i) % RING, x_hi, x_lo)
            sum_squares("cqkv", 3, 6)
            sum_squares("cqkv", 2, 7, 3)
            pe.wait_ge(val_ready, V0["cqkv"] + 5)
            for c in range(2):
                for k in range(4):
                    last = nc.tensor.transpose(pairs(bank[4 + c], k), pairs(acc[:, 3 + c, :], k), ident[:, :])
                last.then_inc(ckt_mm, 1)
            operand("ckt", 2)

            def head_pair(j, name):
                n = int(name[-1])
                hp = j + 4 * n
                u = j * 4 + U0[f"heads{n}"]
                sl = [(U0[f"heads{n}"] + i) % RING for i in range(4)]
                cuts = j * PAIR + K0[f"pairs{n}"]

                def w(which, i):
                    s = sl[which]
                    return cut(w_hi[:, s, :], i), cut(w_lo[:, s, :], i)

                def down(b, which):
                    for k in range(3):
                        last = mm3(bank[b][:, :], *w(which, k), cq_hi[:, k, :], cq_lo[:, k, :], k == 0, k == 2)
                    return last

                pe.wait_ge(split, u + 1)
                pe.wait_ge(lo_ready, cuts)
                down(0, 0).then_inc(q_mm, 1)
                pe.wait_ge(split, u + 3)
                down(1, 2)
                pe.wait_ge(split, u + 4)
                down(2, 3).then_inc(q_mm, 1)
                down(3, 1).then_inc(q_mm, 1)
                for e in range(2):
                    pe.wait_ge(lo_ready, cuts + (2 if e == 0 else 3))
                    for c in range(2):
                        last = mm3(bank[2 * e + c][:, :], *w(e, 3 + c), qn_hi[:, e, :], qn_lo[:, e, :], True, True)
                    last.then_inc(mm_done, 1)

                def scores(i):
                    e, qb = i // 4, i % 4
                    if i % 4 == 0:
                        pe.wait_ge(lo_ready, cuts + (5 + 2 * e))
                    if i >= 2:
                        pe.wait_ge(exp_done, hp * 8 + (i - 1))
                    o = bank[4 + i % 2][:, :]
                    q = slice(qb * P, (qb + 1) * P)
                    for c in range(2):
                        mm3(o, ql_hi[:, 2 * e + c, q], ql_lo[:, 2 * e + c, q], ckv_hi[:, c, :], ckv_lo[:, c, :],
                            c == 0, False)
                    r = slice(64 * e, 64 * e + 64)
                    mm3(o, qr_hi[r, q], qr_lo[r, q], kr_hi[r, :], kr_lo[r, :], False, True).then_inc(sc_mm, 1)

                PT = [7, 8, 9, 10, 13, 14, 16, 17]

                def turn(i):
                    pe.wait_ge(p_ready, hp * 8 + (i + 1))
                    if i >= 2:
                        pe.wait_ge(lo_ready, cuts + (PT[i - 2] + 1))
                    for k in range(4):
                        last = nc.tensor.transpose(pairs(bank[6 + i % 2], k), pairs(probs[:, i % 2, :], k), ident[:, :])
                    last.then_inc(pt_mm, 1)

                def weigh(e):
                    pe.wait_ge(lo_ready, cuts + (PT[4 * e + 3] + 1))
                    for c in range(2):
                        for k in range(4):
                            last = mm3(bank[c][:, :], ckt_hi[:, k, c * P:(c + 1) * P], ckt_lo[:, k, c * P:(c + 1) * P],
                                       pt_hi[:, k, :], pt_lo[:, k, :], k == 0, k == 3)
                    last.then_inc(pv_mm, 1)

                def up(e):
                    pe.wait_ge(lo_ready, cuts + (13 if e == 0 else 20))
                    for c in range(2):
                        last = mm3(bank[2 + e][:, :], *w(2 + e, 3 + c), ol_hi[:, c, :], ol_lo[:, c, :], c == 0, c == 1)
                    last.then_inc(mm_done, 1)

                for t in range(10):
                    if t < 8:
                        scores(t)
                    if t == 6:
                        weigh(0)
                    if t >= 2:
                        turn(t - 2)
                    if t == 7:
                        up(0)
                weigh(1)
                up(1)

            for n in range(2):
                pe.wait_ge(freed, U0[f"heads{n}"])
                with pe.Fori(0, 4) as j:
                    head_pair(j, f"pairs{n}")
                operand(f"pairs{n}", 4 * PAIR)
                units(f"wo{n}", 8, [(x_hi, x_lo)])
            mlp(1)
            ple(1)

        @block.scalar
        def _(act):
            def fn(o, i, f, **kw):
                return nc.scalar.activation(o, i, f, **kw)

            def tick(name, i, r=0, per=0):
                u = U0[name] + i
                if isinstance(r, int):
                    u, r = u + per * r, 0
                    if u + RING >= UNITS:
                        return
                act.wait_ge(mm_done, r * per + (u + 1))
                act.wait_ge(loaded[u % RING], r * (16 * per // RING) + 16 * (u // RING + 2))
                fn(w_hi[:, u % RING, :], stage[:, u % RING, :], ACT.Copy).then_inc(rounded, 1)

            def ticks(name, n, group=RING, first=0):
                with act.Fori(first // group, (first + n) // group) as r:
                    for i in range(group):
                        tick(name, i, r, group)

            def root(name, n=NB, size=D, eps=RMS_EPS, o=std, b=7, first=0):
                act.wait_ge(sq_used, Q0[name] + first + n)
                fn(o[:, :] if o is std else o, bank[b][:, :], ACT.Sqrt, bias=eps_col(eps),
                   scale=1.0 / size).then_inc(std_ready, 1)

            def eps_col(eps):
                return consts[:, 0:1] if eps == LN_EPS else consts[:, 1:2]

            def squares(name, src, ready, base, per=2, scale=1):
                def two(r):
                    for s in range(2):
                        act.wait_ge(ready, r * 2 * scale + (base + scale * (s + 1)))
                        if not isinstance(r, int) or Q0[name] + 2 * r + s >= 2:
                            act.wait_ge(sq_used, r * 2 + (Q0[name] + s - 1))
                        fn(sq[:, s, :], blk(src, r * 2 + s), ACT.Square).then_inc(sq_ready, 1)
                two(0)
                with act.Fori(1, 4) as r:
                    two(r)

            act.dma_start(hres[:, :, :], ins["x"]).then_inc(x_in, 16)
            act.dma_start(prm[:, :], ins["params"]).then_inc(consts_in, 16)
            act.dma_start(ident[:, :], ins["ident"]).then_inc(consts_in, 16)
            act.wait_ge(consts_in, 32)
            fn(sig[:, 0, 0:8], prm[:, COL["c"]:COL["c"] + NB], ACT.Sigmoid).then_inc(act_done, 1)
            for s in range(RING):
                act.wait_ge(loaded[s], 16)
                fn(w_hi[:, s, :], stage[:, s, :], ACT.Copy).then_inc(rounded, 1)
            act.wait_ge(lb_in, 1)
            fn(lbt[:, 0:24], lbt[:, 0:24], ACT.Exp).then_inc(lb_exp, 1)
            for i in range(4):
                tick("ada", i)
            squares("ln_in", acc, centred, 0)
            root("ln_in", eps=LN_EPS)
            with act.Fori(1, 4) as r:
                for i in range(RING):
                    tick("ada", i, r, RING)
            with act.Fori(0, 4) as r:
                for s in range(2):
                    act.wait_ge(val_ready, r * 2 + (s + 1))
                    fn(blk(x_hi, r * 2 + s), blk(acc, r * 2 + s), ACT.Copy).then_inc(hi_ready, 1)

            def rounds(name, n, dst, src):
                for k in range(n):
                    act.wait_ge(val_ready, V0[name] + k + 1)
                    fn(dst(k), src(k), ACT.Copy).then_inc(hi_ready, 1)

            with act.Fori(0, NB) as j:
                for i in range(8):
                    act.wait_ge(mm_done, j * 8 + (U0["proj"] + i + 1))
                    if i in BRANCH_ACT:
                        part, func = BRANCH_ACT[i]
                        dst = {0: sig[:, 0, :], 2: mean[:, :], 4: sig[:, 1, :], 6: std[:, :], 7: rstd_pre[:, :]}[i]
                        fn(dst, bank[(U0["proj"] + i) % RING][:, :], func,
                           bias=prm_col("b_in", j + 8 * part)).then_inc(act_done, 1)
                    tick("proj", i, j, 8)
                act.wait_ge(val_ready, j + (V0["yb"] + 1))
                fn(blk(yb_hi, j), sq[:, 0, :], ACT.Copy).then_inc(hi_ready, 1)
            for half in range(2):
                for k in range(4):
                    tick("avp", 5 * half + k)
                    act.wait_ge(val_ready, V0["ya"] + 8 * half + k + 1)
                    fn(ya_hi[:, 4 * half + k, :], sig[:, k % 2, :], ACT.Copy).then_inc(hi_ready, 1)
                for k in range(4):
                    act.wait_ge(val_ready, V0["ya"] + 8 * half + 4 + k + 1)
                    fn(ya_hi[:, 4 * half + k, :], sig[:, k % 2, :], ACT.Copy).then_inc(hi_ready, 1)
                tick("avp", 5 * half + 4)

            def merge(i):
                name = f"merge{i}"
                with act.Fori(0, 4) as r:
                    for s in range(4):
                        if s % 2 == 0:
                            act.wait_ge(mm_done, r * 4 + (U0[name] + s + 1))
                            fn(sig[:, s // 2, :], bank[(U0[name] + s) % RING][:, :], ACT.Sigmoid,
                               bias=prm_col("b_in", r * 2 + (72 + 8 * i + s // 2))).then_inc(act_done, 1)
                        tick(name, s, r, 4)
                        if i == 2 and s % 2:
                            act.wait_ge(val_ready, r * 2 + (V0["m"] + s // 2 + 1))
                            fn(blk(yb_hi, r * 2 + s // 2), blk(acc, r * 2 + s // 2), ACT.Copy).then_inc(hi_ready, 1)

            merge(0)
            squares("ln_c", hres, centred, 8)
            root("ln_c", eps=LN_EPS)
            with act.Fori(0, 4) as r:
                for s in range(2):
                    act.wait_ge(ln_ready, r * 2 + (s + 1))
                    fn(sig[:, s, :], blk(hres, r * 2 + s), ACT.Sigmoid, scale=prm_col("cf_ln_g", r * 2 + s),
                       bias=prm_col("cf_ln_b", r * 2 + s)).then_inc(act_done, 1)
                for s in range(2):
                    act.wait_ge(val_ready, r * 2 + (V0["yc"] + s + 1))
                    fn(blk(ya_hi, r * 2 + s), tmp[:, s, :], ACT.Copy).then_inc(hi_ready, 1)
            act.wait_ge(lo_ready, K0["yc"] + 8)
            act.dma_start(hres[:, :, :], ins["x"]).then_inc(x_in, 16)
            merge(1)
            merge(2)
            ticks("adag", 8)
            ticks("wout", 8)
            squares("ln_out", hres, centred, 16)
            root("ln_out", eps=LN_EPS)
            with act.Fori(0, 4) as r:
                for s in range(2):
                    act.wait_ge(ln_ready, r * 2 + (8 + s + 1))
                    fn(blk(hres, r * 2 + s), tmp[:, s, :], ACT.Identity, bias=prm_col("ln_b", r * 2 + s)
                       ).then_inc(h_ready, 1)
                    act.wait_ge(h_ready, r * 2 + (s + 1))
                    act.wait_ge(sq_used, r * 2 + (Q0["mix0"] + s - 1))
                    fn(blk(x_hi, r * 2 + s), blk(hres, r * 2 + s), ACT.Copy,
                       scale=prm_col("pre_mix", r * 2 + s)).then_inc(hi_ready, 1)
                    fn(sq[:, s, :], blk(hres, r * 2 + s), ACT.Square).then_inc(sq_ready, 1)
            root("mix0")

            act.dma_start(mask[:, :, :], ins["mask"]).then_inc(gla_in, 16)
            act.dma_start(reset[:, :], ins["reset"]).then_inc(gla_in, 16)

            def head_ticks(h):
                for i in range(4):
                    tick("hg", i, h, 4)

            def gates(h):
                for d in range(2):
                    act.wait_ge(freed, h * 4 + (U0["hg"] + d + 2))
                    fn(hf[:, d, :], hf[:, d, :], ACT.Sigmoid).then_inc(gla_act, 1)
                for d in range(2):
                    act.wait_ge(gla_dve, h * 6 + (d + 1))
                    fn(hg[:, d, :], hf[:, d, :], ACT.Ln).then_inc(gla_act, 1)
                for d in range(2):
                    act.wait_ge(gla_dve, h * 6 + (2 + d + 1))
                    fn(hE[:, d, :], hG[:, d, :], ACT.Exp).then_inc(gla_act, 1)
                    fn(hI[:, d, :], hG[:, d, :], ACT.Exp, scale=-1.0).then_inc(gla_act, 1)
                    act.wait_ge(gla_dve, h * 6 + (4 + d + 1))
                    fn(hg[:, d, :], hg[:, d, :], ACT.Exp).then_inc(gla_act, 1)

            def tokens(c):
                act.wait_ge(v_turned, c)
                fn(v_tok[:, :], bank[4][:, :], ACT.Copy).then_inc(tok_copied, 1)
                act.wait_ge(k_turned, c * 2 - 1)
                fn(k_tok[:, 0, :], bank[5][:, :], ACT.Copy).then_inc(tok_copied, 1)
                act.wait_ge(k_turned, c * 2)
                fn(k_tok[:, 1, :], bank[7][:, :], ACT.Copy).then_inc(tok_copied, 1)

            head_ticks(0)
            gates(0)
            with act.Fori(1, HEADS) as h:
                head_ticks(h)
                tokens(h)
                gates(h)
            tokens(HEADS)
            for h in range(HEADS):
                act.wait_ge(o_read, h + 2)
                if h >= 2:
                    act.wait_ge(sq_used, Q0["o"] + h - 1)
                fn(sq[:, h % 2, :], acc[:, h, :], ACT.Square).then_inc(sq_ready, 1)
                act.wait_ge(sq_used, Q0["o"] + h + 1)
                if h >= 2:
                    act.wait_ge(o_normed, h - 1)
                fn(sig[:, h % 2, :], bank[6 + h % 2][:, :], ACT.Ln, bias=consts[:, 1:2], scale=1.0 / P
                   ).then_inc(gla_act, 1)
                act.wait_ge(gla_act, 10 * HEADS + h + 1)
                fn(sig[:, h % 2, :], sig[:, h % 2, :], ACT.Exp, scale=-0.5).then_inc(o_rstd, 1)
            with act.Fori(0, 2) as r:
                for i in range(4):
                    tick("hggate", i, r, 4)
                    act.wait_ge(freed, r * 4 + (U0["hggate"] + i + 1))
                    fn(sig[:, i % 2, :], tmp[:, i % 2, :], ACT.Sigmoid).then_inc(gate_sig, 1)
                    act.wait_ge(val_ready, r * 4 + (V0["o"] + i + 1))
                    fn(blk(y_hi, r * 4 + i), tmp[:, i % 2, :], ACT.Copy).then_inc(hi_ready, 1)
            ticks("hgout", 8)

            hblocks = {"mlp0": 1, "ple0": 2, "mix1": 3, "mlp1": 4, "ple1": 5, "end": 6}

            def next_operand(name, gain, layer, normed):
                with act.Fori(0, 4) as r:
                    for s in range(2):
                        act.wait_ge(h_ready, r * 2 + (8 * hblocks[name] + s + 1))
                        if normed:
                            act.wait_ge(sq_used, r * 2 + (Q0[name] + s - 1))
                        kw = dict(scale=prm_col(gain, r * 2 + (8 * layer + s))) if gain else {}
                        fn(blk(x_hi, r * 2 + s), blk(hres, r * 2 + s), ACT.Copy, **kw).then_inc(hi_ready, 1)
                        if normed:
                            fn(sq[:, s, :], blk(hres, r * 2 + s), ACT.Square).then_inc(sq_ready, 1)
                if normed:
                    root(name)

            def post(name, phase):
                squares(name, acc, freed, U0[phase])
                root(name)

            def mlp(i, mixer):
                name = f"mlp{i}"
                act.dma_start(p_in[:, :, :], ins[f"p{i}"]).then_inc(p_arrived, 16)
                post(f"post_mix{i}", mixer)
                next_operand(name, "pre_mlp", i, True)
                act.wait_ge(p_arrived, 16 * (i + 1))
                for k in range(2):
                    fn(p_hi[:, k, :], p_in[:, k, :], ACT.Copy).then_inc(hi_ready, 1)
                with act.Fori(0, 4) as q:
                    for v in range(8):
                        tick(name, v, q, 16)
                        s = v % 2
                        act.wait_ge(freed, q * 16 + (U0[name] + v + 1))
                        fn(tmp[:, s, :], tmp[:, s, :], ACT.Square).then_inc(squared, 1)
                        act.wait_ge(squared, q * 8 + (32 * i + v + 1))
                        fn(y_hi[:, v, :], tmp[:, s, :], ACT.Copy).then_inc(hi_ready, 1)
                    for v in range(8, 16):
                        tick(name, v, q, 16)

            def ple(i):
                for e in range(2):
                    tick(f"plee{i}", e)
                squares(f"post_mlp{i}", acc, freed, U0[f"mlp{i}"] + 56)
                root(f"post_mlp{i}")
                next_operand(f"ple{i}", None, 0, False)
                name = f"pleg{i}"
                last = U0[name] + 8 == UNITS

                def four(r):
                    for v in range(4):
                        if isinstance(r, int):
                            act.wait_ge(mm_done, r * 4 + U0[name] + v + 1)
                        else:
                            act.wait_ge(mm_done, r * 4 + (U0[name] + v + 1))
                        act.wait_ge(freed, r * 4 + (U0[name] + v - 1))
                        fn(sig[:, v % 2, :], bank[(U0[name] + v) % RING][:, :], ACT.Sigmoid).then_inc(ple_sig, 1)
                        tick(name, v, r, 4)

                if last:
                    four(0)
                    four(1)
                else:
                    with act.Fori(0, 2) as r:
                        four(r)
                post(f"post_ple{i}", name)

            mlp(0, "hgout")
            ple(0)
            next_operand("mix1", "pre_mix", 1, True)

            act.dma_start(pos_i[:, :], ins["positions"].partition_broadcast(P)).then_inc(pos_in, 16)
            for i in range(2):
                act.wait_ge(trig_arg, i + 1)
                fn((sin, cos)[i][:, :], (sin, cos)[i][:, :], ACT.Sin).then_inc(trig, 1)
            for i in range(7):
                tick("mlain", i)
            for k in range(5):
                act.wait_ge(freed, U0["mlain"] + k + 1)
                if k >= 2:
                    act.wait_ge(sq_used, Q0["cqkv"] + k - 1)
                fn(sq[:, k % 2, :], acc[:, k, :], ACT.Square).then_inc(sq_ready, 1)
            root("cqkv", 3, 384, o=std, b=6)
            root("cqkv", 2, 256, o=sig[:, 0, :], b=7, first=3)
            rounds("cqkv", 5, lambda k: cq_hi[:, k, :] if k < 3 else ckv_hi[:, k - 3, :], lambda k: acc[:, k, :])
            rounds("kr", 1, lambda k: kr_hi[:, :], lambda k: sig[:, 1, :])
            act.wait_ge(ckt_mm, 1)
            for c in range(2):
                act.wait_ge(ckt_mm, c + 1)
                fn(ckt_hi[:, :, c * P:(c + 1) * P], bank[4 + c][:, :].rearrange("p (k n) -> p k n", n=P),
                   ACT.Copy).then_inc(hi_ready, 1)

            def head_pair(j, n):
                hp = j + 4 * n
                phase = f"heads{n}"

                def cut_bank(dst, b):
                    fn(dst, bank[b][:, :], ACT.Copy).then_inc(hi_ready, 1)

                act.wait_ge(q_mm, hp * 3 + 1)
                cut_bank(qn_hi[:, 0, :], 0)
                act.wait_ge(val_ready, j + (V0[f"pairs{n}"] + 1))
                fn(qr_hi[:, :], sig[:, 0, :], ACT.Copy).then_inc(hi_ready, 1)
                act.wait_ge(q_mm, hp * 3 + 3)
                cut_bank(qn_hi[:, 1, :], 3)
                for e in range(2):
                    act.wait_ge(mm_done, j * 4 + (U0[phase] + e + 1))
                    for c in range(2):
                        cut_bank(ql_hi[:, 2 * e + c, :], 2 * e + c)
                for e in range(2):
                    tick(phase, e, j, 4)

                def exp(i):
                    s = i % 2
                    act.wait_ge(mx_ready, hp * 8 + (i + 1))
                    if i >= 2:
                        act.wait_ge(pt_mm, hp * 8 + (i - 1))
                    fn(probs[:, s, :], bank[4 + s][:, :], ACT.Exp, bias=small[:, 4 * s + 1:4 * s + 2], scale=MLA_SCALE,
                       accum_out=small[:, 4 * s + 2:4 * s + 3]).then_inc(exp_done, 1)

                def pt(i):
                    qb = i % 4
                    act.wait_ge(pt_mm, hp * 8 + (i + 1))
                    if i == 4:
                        act.wait_ge(pv_mm, hp * 2 + 1)
                    fn(pt_hi[:, :, qb * P:(qb + 1) * P], bank[6 + i % 2][:, :].rearrange("p (k n) -> p k n", n=P),
                       ACT.Copy).then_inc(hi_ready, 1)

                def ol(e):
                    act.wait_ge(pv_mm, hp * 2 + (e + 1))
                    if e:
                        act.wait_ge(mm_done, j * 4 + (U0[phase] + 3))
                    for c in range(2):
                        cut_bank(ol_hi[:, c, :], c)

                def o(e):
                    act.wait_ge(mm_done, j * 4 + (U0[phase] + 3 + e))
                    cut_bank(blk(x_hi, j * 2 + e), 2 + e)

                for t in range(10):
                    if t < 8:
                        exp(t)
                    if t == 6:
                        ol(0)
                    if t >= 2:
                        pt(t - 2)
                    if t == 7:
                        o(0)
                        tick(phase, 2, j, 4)
                ol(1)
                o(1)
                tick(phase, 3, j, 4)

            for n in range(2):
                with act.Fori(0, 4) as j:
                    head_pair(j, n)
                ticks(f"wo{n}", 8)
            mlp(1, "wo1")
            ple(1)

        @block.vector
        def _(dve):
            v = nc.vector
            chain = Steps(dve, step)

            def did(ins):
                chain.did(ins)
                chain.wait()

            def lo(dst, value, hi, name, k):
                dve.wait_ge(hi_ready, k + (K0[name] + 1))
                v.tensor_tensor(dst, value, hi.bitcast(F32), ALU.subtract).then_inc(lo_ready, 1)

            def bank_of(name, i):
                return bank[(U0[name] + i) % RING][:, :]

            def multiplied(name, i, r=0, per=0):
                dve.wait_ge(mm_done, r * per + (U0[name] + i + 1))

            def recip(name, o, i=None):
                dve.wait_ge(std_ready, STD0[name] + 1)
                did(v.reciprocal(o, std[:, :]))

            def centre(src, dst, nth):
                dve.wait_ge(sum_done, nth + 1)
                did(v.tensor_scalar(mean[:, :], bank[6][:, :], 1.0 / D, None, ALU.mult))
                with dve.Fori(0, NB) as k:
                    v.tensor_tensor(blk(dst, k), blk(src, k), mean[:, :], ALU.subtract).then_inc(centred, 1)

            dve.wait_ge(consts_in, 32)
            v.memset(ones[:, :], 1.0).then_inc(consts_set, 1)
            v.memset(zpad[:, 0:TAPS - 1], 0.0).then_inc(hc_ready, 1)
            v.memset(qpad[:, 0:2], 0.0)
            v.memset(consts[:, 0:1], LN_EPS)
            did(v.memset(consts[:, 1:2], RMS_EPS))
            dve.wait_ge(act_done, 1)
            cs = tmp[:, 0, 0:NB]
            did(v.tensor_tensor(cs, prm[:, COL["c"]:COL["c"] + NB], sig[:, 0, 0:NB], ALU.mult))
            for i in range(2):
                did(v.tensor_copy(c_hi[:, :, i], cs))
            for i in range(2):
                last = v.tensor_tensor(c_lo[:, :, i], cs, c_hi[:, :, i].bitcast(F32), ALU.subtract)
            last.then_inc(c_ready, 1)
            lg = [prm[:, COL["hg_lb"] + 8 * i:COL["hg_lb"] + 8 * i + 8] for i in range(3)]
            did(v.tensor_tensor(lbt[:, 24:32], lg[0], lg[1], ALU.max))
            did(v.tensor_tensor(lbt[:, 24:32], lbt[:, 24:32], lg[2], ALU.max))
            for i in range(3):
                last = v.tensor_tensor(lbt[:, 8 * i:8 * i + 8], lg[i], lbt[:, 24:32], ALU.subtract)
            last.then_inc(lb_in, 1)
            dve.wait_ge(lb_exp, 1)
            did(v.tensor_tensor(lbt[:, 24:32], lbt[:, 0:8], lbt[:, 8:16], ALU.add))
            did(v.tensor_tensor(lbt[:, 24:32], lbt[:, 24:32], lbt[:, 16:24], ALU.add))
            did(v.reciprocal(lbt[:, 32:40], lbt[:, 24:32]))
            did(v.tensor_tensor(lbt[:, 24:32], lbt[:, 0:8], lbt[:, 32:40], ALU.mult))
            did(v.tensor_scalar(lbt[:, 32:40], lbt[:, 24:32], -1.0, 1.0, ALU.mult, ALU.add))

            centre(hres, acc, 0)

            def modulate(name, first, i, r=0):
                j = r * RING + (first + i)
                multiplied(name, i, r, RING)
                at = j if isinstance(j, int) else bass.ds(j, 1)
                o = mod[:, j:j + 1] if isinstance(j, int) else mod[:, at]
                v.tensor_tensor(o, bank_of(name, i)[:, 0:1], prm_col("b_ada", j), ALU.add).then_inc(freed, 1)

            for i in range(RING):
                modulate("ada", 0, i)
            recip("ln_in", rstd_pre[:, :])
            with chain.loop(NB, 1) as k:
                chain.did(v.tensor_tensor(blk(acc, k), blk(acc, k), rstd_pre[:, :], ALU.mult))
            with dve.Fori(1, 4) as r:
                for i in range(RING):
                    modulate("ada", 0, i, r)
            dve.wait_ge(freed, 16)
            did(v.tensor_scalar(mod[:, 8:16], mod[:, 8:16], 1.0, None, ALU.add))
            with dve.Fori(0, NB) as k:
                v.tensor_scalar(blk(acc, k), blk(acc, k), mod[:, bass.ds(k + 8, 1)], mod[:, bass.ds(k, 1)],
                                ALU.mult, ALU.add).then_inc(val_ready, 1)
            with dve.Fori(0, NB) as k:
                lo(blk(x_lo, k), blk(acc, k), blk(x_hi, k), "u", k)

            def taps(j, first, last):
                for t in range(first, last):
                    z, w = zpad[:, t:t + T], prm_col("cf_w", j * TAPS + t)
                    h = blk(hres, j)
                    if t == 0:
                        did(v.tensor_scalar(h, z, w, prm_col("cf_b", j), ALU.mult, ALU.add))
                    elif t < TAPS - 1:
                        did(v.scalar_tensor_tensor(h, z, w, h, ALU.mult, ALU.add))
                    else:
                        v.scalar_tensor_tensor(h, z, w, h, ALU.mult, ALU.add).then_inc(hc_ready, 1)

            def biased(o, j, i, by):
                return v.scalar_tensor_tensor(o, bank_of("proj", i), prm_col("b_in", j + 8 * BRANCH_UNITS[i]), by,
                                              ALU.add, ALU.mult)

            with chain.loop(NB, 34) as j:
                dve.wait_ge(hc_ready, j + 1)
                multiplied("proj", 1, j, 8)
                dve.wait_ge(act_done, j * 5 + 2)
                biased(zpad[:, TAPS - 1:], j, 1, sig[:, 0, :]).then_inc(freed, 2)
                dve.wait_ge(freed, j * 8 + (U0["proj"] + 2))
                taps(j, 0, 10)
                multiplied("proj", 3, j, 8)
                dve.wait_ge(act_done, j * 5 + 3)
                biased(qpad[:, 2:], j, 3, mean[:, :]).then_inc(freed, 2)
                dve.wait_ge(freed, j * 8 + (U0["proj"] + 4))
                conv = rstd_post[:, :]
                did(v.tensor_scalar(conv, qpad[:, 0:T], prm_col("sc_w", j * 3), prm_col("sc_b", j), ALU.mult, ALU.add))
                for t in (1, 2):
                    did(v.scalar_tensor_tensor(conv, qpad[:, t:t + T], prm_col("sc_w", j * 3 + t), conv,
                                               ALU.mult, ALU.add))
                taps(j, 10, 18)
                dve.wait_ge(act_done, j * 5 + 4)
                biased(tmp[:, 0, :], j, 4, sig[:, 1, :]).then_inc(freed, 1)
                multiplied("proj", 5, j, 8)
                dve.wait_ge(freed, j * 8 + (U0["proj"] + 5))
                biased(tmp[:, 1, :], j, 5, tmp[:, 0, :]).then_inc(freed, 1)
                dve.wait_ge(freed, j * 8 + (U0["proj"] + 6))
                v.tensor_tensor(sq[:, 0, :], tmp[:, 1, :], conv, ALU.mult).then_inc(val_ready, 1)
                taps(j, 18, 25)
                dve.wait_ge(act_done, j * 5 + 5)
                biased(blk(acc, j), j, 6, std[:, :]).then_inc(freed, 1)
                dve.wait_ge(freed, j * 8 + (U0["proj"] + 7))
                did(v.tensor_scalar(blk(acc, j), blk(acc, j), prm_col("pool_scale", j), None, ALU.mult))
                dve.wait_ge(act_done, j * 5 + 6)
                biased(blk(gate_c, j), j, 7, rstd_pre[:, :]).then_inc(freed, 1)
                taps(j, 25, TAPS)
                lo(blk(yb_lo, j), sq[:, 0, :], blk(yb_hi, j), "yb", j)

            ping = tmp[:, :, :].rearrange("p a n -> p (a n)")
            pong = sq[:, :, :].rearrange("p a n -> p (a n)")
            for half in range(2):
                for k in range(4):
                    j = 4 * half + k
                    g = j // 2
                    w = POOLS[g]
                    front = w - 2
                    if j == 0:
                        dve.wait_ge(hc_ready, NB + 1)
                    multiplied("avp", 5 * half + k)
                    v.tensor_scalar(zpad[:, TAPS - 1:], bank_of("avp", 5 * half + k), prm_col("b_in", j), None,
                                    ALU.add).then_inc(freed, 1)
                    dve.wait_ge(freed, U0["avp"] + 5 * half + k + 1)
                    z0 = TAPS - 1
                    did(v.tensor_tensor(ping[:, 0:T + front], zpad[:, z0 - front:z0 + T],
                                        zpad[:, z0 - front - 1:z0 + T - 1], ALU.add))
                    src, dst, width, at = ping, pong, 2, front
                    while width < w:
                        rest = at - width
                        did(v.tensor_tensor(dst[:, 0:T + rest], src[:, width:width + T + rest], src[:, 0:T + rest],
                                            ALU.add))
                        src, dst, width, at = dst, src, 2 * width, rest
                    vals = sig[:, k % 2, :]
                    z = zpad[:, z0:z0 + T]
                    did(v.scalar_tensor_tensor(vals, src[:, 0:T], 1.0 / w, z, ALU.mult, ALU.subtract))
                    ic = COL["inv_count"] + 16 * g
                    did(v.tensor_tensor(vals[:, 0:w], src[:, 0:w], prm[:, ic:ic + w], ALU.mult))
                    v.tensor_tensor(vals[:, 0:w], vals[:, 0:w], z[:, 0:w], ALU.subtract).then_inc(val_ready, 1)
                    lo(ya_lo[:, j, :], vals, ya_hi[:, j, :], "ya", 8 * half + k)
                for k in range(4):
                    g, m = 2 * half + k // 2, k % 2
                    j = 4 * half + k
                    if k == 0:
                        dve.wait_ge(pool_mm, half + 1)
                    if k == 2:
                        multiplied("avp", 5 * half + 4)
                    vals = sig[:, k % 2, :]
                    v.tensor_tensor(vals, bank[4 + 2 * (g % 2) + m][:, :], acc[:, j, :], ALU.mult
                                    ).then_inc(val_ready, 1)
                    dve.wait_ge(hi_ready, K0["ya"] + 8 * half + 4 + k + 1)
                    v.tensor_tensor(ya_lo[:, j, :], vals, ya_hi[:, j, :].bitcast(F32), ALU.subtract
                                    ).then_inc(lo_ready, 1)
                dve.wait_ge(lo_ready, K0["ya"] + 8 * half + 8)
                dve.sem_inc(freed, 1)
            centre(hres, hres, 1)

            def merge(i):
                name = f"merge{i}"
                with chain.loop(4, 2 if i == 1 else 0) as r:
                    for s in range(2):
                        j = r * 2 + s
                        multiplied(name, 2 * s + 1, r, 4)
                        dve.wait_ge(act_done, r * 2 + (A0[name] + s + 1))
                        if i == 0:
                            v.tensor_tensor(blk(acc, j), bank_of(name, 2 * s + 1), sig[:, s, :], ALU.mult
                                            ).then_inc(freed, 2)
                            continue
                        chain.wait()
                        v.tensor_tensor(tmp[:, s, :], bank_of(name, 2 * s + 1), sig[:, s, :], ALU.mult
                                        ).then_inc(freed, 2)
                        dve.wait_ge(freed, r * 4 + (U0[name] + 2 * s + 2))
                        add = v.tensor_tensor(blk(acc, j), blk(acc, j), tmp[:, s, :], ALU.add)
                        if i == 1:
                            chain.did(add)
                        else:
                            add.then_inc(val_ready, 1)
                            lo(blk(yb_lo, j), blk(acc, j), blk(yb_hi, j), "m", j)

            merge(0)
            recip("ln_c", rstd_post[:, :])
            with dve.Fori(0, NB) as k:
                v.tensor_tensor(blk(hres, k), blk(hres, k), rstd_post[:, :], ALU.mult).then_inc(ln_ready, 1)
            dve.wait_ge(ln_ready, NB)
            with chain.loop(4, 4) as r:
                dve.wait_ge(lo_ready, r * 2 + K0["yc"])
                for s in range(2):
                    j = r * 2 + s
                    t = tmp[:, s, :]
                    did(v.tensor_scalar(t, blk(hres, j), prm_col("cf_ln_g", j), prm_col("cf_ln_b", j),
                                        ALU.mult, ALU.add))
                    dve.wait_ge(act_done, r * 2 + (A0["yc"] + s + 1))
                    did(v.tensor_tensor(t, t, sig[:, s, :], ALU.mult))
                    v.tensor_tensor(t, t, blk(gate_c, j), ALU.mult).then_inc(val_ready, 1)
                for s in range(2):
                    lo(blk(ya_lo, r * 2 + s), tmp[:, s, :], blk(ya_hi, r * 2 + s), "yc", r * 2 + s)
            dve.wait_ge(lo_ready, K0["yc"] + NB)
            merge(1)
            merge(2)
            with dve.Fori(0, 2) as r:
                for i in range(RING):
                    modulate("adag", 16, i, r)
            dve.wait_ge(x_in, 32)
            with chain.loop(2, 0) as r:
                for i in range(4):
                    j = r * 4 + i
                    multiplied("wout", i, r, 4)
                    if i == 0:
                        dve.wait_ge(freed, r * 4 + U0["wout"])
                    t = (tmp, sig)[i // 2][:, i % 2, :]
                    v.tensor_scalar(t, bank_of("wout", i), mod[:, bass.ds(j + 16, 1)], None, ALU.mult
                                    ).then_inc(freed, 1)
                    dve.wait_ge(freed, r * 4 + (U0["wout"] + i + 1))
                    v.scalar_tensor_tensor(blk(hres, j), blk(hres, j), ALPHA, t, ALU.mult, ALU.add
                                           ).then_inc(r_ready, 1)
            centre(hres, hres, 2)
            recip("ln_out", rstd_post[:, :])
            with dve.Fori(0, 4) as r:
                for s in range(2):
                    j = r * 2 + s
                    v.scalar_tensor_tensor(tmp[:, s, :], blk(hres, j), prm_col("ln_g", j), rstd_post[:, :],
                                           ALU.mult, ALU.mult).then_inc(ln_ready, 1)
                for s in range(2):
                    j = r * 2 + s
                    dve.wait_ge(hi_ready, r * 2 + (K0["mix0"] + s + 1))
                    v.scalar_tensor_tensor(blk(x_lo, j), blk(hres, j), prm_col("pre_mix", j), blk(x_hi, j).bitcast(F32),
                                           ALU.mult, ALU.subtract).then_inc(lo_ready, 1)
            recip("mix0", rstd_pre[:, :])

            v.memset(attn[:, 0, :], 0.0).then_inc(o_read, 1)
            did(v.memset(attn[:, 1, :], 0.0))
            dve.wait_ge(gla_in, 32)

            def head(h):
                b = [bank_of("hg", i) for i in range(4)]
                multiplied("hg", 0, h, 4)
                v.scalar_tensor_tensor(hq[:, :], b[0], float(P) ** -0.5, rstd_pre[:, :], ALU.mult, ALU.mult
                                       ).then_inc(freed, 1)
                for d in range(2):
                    multiplied("hg", 1 + d, h, 4)
                    v.tensor_tensor(hf[:, d, :], b[1 + d], rstd_pre[:, :], ALU.mult).then_inc(freed, 1)
                multiplied("hg", 3, h, 4)
                v.tensor_tensor(hvT[:, :], b[3], rstd_pre[:, :], ALU.mult).then_inc(freed, 1)
                at = lambda first: lbt[:, bass.ds(h + first, 1)] if not isinstance(h, int) else lbt[:, first + h:first + h + 1]
                for d in range(2):
                    dve.wait_ge(gla_act, h * 10 + (d + 1))
                    v.tensor_scalar(hf[:, d, :], hf[:, d, :], at(32), at(24), ALU.mult, ALU.add).then_inc(gla_dve, 1)
                    dve.wait_ge(gla_dve, h * 6 + (d + 1))
                    chain.did(v.tensor_scalar(hk[:, d, :], hf[:, d, :], -1.0, 1.0, ALU.mult, ALU.add))
                for d in range(2):
                    way = (slice(None), d, slice(None, None, -1) if d else slice(None))
                    dve.wait_ge(gla_act, h * 10 + (2 + d + 1))
                    v.tensor_tensor_scan(hG[way], reset[:, :], hg[way], 0.0, ALU.mult, ALU.add).then_inc(gla_dve, 1)
                for d in range(2):
                    dve.wait_ge(gla_dve, h * 6 + (2 + d + 1))
                    G = hG[:, d, :].rearrange("p (c t) -> p c t", t=CH)
                    end = G[:, :, 0:1] if d else G[:, :, CH - 1:CH]
                    v.tensor_tensor(hg[:, d, :].rearrange("p (c t) -> p c t", t=CH), end.to_broadcast([P, NCH, CH]), G,
                                    ALU.subtract).then_inc(gla_dve, 1)
                for d in range(2):
                    dve.wait_ge(gla_act, h * 10 + (4 + 3 * d + 2))
                    chain.did(v.tensor_tensor(hf[:, d, :], hq[:, :], hE[:, d, :], ALU.mult))
                    chain.wait()
                    v.tensor_tensor(hI[:, d, :], hk[:, d, :], hI[:, d, :], ALU.mult).then_inc(decayed, 1)
                    dve.wait_ge(gla_act, h * 10 + (4 + 3 * d + 3))
                    v.tensor_tensor(hg[:, d, :], hk[:, d, :], hg[:, d, :], ALU.mult).then_inc(kend_ready, 1)

            def scans(c):
                for d in range(2):
                    dve.wait_ge(attn_mm, c * 2 - 1 + d)
                    v.memset(small[:, d:d + 1], 0.0)
                    v.copy_predicated(attn[:, d, :], mask[:, d, :], bank[7 - d][:, :]).then_inc(masked, 1)
                for d in range(2):
                    dve.wait_ge(kv_mm, c * 2 - 1 + d)
                    kv = lambda n: bank[4 + 2 * d + n % 2][:, n // 2 * P:(n // 2 + 1) * P]
                    order = list(range(NCH)) if d == 0 else list(range(NCH - 1, -1, -1))
                    for i in range(NCH - 1):
                        n, to = order[i], order[i + 1]
                        if i == 0:
                            ins_ = v.tensor_copy(state[:, d, to, :], kv(n))
                        else:
                            e = n * CH if d else n * CH + CH - 1
                            ins_ = v.scalar_tensor_tensor(state[:, d, to, :], state[:, d, n, :], hE[:, d, e:e + 1],
                                                          kv(n), ALU.mult, ALU.add)
                        if i == NCH - 2:
                            ins_.then_inc(states_done, 1)
                        else:
                            did(ins_)
                dve.wait_ge(o_mm, c)
                v.tensor_copy(blk(acc, c - 1), bank[4][:, :]).then_inc(o_read, 1)

            GLA_HEAD, GLA_SCAN = 4, 12
            head(0)
            with chain.loop(HEADS - 1, GLA_HEAD + GLA_SCAN) as r:
                h = r + 1
                scans(h)
                head(h)
            scans(HEADS)
            for h in range(HEADS):
                dve.wait_ge(o_rstd, h + 1)
                v.scalar_tensor_tensor(acc[:, h, :], acc[:, h, :], prm_col("o_norm", h), sig[:, h % 2, :],
                                       ALU.mult, ALU.mult).then_inc(o_normed, 1)
            dve.wait_ge(o_normed, HEADS)
            with chain.loop(2, 4) as r:
                for i in range(4):
                    t = tmp[:, i % 2, :]
                    dve.wait_ge(lo_ready, r * 4 + (K0["o"] + i))
                    multiplied("hggate", i, r, 4)
                    v.tensor_tensor(t, bank_of("hggate", i), rstd_pre[:, :], ALU.mult).then_inc(freed, 1)
                    dve.wait_ge(gate_sig, r * 4 + (i + 1))
                    did(v.tensor_tensor(t, t, sig[:, i % 2, :], ALU.mult))
                    v.tensor_tensor(t, t, blk(acc, r * 4 + i), ALU.mult).then_inc(val_ready, 1)
                    lo(blk(y_lo, r * 4 + i), t, blk(y_hi, r * 4 + i), "o", r * 4 + i)

            def read_out(name):
                with dve.Fori(0, 2) as r:
                    for i in range(4):
                        multiplied(name, i, r, 4)
                        v.tensor_copy(blk(acc, r * 4 + i), bank_of(name, i)).then_inc(freed, 1)

            read_out("hgout")

            hblocks = {"mlp0": 1, "ple0": 2, "mix1": 3, "mlp1": 4, "ple1": 5, "end": 6}

            def residual(norm, gain, layer, name, next_gain, next_layer):
                recip(norm, rstd_post[:, :])
                if name != "end":
                    dve.wait_ge(lo_ready, K0[name])
                with chain.loop(4, 2) as r:
                    dve.wait_ge(h_ready, r * 2 + 8 * hblocks[name])
                    for s in range(2):
                        j = r * 2 + s
                        did(v.scalar_tensor_tensor(tmp[:, s, :], blk(acc, j), prm_col(gain, j + 8 * layer),
                                                   rstd_post[:, :], ALU.mult, ALU.mult))
                        v.tensor_tensor(blk(hres, j), blk(hres, j), tmp[:, s, :], ALU.add).then_inc(h_ready, 1)
                    for s in range(2):
                        j = r * 2 + s
                        if name == "end":
                            continue
                        dve.wait_ge(hi_ready, j + (K0[name] + 1))
                        if next_gain:
                            v.scalar_tensor_tensor(blk(x_lo, j), blk(hres, j), prm_col(next_gain, j + 8 * next_layer),
                                                   blk(x_hi, j).bitcast(F32), ALU.mult, ALU.subtract
                                                   ).then_inc(lo_ready, 1)
                        else:
                            v.tensor_tensor(blk(x_lo, j), blk(hres, j), blk(x_hi, j).bitcast(F32), ALU.subtract
                                            ).then_inc(lo_ready, 1)

            def mlp(i):
                name = f"mlp{i}"
                residual(f"post_mix{i}", "post_mix", i, name, "pre_mlp", i)
                recip(name, rstd_pre[:, :])
                dve.wait_ge(p_arrived, 16 * (i + 1))
                for k in range(2):
                    lo(p_lo[:, k, :], p_in[:, k, :], p_hi[:, k, :], f"p{i}", k)
                did(v.memset(acc[:, :, :], 0.0))
                with dve.Fori(0, 4) as q:
                    for u in range(8):
                        s = u % 2
                        dve.wait_ge(lo_ready, q * 8 + (K0[f"f{i}"] + u))
                        multiplied(name, u, q, 16)
                        v.scalar_tensor_tensor(tmp[:, s, :], bank_of(name, u), 0.0, rstd_pre[:, :], ALU.max, ALU.mult
                                               ).then_inc(freed, 1)
                        lo(y_lo[:, u, :], tmp[:, s, :], y_hi[:, u, :], f"f{i}", q * 8 + u)
                    for u in range(8):
                        multiplied(name, 8 + u, q, 16)
                        v.tensor_tensor(acc[:, u, :], acc[:, u, :], bank_of(name, 8 + u), ALU.add).then_inc(freed, 1)

            def ple(i, nxt):
                for e in range(2):
                    multiplied(f"plee{i}", e)
                    for o in range(4):
                        last = v.tensor_copy(e_buf[:, 4 * e + o, :], bank[4 + o][:, :])
                    last.then_inc(freed, 1)
                residual(f"post_mlp{i}", "post_mlp", i, f"ple{i}", None, 0)
                name = f"pleg{i}"
                with dve.Fori(0, 2) as r:
                    for u in range(4):
                        j = r * 4 + u
                        dve.wait_ge(ple_sig, j + (8 * i + 1))
                        v.tensor_tensor(blk(acc, j), sig[:, u % 2, :], blk(e_buf, j), ALU.mult).then_inc(freed, 1)
                residual(f"post_ple{i}", "ple_norm", i, nxt, "pre_mix", 1)

            mlp(0)
            ple(0, "mix1")
            recip("mix1", rstd_pre[:, :])

            dve.wait_ge(pos_in, 16)
            ang, n_turns = tmp[:, 0, :], tmp[:, 1, :]
            did(v.tensor_copy(ang, pos_i[:, :]))
            did(v.tensor_scalar(ang, ang, prm_col("inv_freq"), None, ALU.mult))
            for i, shift in enumerate((0.0, TWO_PI / 4)):
                o = (sin, cos)[i][:, :]
                did(v.tensor_scalar(n_turns, ang, 1.0 / TWO_PI, shift / TWO_PI, ALU.mult, ALU.add))
                did(v.tensor_scalar(n_turns, n_turns, ROUNDER, None, ALU.add))
                did(v.tensor_scalar(n_turns, n_turns, -ROUNDER, None, ALU.add))
                did(v.scalar_tensor_tensor(o, n_turns, -TWO_PI_PARTS[0], ang, ALU.mult, ALU.add))
                for part in TWO_PI_PARTS[1:]:
                    did(v.scalar_tensor_tensor(o, n_turns, -part, o, ALU.mult, ALU.add))
                did(v.tensor_scalar(o, o, shift, None, ALU.add))
                v.tensor_scalar(o, o, PI_LO, -PI_LO, ALU.min, ALU.max).then_inc(trig_arg, 1)
            for i in range(7):
                multiplied("mlain", i)
                v.tensor_tensor(acc[:, i, :], bank_of("mlain", i), rstd_pre[:, :], ALU.mult).then_inc(freed, 1)
            dve.wait_ge(std_ready, STD0["cqkv"] + 1)
            v.reciprocal(tmp[:, 0, :], std[:, :])
            dve.wait_ge(std_ready, STD0["cqkv"] + 2)
            did(v.reciprocal(tmp[:, 1, :], sig[:, 0, :]))
            for k in range(5):
                gain = prm_col("q_norm", k) if k < 3 else prm_col("kv_norm", k - 3)
                v.scalar_tensor_tensor(acc[:, k, :], acc[:, k, :], gain, tmp[:, 0 if k < 3 else 1, :],
                                       ALU.mult, ALU.mult).then_inc(val_ready, 1)
            for k in range(5):
                hi, lo_ = (cq_hi[:, k, :], cq_lo[:, k, :]) if k < 3 else (ckv_hi[:, k - 3, :], ckv_lo[:, k - 3, :])
                lo(lo_, acc[:, k, :], hi, "cqkv", k)
            dve.wait_ge(trig, 2)
            did(v.tensor_scalar(sin[:, :], sin[:, :], prm_col("rope_sign"), None, ALU.mult))
            did(v.tensor_tensor(tmp[:, 0, :], acc[:, 5, :], cos[:, :], ALU.mult))
            did(v.tensor_tensor(tmp[:, 1, :], acc[:, 6, :], sin[:, :], ALU.mult))
            v.tensor_tensor(sig[:, 1, :], tmp[:, 0, :], tmp[:, 1, :], ALU.add).then_inc(val_ready, 1)
            lo(kr_lo[:, :], sig[:, 1, :], kr_hi[:, :], "kr", 0)
            for c in range(2):
                dve.wait_ge(hi_ready, K0["ckt"] + c + 1)
                part = slice(c * P, (c + 1) * P)
                v.tensor_tensor(ckt_lo[:, :, part], bank[4 + c][:, :].rearrange("p (k n) -> p k n", n=P),
                                ckt_hi[:, :, part].bitcast(F32), ALU.subtract).then_inc(lo_ready, 1)

            def head_pair(j, n):
                hp = j + 4 * n
                name = f"pairs{n}"
                at = iter(range(PAIR))

                def rest(dst, b, hi):
                    dve.wait_ge(hi_ready, j * PAIR + (K0[name] + next(at) + 1))
                    ins_ = v.tensor_tensor(dst, b, hi.bitcast(F32), ALU.subtract)
                    ins_.then_inc(lo_ready, 1)

                rest(qn_lo[:, 0, :], bank[0][:, :], qn_hi[:, 0, :])
                dve.wait_ge(q_mm, hp * 3 + 2)
                chain.did(v.tensor_tensor(tmp[:, 0, :], bank[1][:, :], cos[:, :], ALU.mult))
                did(v.tensor_tensor(tmp[:, 1, :], bank[2][:, :], sin[:, :], ALU.mult))
                v.tensor_tensor(sig[:, 0, :], tmp[:, 0, :], tmp[:, 1, :], ALU.add).then_inc(val_ready, 1)
                rest(qr_lo[:, :], sig[:, 0, :], qr_hi[:, :])
                rest(qn_lo[:, 1, :], bank[3][:, :], qn_hi[:, 1, :])
                for e in range(2):
                    for c in range(2):
                        rest(ql_lo[:, 2 * e + c, :], bank[2 * e + c][:, :], ql_hi[:, 2 * e + c, :])

                def top(i):
                    s = i % 2
                    dve.wait_ge(sc_mm, hp * 8 + (i + 1))
                    did(v.tensor_reduce(small[:, 4 * s:4 * s + 1], bank[4 + s][:, :], AX_X, ALU.max))
                    v.tensor_scalar(small[:, 4 * s + 1:4 * s + 2], small[:, 4 * s:4 * s + 1], -MLA_SCALE, None,
                                    ALU.mult).then_inc(mx_ready, 1)

                def normed(i):
                    s = i % 2
                    dve.wait_ge(exp_done, hp * 8 + (i + 1))
                    did(v.reciprocal(small[:, 4 * s + 3:4 * s + 4], small[:, 4 * s + 2:4 * s + 3]))
                    v.tensor_scalar(probs[:, s, :], probs[:, s, :], small[:, 4 * s + 3:4 * s + 4], None,
                                    ALU.mult).then_inc(p_ready, 1)

                def pt(i):
                    part = slice(i % 4 * P, (i % 4 + 1) * P)
                    rest(pt_lo[:, :, part], bank[6 + i % 2][:, :].rearrange("p (k n) -> p k n", n=P),
                         pt_hi[:, :, part])

                def ol():
                    for c in range(2):
                        rest(ol_lo[:, c, :], bank[c][:, :], ol_hi[:, c, :])

                for t in range(10):
                    if t < 8:
                        top(t)
                    if 1 <= t < 9:
                        normed(t - 1)
                    if t == 6:
                        ol()
                    if t >= 2:
                        pt(t - 2)
                    if t == 7:
                        rest(blk(x_lo, j * 2), bank[2][:, :], blk(x_hi, j * 2))
                ol()
                rest(blk(x_lo, j * 2 + 1), bank[3][:, :], blk(x_hi, j * 2 + 1))

            for n in range(2):
                with chain.loop(4, 18) as j:
                    head_pair(j, n)
                dve.wait_ge(lo_ready, K0[f"pairs{n}"] + 4 * PAIR)
                dve.sem_inc(freed, 16)
                if n == 0:
                    read_out("wo0")
                else:
                    with dve.Fori(0, 2) as r:
                        for i in range(4):
                            multiplied("wo1", i, r, 4)
                            v.tensor_tensor(blk(acc, r * 4 + i), blk(acc, r * 4 + i), bank_of("wo1", i), ALU.add
                                            ).then_inc(freed, 1)
            mlp(1)
            ple(1, "end")


def blocks(w):
    k, n = w.shape
    return w.reshape(k // P, P, n // P, P).transpose(2, 1, 0, 3)


def as_units(w):
    b = blocks(w)
    return b.reshape(b.shape[0], P, UNIT)


def weight_stream(a):
    w_in = as_units(a["w_in"][0]).reshape(12, NB, P, UNIT)
    ada = as_units(a["w_ada"][0])
    parts = [ada[:16], np.stack([w_in[p] for p in BRANCH_UNITS], 1).reshape(64, P, UNIT)]
    pool = blocks(a["pool_w"][0].reshape(4 * 256, 256))
    pool = pool.reshape(2, P, 4, 2, P).transpose(2, 1, 3, 0, 4)
    for half in range(2):
        parts += [w_in[0][4 * half:4 * half + 4],
                  pool[2 * half:2 * half + 2].transpose(1, 0, 2, 3, 4).reshape(1, P, UNIT)]
    for i in range(3):
        parts.append(np.stack([w_in[9 + i], as_units(a["w_branch"][0, i])], 1).reshape(16, P, UNIT))
    parts += [ada[16:], as_units(a["w_out"][0])]
    hg = as_units(a["hg_w_in_2"][0]).reshape(5, NB, P, UNIT)
    parts += [np.stack([hg[p] for p in range(4)], 1).reshape(32, P, UNIT), hg[4], as_units(a["hg_w_out_2"][0])]

    def mlp(i):
        w1 = as_units(a["w_mlp_in_2"][i]).reshape(4, 8, P, UNIT)
        w2 = np.stack([as_units(a["w_mlp_out_2"][i][q * D:(q + 1) * D]) for q in range(4)])
        e = blocks(a["w_ple_proj_2"][i]).reshape(2, 4, P, 2, P).transpose(0, 2, 1, 3, 4).reshape(2, P, UNIT)
        return [np.stack([w1, w2], 1).reshape(64, P, UNIT), e, as_units(a["w_ple_gate_2"][i])]

    parts += mlp(0)
    w = a["mla_w_in_2"][0]
    kr = w[:, 640:704]
    ks = np.concatenate([kr[:, 32:], kr[:, :32]], 1)
    parts.append(as_units(np.concatenate([w[:, :640], kr, kr, ks, ks], 1)))
    uq = a["mla_w_uq_2"][0].reshape(384, MH, 192)
    ukv = a["mla_w_ukv_2"][0].reshape(256, MH, 256)
    swap = np.concatenate([uq[:, :, 160:192], uq[:, :, 128:160]], 2)
    pad = np.zeros((P, 3, P), np.float32)
    wo = a["mla_w_o_2"][0]
    for half in range(2):
        for j in range(4):
            h = 8 * half + 2 * j
            cols = [blocks(uq[:, h + e, :128])[0] for e in range(2)]
            cols += [blocks(x.reshape(384, P))[0] for x in (uq[:, h:h + 2, 128:], swap[:, h:h + 2])]
            for e in range(2):
                uk = ukv[:, h + e, :128].T
                cols[e] = np.concatenate([cols[e], uk.reshape(P, 2, P), pad], 1)
                cols[2 + e] = np.concatenate([cols[2 + e], blocks(ukv[:, h + e, 128:])[0], pad], 1)
            parts.append(np.stack(cols).reshape(4, P, UNIT))
        parts.append(as_units(wo[half * D:(half + 1) * D]))
    parts += mlp(1)
    return np.ascontiguousarray(np.concatenate(parts))


def columns(v):
    return v.reshape(-1, P).T


def lay_out(a):
    f = {n: a[n + "_2"] for n in ("hg_lb", "o_norm") if n + "_2" in a}
    t = np.arange(16)
    inv = (1.0 / (np.float32(10000.0) ** (np.arange(0, 64, 2, dtype=np.float32) / np.float32(64)))).astype(np.float32)
    by_name = {
        "b_ada": columns(a["b_ada"]), "b_in": columns(a["b_in"]), "pool_scale": columns(a["pool_scale"]),
        "sc_w": a["sc_w"][0].reshape(3, NB, P).transpose(2, 1, 0).reshape(P, -1), "sc_b": columns(a["sc_b"]),
        "cf_w": a["cf_w"][0].reshape(TAPS, NB, P).transpose(2, 1, 0).reshape(P, -1), "cf_b": columns(a["cf_b"]),
        "cf_ln_g": columns(a["cf_ln_g"]), "cf_ln_b": columns(a["cf_ln_b"]), "ln_g": columns(a["ln_g"]),
        "ln_b": columns(a["ln_b"]), "pre_mix": columns(a["pre_mix_norm_2"]), "post_mix": columns(a["post_mix_norm_2"]),
        "pre_mlp": columns(a["pre_mlp_norm_2"]), "post_mlp": columns(a["post_mlp_norm_2"]),
        "ple_norm": columns(a["ple_norm_2"]), "hg_lb": columns(a["hg_lb_logits_2"]),
        "o_norm": columns(a["hg_o_norm_2"]), "q_norm": columns(a["mla_q_norm_2"]), "kv_norm": columns(a["mla_kv_norm_2"]),
        "inv_freq": np.tile(inv, 4)[:, None], "rope_sign": np.tile(np.repeat([-1.0, 1.0], 32), 2)[:, None],
        "c": columns(a["c"]),
        "inv_count": np.tile(np.concatenate([1.0 / np.minimum(t + 1, w) for w in POOLS]), (P, 1)),
    }
    params = np.concatenate([by_name[n].astype(np.float32) for n, _ in PARAMS], 1)
    assert params.shape == (P, NCOL)

    def turned(x):
        return np.ascontiguousarray(x.T.reshape(-1, P, T).transpose(1, 0, 2))

    tok = np.arange(P)
    same = tok[:, None] // CH == tok[None, :] // CH
    fwd = same & (tok[:, None] <= tok[None, :])
    bwd = same & (tok[:, None] >= tok[None, :])
    mask = np.stack([np.tile(fwd, (1, 4)), np.tile(bwd, (1, 4))], 1).astype(np.int32)
    return {
        "weights": weight_stream(a), "x": turned(a["x"][0]), "params": np.ascontiguousarray(params),
        "ident": np.eye(P, dtype=np.float32), "mask": mask,
        "reset": np.tile((np.arange(T) % CH != 0).astype(np.float32), (P, 1)),
        "p0": turned(a["p_2"][0, 0]), "p1": turned(a["p_2"][1, 0]), "positions": a["positions_2"].reshape(T),
    }


def kernel(**inputs):
    import concourse.bacc as _bacc
    from concourse.bass_utils import run_bass_kernel_spmd as _run

    arrays = lay_out({n: np.asarray(v) for n, v in inputs.items()})
    nc = _bacc.Bacc("TRN2", target_bir_lowering=False, num_devices=1, dynamic_dma_scratch_size=1024)
    ins = {n: nc.dram_tensor(f"{n}_dram", v.shape, mybir.dt.from_np(v.dtype), kind="ExternalInput").ap()
           for n, v in arrays.items()}
    out = nc.dram_tensor("out", (NB, P, T), F32, kind="ExternalOutput").ap()
    build(nc, ins, out)
    r = _run(nc, [{f"{n}_dram": v for n, v in arrays.items()}], core_ids=[0])
    return r.results[0]["out"].reshape(D, T).T.reshape(1, T, D)
```

```python
from contextlib import ExitStack

import numpy as np

import concourse.bass as bass
from concourse import mybir

F32 = mybir.dt.float32
F32R = mybir.dt.float32r
I32 = mybir.dt.int32
ALU = mybir.AluOpType
ACT = mybir.ActivationFunctionType
AX_X = mybir.AxisListType.X

P = 128
T = 512
D = 1024
NB = D // P
RING = 4
UNIT = 8 * P
TAPS = 31
POOLS = (2, 4, 8, 16)
ALPHA = 2.0 ** 0.25
LN_EPS = 1e-5
RMS_EPS = 1e-6
CH = 64
NCH = T // CH
HEADS = 8
MH = 16
MLA_SCALE = float(128 + 64) ** -0.5
TWO_PI = 6.283185307179586
PI_LO = 3.1415925

PARAMS = (("b_ada", 24), ("b_in", 96), ("pool_scale", 8), ("sc_w", 24), ("sc_b", 8), ("cf_w", 8 * TAPS),
          ("cf_b", 8), ("cf_ln_g", 8), ("cf_ln_b", 8), ("ln_g", 8), ("ln_b", 8), ("pre_mix", 16),
          ("post_mix", 16), ("pre_mlp", 16), ("post_mlp", 16), ("ple_norm", 16), ("hg_lb", 24),
          ("o_norm", 8), ("q_norm", 3), ("kv_norm", 2), ("inv_freq", 1), ("rope_sign", 1), ("c", 8), ("inv_count", 64))
COL = {}
_at = 0
for _name, _n in PARAMS:
    COL[_name] = _at
    _at += _n
NCOL = _at

BRANCH_UNITS = (7, 6, 3, 4, 5, 2, 1, 8)
BRANCH_ACT = {0: (7, ACT.Sigmoid), 2: (3, ACT.Identity), 4: (5, ACT.Sigmoid), 6: (1, ACT.Sigmoid), 7: (8, ACT.Sigmoid)}

STREAM = (("ada", 16), ("proj", 64), ("avp", 10), ("merge1", 16), ("merge0", 16), ("merge2", 16), ("adag", 8),
          ("wout", 8), ("hg", 32), ("hggate", 8), ("hgout", 8), ("mlp0", 64), ("plee0", 2), ("pleg0", 8),
          ("mlain", 7), ("heads0", 16), ("wo0", 8), ("heads1", 16), ("wo1", 8), ("mlp1", 64),
          ("plee1", 2), ("pleg1", 8))
U0 = {}
_at = 0
for _name, _n in STREAM:
    U0[_name] = _at
    _at += _n
UNITS = _at

PAIR = 21
SPLITS = (("u", 8, 1), ("yb", 8, 1), ("ya", 16, 1), ("yc", 8, 1), ("m", 8, 1), ("mix0", 8, 0), ("o", 8, 1),
          ("mlp0", 8, 0), ("f0", 32, 0), ("p0", 2, 0), ("ple0", 8, 0), ("mix1", 8, 0), ("cqkv", 5, 1), ("kr", 1, 1),
          ("ckt", 2, 0), ("pairs0", 4 * PAIR, 0.5), ("pairs1", 4 * PAIR, 0.5), ("mlp1", 8, 0), ("f1", 32, 0),
          ("p1", 2, 0), ("ple1", 8, 0))
K0, V0 = {}, {}
_at = _val = 0
for _name, _n, _has in SPLITS:
    K0[_name], V0[_name] = _at, _val
    _at += _n
    _val += {1: _n, 0: 0, 0.5: 4}[_has]

NORMS = (("ln_in", 8), ("ln_c", 8), ("ln_out", 8), ("mix0", 8), ("o", 8), ("post_mix0", 8), ("mlp0", 8),
         ("post_mlp0", 8), ("post_ple0", 8), ("mix1", 8), ("cqkv", 5), ("post_mix1", 8), ("mlp1", 8),
         ("post_mlp1", 8), ("post_ple1", 8))
Q0, R0 = {}, {}
_at = _i = 0
for _name, _n in NORMS:
    Q0[_name], R0[_name] = _at, _i
    _at += _n
    _i += 1


A0 = {"proj": 1, "merge1": 1 + 5 * NB, "merge0": 1 + 6 * NB, "merge2": 1 + 8 * NB}
TOTALS = ("ln_c", "post_mix0", "mlp0", "post_mlp0", "post_ple0", "mix1", "post_mix1", "mlp1", "post_mlp1", "post_ple1")
STD0 = {n: i for i, n in enumerate(("ln_in", "ln_c", "ln_out", "mix0", "post_mix0", "mlp0", "post_mlp0", "post_ple0",
                                    "mix1", "cqkv", "cqkv_second", "post_mix1", "mlp1", "post_mlp1", "post_ple1"))}
ROUNDER = 12582912.0
TWO_PI_PARTS = (6.28125, 0.0019350051879882812, 3.0199159819567e-07)


class Steps:

    def __init__(self, eng, sem):
        self.eng, self.sem, self.base, self.n = eng, sem, 0, 0

    def did(self, ins):
        ins.then_inc(self.sem, 1)
        self.n += 1

    def wait(self):
        self.eng.wait_ge(self.sem, self.base + self.n)

    def loop(self, rounds, per):
        return _Loop(self, rounds, per)


class _Loop:
    def __init__(self, steps, rounds, per):
        self.steps, self.rounds, self.per = steps, rounds, per

    def __enter__(self):
        k = self.steps
        self.before = k.base + k.n
        self.fori = k.eng.Fori(0, self.rounds)
        r = self.fori.__enter__()
        k.base, k.n = r * self.per + self.before, 0
        return r

    def __exit__(self, *exc):
        k = self.steps
        assert exc[0] or k.n == self.per, f"the loop signals {k.n} times a round, not {self.per}"
        k.base, k.n = self.before + self.rounds * self.per, 0
        return self.fori.__exit__(*exc)


def blk(buf, j):
    if isinstance(j, int):
        return buf[:, j, :]
    return buf[:, bass.ds(j, 1), :].rearrange("p a n -> p (a n)")


def cut(t, i):
    return t[:, i * P:(i + 1) * P]


def build(nc, ins, out):
    ctx = ExitStack()
    with ctx:
        def sb(name, shape, dt=F32, stack=ctx):
            return stack.enter_context(nc.sbuf_tensor(name, shape, dt))

        def sem(name):
            return ctx.enter_context(nc.semaphore(name))

        stage = sb("stage", [P, RING, UNIT])
        w_hi = sb("w_hi", [P, RING, UNIT], F32R)
        w_lo = sb("w_lo", [P, RING, UNIT], F32R)
        x_hi = sb("x_hi", [P, NB, T], F32R)
        x_lo = sb("x_lo", [P, NB, T], F32R)
        hres = sb("hres", [P, NB, T])
        acc = sb("acc", [P, NB, T])
        prm = sb("prm", [P, NCOL])
        ones = sb("ones", [P, P])
        ident = sb("ident", [P, P])
        mod = sb("mod", [P, 24])
        mean = sb("mean", [P, T])
        std = sb("std", [P, T])
        rstd_pre = sb("rstd_pre", [P, T])
        rstd_post = sb("rstd_post", [P, T])
        sq = sb("sq", [P, 2, T])
        tmp = sb("tmp", [P, 2, T])
        sig = sb("sig", [P, 2, T])
        consts = sb("consts", [P, 2])
        lbt = sb("lbt", [P, 40])
        small = sb("small", [P, 8])
        with ExitStack() as own:
            ya_hi = sb("ya_hi", [P, NB, T], F32R, own)
            ya_lo = sb("ya_lo", [P, NB, T], F32R, own)
            yb_hi = sb("yb_hi", [P, NB, T], F32R, own)
            yb_lo = sb("yb_lo", [P, NB, T], F32R, own)
            gate_c = sb("gate_c", [P, NB, T], F32, own)
            zpad = sb("zpad", [P, TAPS - 1 + T], F32, own)
            qpad = sb("qpad", [P, 2 + T], F32, own)
        with ExitStack() as own:
            y_hi = sb("y_hi", [P, NB, T], F32R, own)
            y_lo = sb("y_lo", [P, NB, T], F32R, own)
            with ExitStack() as own2:
                p_in = sb("p_in", [P, 2, T], F32, own2)
                p_hi = sb("p_hi", [P, 2, T], F32R, own2)
                p_lo = sb("p_lo", [P, 2, T], F32R, own2)
                e_buf = sb("e_buf", [P, NB, T], F32, own2)
            with ExitStack() as own2:
                hq = sb("hq", [P, T], F32, own2)
                hvT = sb("hvT", [P, T], F32, own2)
                hf = sb("hf", [P, 2, T], F32, own2)
                hk = sb("hk", [P, 2, T], F32, own2)
                hg = sb("hg", [P, 2, T], F32, own2)
                hG = sb("hG", [P, 2, T], F32, own2)
                hE = sb("hE", [P, 2, T], F32, own2)
                hI = sb("hI", [P, 2, T], F32, own2)
                v_tok = sb("v_tok", [P, T], F32, own2)
                k_tok = sb("k_tok", [P, 2, T], F32, own2)
                attn = sb("attn", [P, 2, T], F32, own2)
                state = sb("state", [P, 2, NCH, P], F32, own2)
                mask = sb("mask", [P, 2, T], I32, own2)
                reset = sb("reset", [P, T], F32, own2)
        with ExitStack() as own:
            ckv_hi = sb("ckv_hi", [P, 2, T], F32R, own)
            ckv_lo = sb("ckv_lo", [P, 2, T], F32R, own)
            ckt_hi = sb("ckt_hi", [P, 4, 2 * P], F32R, own)
            ckt_lo = sb("ckt_lo", [P, 4, 2 * P], F32R, own)
            kr_hi = sb("kr_hi", [P, T], F32R, own)
            kr_lo = sb("kr_lo", [P, T], F32R, own)
            cq_hi = sb("cq_hi", [P, 3, T], F32R, own)
            cq_lo = sb("cq_lo", [P, 3, T], F32R, own)
            qn_hi = sb("qn_hi", [P, 2, T], F32R, own)
            qn_lo = sb("qn_lo", [P, 2, T], F32R, own)
            ql_hi = sb("ql_hi", [P, 4, T], F32R, own)
            ql_lo = sb("ql_lo", [P, 4, T], F32R, own)
            qr_hi = sb("qr_hi", [P, T], F32R, own)
            qr_lo = sb("qr_lo", [P, T], F32R, own)
            pt_hi = sb("pt_hi", [P, 4, T], F32R, own)
            pt_lo = sb("pt_lo", [P, 4, T], F32R, own)
            ol_hi = sb("ol_hi", [P, 2, T], F32R, own)
            ol_lo = sb("ol_lo", [P, 2, T], F32R, own)
            pos_i = sb("pos_i", [P, T], I32, own)
        probs = sq
        cos, sin = mean, rstd_post

        bank = [ctx.enter_context(nc.psum_tensor(f"bank{i}", [P, T], F32)) for i in range(8)]

        loaded = [sem(f"unit_loaded{i}") for i in range(RING)]
        rounded = sem("unit_rounded")
        split = sem("unit_split")
        mm_done = sem("unit_multiplied")
        freed = sem("bank_freed")

        consts_in = sem("consts_in")
        x_in = sem("x_in")
        consts_set = sem("consts_set")
        out_sent = sem("out_sent")

        def c_rep(buf, k):
            return buf[:, k // 4, k % 4 * P:(k % 4 + 1) * P]

        def prm_col(name, j=0):
            if isinstance(j, int):
                return prm[:, COL[name] + j:COL[name] + j + 1]
            return prm[:, bass.ds(j + COL[name], 1)]

        sq_ready = sem("square_ready")
        sq_used = sem("square_summed")
        totalled = sem("squares_totalled")
        std_ready = sem("std_ready")
        rstd_ready = sem("rstd_ready")
        sum_done = sem("sum_done")
        mean_ready = sem("mean_ready")
        centred = sem("centred")

        block = ctx.enter_context(nc.Block())

        c_ready = sem("c_ready")
        act_done = sem("branch_act_done")
        hc_ready = sem("conv_ready")
        pool_mm = sem("pool_multiplied")
        r_ready = sem("row_ready")
        val_ready = sem("value_ready")
        hi_ready = sem("hi_ready")
        lo_ready = sem("lo_ready")
        h_ready = sem("h_ready")
        ln_ready = sem("ln_ready")
        step = sem("dve_step")
        lb_exp = sem("lb_exp")
        lb_in = sem("lb_in")

        gla_in = sem("gla_consts_in")
        gla_act = sem("gla_act")
        gla_dve = sem("gla_dve")
        decayed = sem("decayed")
        kend_ready = sem("kend_ready")
        masked = sem("masked")
        states_done = sem("states_done")
        attn_mm = sem("attn_mm")
        v_turned = sem("v_turned")
        k_turned = sem("k_turned")
        kv_mm = sem("kv_mm")
        o_mm = sem("o_mm")
        o_read = sem("o_read")
        tok_copied = sem("tok_copied")
        o_rstd = sem("o_rstd")
        o_normed = sem("o_normed")
        gate_sig = sem("gate_sig")

        squared = sem("squared")
        p_arrived = sem("p_arrived")
        e_mm = sem("e_mm")
        ple_sig = sem("ple_sig")

        pos_in = sem("pos_in")
        trig_arg = sem("trig_arg")
        trig = sem("trig")
        cq_std = sem("cq_std")
        ckt_mm = sem("ckt_mm")
        q_mm = sem("q_mm")
        sc_mm = sem("score_mm")
        mx_ready = sem("max_ready")
        exp_done = sem("exp_done")
        p_ready = sem("prob_ready")
        pt_mm = sem("prob_turned")
        pv_mm = sem("pv_mm")
        uv_mm = sem("uv_mm")

        @block.sync
        def _(sp):
            units = ins["weights"]

            def load(u, s, src):
                sp.dma_start(stage[:, s, :], src).then_inc(loaded[s], 16)

            for s in range(RING):
                load(s, s, units[s])
            with sp.Fori(1, UNITS // RING) as r:
                for s in range(RING):
                    sp.wait_ge(split, r * RING + (s - RING + 1))
                    load(0, s, units[bass.ds(r * RING + s, 1)].rearrange("a p n -> p (a n)"))
            for u in range(UNITS // RING * RING, UNITS):
                sp.wait_ge(split, u - RING + 1)
                load(u, u % RING, units[u])
            for j in range(NB):
                sp.wait_ge(h_ready, 8 * 6 + j + 1)
                sp.dma_start(out[j], hres[:, j, :]).then_inc(out_sent, 16)
            sp.wait_ge(out_sent, 16 * NB)

        @block.gpsimd
        def _(pool):
            def lo(u, s):
                pool.wait_ge(rounded, u + 1)
                nc.gpsimd.tensor_tensor(w_lo[:, s, :], stage[:, s, :], w_hi[:, s, :].bitcast(F32),
                                        ALU.subtract).then_inc(split, 1)

            with pool.Fori(0, UNITS // RING) as r:
                for s in range(RING):
                    lo(r * RING + s, s)
            for u in range(UNITS // RING * RING, UNITS):
                lo(u, u % RING)

        @block.tensor
        def _(pe):
            def mm3(o, wh, wl, xh, xl, start, stop):
                nc.tensor.matmul(o, wh, xh, start=start, stop=False)
                nc.tensor.matmul(o, wh, xl, start=False, stop=False)
                return nc.tensor.matmul(o, wl, xh, start=False, stop=stop)

            def unit(u, s, xh, xl, ready=None, b=None):
                pe.wait_ge(split, u + 1)
                if b is None:
                    pe.wait_ge(freed, u - (RING - 1))
                else:
                    pe.wait_ge(freed, u - 7)
                for k in range(8):
                    if ready is not None:
                        pe.wait_ge(lo_ready, ready + (k + 1))
                    last = mm3(bank[s if b is None else b][:, :], cut(w_hi[:, s, :], k), cut(w_lo[:, s, :], k),
                               xh[:, k, :], xl[:, k, :], k == 0, k == 7)
                last.then_inc(mm_done, 1)

            def quad(u, s, xs, ready, wide=False):
                for k in range(8):
                    pe.wait_ge(lo_ready, ready + (k + 1))
                    for i in range(RING):
                        slot, (xh, xl) = (s + i) % RING, xs[i % len(xs)]
                        if k == 0:
                            pe.wait_ge(split, u + (i + 1))
                            pe.wait_ge(freed, u + (i - RING + 1))
                        last = mm3(bank[i if wide else slot][:, :], cut(w_hi[:, slot, :], k), cut(w_lo[:, slot, :], k),
                                   xh[:, k, :], xl[:, k, :], k == 0, k == 7)
                        if k == 7:
                            last.then_inc(mm_done, 1)

            def units(name, n, xs, ready, slow=False, then=lambda: None):
                if slow:
                    quad(U0[name], U0[name] % RING, xs, ready)
                else:
                    for i in range(RING):
                        unit(U0[name] + i, (U0[name] + i) % RING, *xs[i % len(xs)],
                             ready=ready if i == len(xs) - 1 else None)
                then()
                if n == 2 * RING:
                    for i in range(RING, n):
                        unit(U0[name] + i, (U0[name] + i) % RING, *xs[i % len(xs)])
                    return
                with pe.Fori(1, n // RING) as r:
                    for i in range(RING):
                        unit(r * RING + (U0[name] + i), (U0[name] + i) % RING, *xs[i % len(xs)])

            def sum_features(src, ready, base):
                for k in range(NB):
                    pe.wait_ge(ready, base(k))
                    last = nc.tensor.matmul(bank[6][:, :], ones[:, :], src[:, k, :], start=k == 0, stop=k == NB - 1)
                last.then_inc(sum_done, 1)

            def sum_squares(name, n=NB, b=7, first=0, size=None):
                for k in range(n):
                    pe.wait_ge(sq_ready, Q0[name] + first + k + 1)
                    nc.tensor.matmul(bank[b][:, :], ones[:, :], sq[:, (first + k) % 2, :],
                                     start=k == 0, stop=k == n - 1).then_inc(sq_used, 1)

            def sum_total(name, b=7):
                pe.wait_ge(sq_used, Q0[name] + NB)
                nc.tensor.matmul(bank[b][:, :], ones[:, :], std[:, :], start=True, stop=True).then_inc(totalled, 1)

            def operand(name, n):
                pe.wait_ge(lo_ready, K0[name] + n)

            def modulation(name, first, b):
                pe.wait_ge(c_ready, 1 if name == "ada" else 2)
                if name == "adag":
                    pe.wait_ge(freed, U0[name])
                for k in range(8):
                    u = U0[name] + first + k
                    s = u % RING
                    pe.wait_ge(split, u + 1)
                    for n in range(2):
                        half = slice(n * T, (n + 1) * T)
                        last = mm3(bank[b + n][:, :], c_rep(x_hi, k), c_rep(x_lo, k), w_hi[:, s, half], w_lo[:, s, half],
                                   k == 0, k == 7)
                    last.then_inc(mm_done, 1)

            pe.wait_ge(consts_set, 1)
            pe.wait_ge(x_in, 16)
            sum_features(hres, x_in, lambda k: 16)
            modulation("ada", 0, 0)
            sum_squares("ln_in")
            modulation("ada", 8, 2)
            units("proj", 64, [(x_hi, x_lo)], K0["u"], slow=True)
            for half in range(2):
                a0 = U0["avp"] + 5 * half
                for i in range(4):
                    unit(a0 + i, (a0 + i) % RING, x_hi, x_lo)
                s = (a0 + 4) % RING
                pe.wait_ge(split, a0 + 5)
                for g in (2 * half, 2 * half + 1):
                    operand("ya", 8 * half + 2 * (g % 2) + 2)
                    if half:
                        operand("ya", 8)
                    for m in range(2):
                        o = bank[4 + 2 * (g % 2) + m][:, :]
                        for k in range(2):
                            i = 4 * (g % 2) + 2 * k + m
                            last = mm3(o, cut(w_hi[:, s, :], i), cut(w_lo[:, s, :], i),
                                       ya_hi[:, 2 * g + k, :], ya_lo[:, 2 * g + k, :], k == 0, k == 1)
                    last.then_inc(mm_done if g % 2 else pool_mm, 1)
            operand("ya", 16)
            sum_features(hres, hc_ready, lambda k: k + 2)
            units("merge1", 16, [(x_hi, x_lo), (yb_hi, yb_lo)], K0["yb"], then=lambda: sum_total("ln_c"))
            units("merge0", 16, [(x_hi, x_lo), (ya_hi, ya_lo)], K0["ya"] + 8)
            units("merge2", 16, [(x_hi, x_lo), (yb_hi, yb_lo)], K0["yc"])
            modulation("adag", 0, 0)
            units("wout", 8, [(ya_hi, ya_lo)], K0["m"])
            sum_features(hres, r_ready, lambda k: k + 1)
            sum_squares("ln_out")
            sum_squares("mix0")

            def head_units(h):
                for i in range(4):
                    unit(h * 4 + (U0["hg"] + i), (U0["hg"] + i) % RING, x_hi, x_lo)

            def pairs(t, p):
                return t[:, p * P:(p + 1) * P]

            def gla(c):
                pe.wait_ge(decayed, c * 2 - 1)
                for p in range(4):
                    last = nc.tensor.matmul(pairs(bank[7], p), pairs(hI[:, 0, :], p), pairs(hf[:, 0, :], p),
                                            start=True, stop=True)
                last.then_inc(attn_mm, 1)
                pe.wait_ge(freed, c * 4 + U0["hg"])
                pe.wait_ge(o_read, c)
                for p in range(4):
                    last = nc.tensor.transpose(pairs(bank[4], p), pairs(hvT[:, :], p), ident[:, :])
                last.then_inc(v_turned, 1)
                pe.wait_ge(kend_ready, c * 2 - 1)
                for p in range(4):
                    last = nc.tensor.transpose(pairs(bank[5], p), pairs(hg[:, 0, :], p), ident[:, :])
                last.then_inc(k_turned, 1)
                pe.wait_ge(decayed, c * 2)
                for p in range(4):
                    last = nc.tensor.matmul(pairs(bank[6], p), pairs(hI[:, 1, :], p), pairs(hf[:, 1, :], p),
                                            start=True, stop=True)
                last.then_inc(attn_mm, 1)
                pe.wait_ge(kend_ready, c * 2)
                pe.wait_ge(masked, c * 2 - 1)
                for p in range(4):
                    last = nc.tensor.transpose(pairs(bank[7], p), pairs(hg[:, 1, :], p), ident[:, :])
                last.then_inc(k_turned, 1)

                def chunk_kv(d, n):
                    half, p = 64 * (n % 2), n // 2
                    return nc.tensor.matmul(pairs(bank[4 + 2 * d + n % 2], n // 2),
                                            k_tok[half:half + CH, d, p * P:(p + 1) * P],
                                            v_tok[half:half + CH, p * P:(p + 1) * P], start=True, stop=True)

                pe.wait_ge(tok_copied, c * 3 - 1)
                for n in range(NCH - 1):
                    last = chunk_kv(0, n)
                last.then_inc(kv_mm, 1)
                pe.wait_ge(tok_copied, c * 3)
                pe.wait_ge(masked, c * 2)
                for n in range(NCH - 1, 0, -1):
                    last = chunk_kv(1, n)
                last.then_inc(kv_mm, 1)
                pe.wait_ge(states_done, c * 2 - 1)
                for d in range(2):
                    if d:
                        pe.wait_ge(states_done, c * 2)
                    for p in range(4):
                        nc.tensor.matmul(pairs(bank[4], p), pairs(v_tok[:, :], p), pairs(attn[:, d, :], p),
                                         start=d == 0 and p == 0, stop=False, skip_group_check=True)
                    for n in range(1 - d, NCH - d):
                        last = nc.tensor.matmul(bank[4][:, n * CH:(n + 1) * CH], state[:, d, n, :],
                                                hf[:, d, n * CH:(n + 1) * CH], start=False,
                                                stop=d == 1 and n == NCH - 2, skip_group_check=True)
                last.then_inc(o_mm, 1)

            quad(U0["hg"], U0["hg"] % RING, [(x_hi, x_lo)], K0["mix0"])
            with pe.Fori(1, HEADS) as h:
                head_units(h)
                gla(h)
            gla(HEADS)
            for h in range(HEADS):
                pe.wait_ge(sq_ready, Q0["o"] + h + 1)
                if h >= 2:
                    pe.wait_ge(o_rstd, h - 1)
                nc.tensor.matmul(bank[6 + h % 2][:, :], ones[:, :], sq[:, h % 2, :],
                                 start=True, stop=True).then_inc(sq_used, 1)
            units("hggate", 8, [(x_hi, x_lo)], K0["mix0"])
            units("hgout", 8, [(y_hi, y_lo)], K0["o"])

            def mlp(i):
                sum_total(f"post_mix{i}")
                name = f"mlp{i}"

                def quarter(q):
                    for v in range(8):
                        if v or not isinstance(q, int):
                            if not isinstance(q, int) or v >= 4:
                                if v == 7 and isinstance(q, int):
                                    pe.wait_ge(std_ready, STD0[name] + 1)
                                unit(q * 16 + (U0[name] + v), (U0[name] + v) % RING, x_hi, x_lo, b=v)
                        else:
                            quad(U0[name], U0[name] % RING, [(x_hi, x_lo)], K0[name], wide=True)
                            sum_total(name)
                    for v in range(8, 16):
                        unit(q * 16 + (U0[name] + v), (U0[name] + v) % RING, y_hi, y_lo,
                             ready=q * 8 + K0[f"f{i}"] if v == 8 else None, b=v - 8)

                quarter(0)
                with pe.Fori(1, 4) as q:
                    quarter(q)

            def ple(i):
                pe.wait_ge(freed, U0[f"plee{i}"])
                sum_total(f"post_mlp{i}", 3)
                operand(f"p{i}", 2)
                for e in range(2):
                    u = U0[f"plee{i}"] + e
                    pe.wait_ge(split, u + 1)
                    if e:
                        pe.wait_ge(freed, u)
                    for o in range(4):
                        for k in range(2):
                            w = 2 * o + k
                            last = mm3(bank[4 + o][:, :], cut(w_hi[:, u % RING, :], w), cut(w_lo[:, u % RING, :], w),
                                       p_hi[:, k, :], p_lo[:, k, :], k == 0, k == 1)
                    last.then_inc(mm_done, 1)
                units(f"pleg{i}", 8, [(x_hi, x_lo)], K0[f"ple{i}"], slow=True)
                sum_total(f"post_ple{i}")

            mlp(0)
            ple(0)

            quad(U0["mlain"], U0["mlain"] % RING, [(x_hi, x_lo)], K0["mix1"], wide=True)
            sum_total("mix1")
            for i in range(RING, 7):
                unit(U0["mlain"] + i, (U0["mlain"] + i) % RING, x_hi, x_lo, b=i)
            pe.wait_ge(freed, U0["mlain"] + 7)
            sum_squares("cqkv", 3, 6)
            sum_squares("cqkv", 2, 7, 3)
            pe.wait_ge(val_ready, V0["cqkv"] + 5)
            for c in range(2):
                for k in range(4):
                    last = nc.tensor.transpose(pairs(bank[4 + c], k), pairs(acc[:, 3 + c, :], k), ident[:, :])
                last.then_inc(ckt_mm, 1)
            operand("ckt", 2)

            def head_pair(j, name):
                n = int(name[-1])
                hp = j + 4 * n
                u = j * 4 + U0[f"heads{n}"]
                sl = [(U0[f"heads{n}"] + i) % RING for i in range(4)]
                cuts = j * PAIR + K0[f"pairs{n}"]

                def w(which, i):
                    s = sl[which]
                    return cut(w_hi[:, s, :], i), cut(w_lo[:, s, :], i)

                def down(b, which):
                    for k in range(3):
                        last = mm3(bank[b][:, :], *w(which, k), cq_hi[:, k, :], cq_lo[:, k, :], k == 0, k == 2)
                    return last

                pe.wait_ge(split, u + 1)
                pe.wait_ge(lo_ready, cuts)
                down(0, 0).then_inc(q_mm, 1)
                pe.wait_ge(split, u + 3)
                down(1, 2)
                pe.wait_ge(split, u + 4)
                down(2, 3).then_inc(q_mm, 1)
                down(3, 1).then_inc(q_mm, 1)
                for e in range(2):
                    pe.wait_ge(lo_ready, cuts + (2 if e == 0 else 3))
                    for c in range(2):
                        last = mm3(bank[2 * e + c][:, :], *w(e, 3 + c), qn_hi[:, e, :], qn_lo[:, e, :], True, True)
                    last.then_inc(mm_done, 1)

                def scores(i):
                    e, qb = i // 4, i % 4
                    if i % 4 == 0:
                        pe.wait_ge(lo_ready, cuts + (5 + 2 * e))
                    if i >= 2:
                        pe.wait_ge(exp_done, hp * 8 + (i - 1))
                    o = bank[4 + i % 2][:, :]
                    q = slice(qb * P, (qb + 1) * P)
                    for c in range(2):
                        mm3(o, ql_hi[:, 2 * e + c, q], ql_lo[:, 2 * e + c, q], ckv_hi[:, c, :], ckv_lo[:, c, :],
                            c == 0, False)
                    r = slice(64 * e, 64 * e + 64)
                    mm3(o, qr_hi[r, q], qr_lo[r, q], kr_hi[r, :], kr_lo[r, :], False, True).then_inc(sc_mm, 1)

                PT = [7, 8, 9, 10, 13, 14, 16, 17]

                def turn(i):
                    pe.wait_ge(p_ready, hp * 8 + (i + 1))
                    if i >= 2:
                        pe.wait_ge(lo_ready, cuts + (PT[i - 2] + 1))
                    for k in range(4):
                        last = nc.tensor.transpose(pairs(bank[6 + i % 2], k), pairs(probs[:, i % 2, :], k), ident[:, :])
                    last.then_inc(pt_mm, 1)

                def weigh(e):
                    pe.wait_ge(lo_ready, cuts + (PT[4 * e + 3] + 1))
                    for c in range(2):
                        for k in range(4):
                            last = mm3(bank[c][:, :], ckt_hi[:, k, c * P:(c + 1) * P], ckt_lo[:, k, c * P:(c + 1) * P],
                                       pt_hi[:, k, :], pt_lo[:, k, :], k == 0, k == 3)
                    last.then_inc(pv_mm, 1)

                def up(e):
                    pe.wait_ge(lo_ready, cuts + (13 if e == 0 else 20))
                    for c in range(2):
                        last = mm3(bank[2 + e][:, :], *w(2 + e, 3 + c), ol_hi[:, c, :], ol_lo[:, c, :], c == 0, c == 1)
                    last.then_inc(mm_done, 1)

                for t in range(10):
                    if t < 8:
                        scores(t)
                    if t == 6:
                        weigh(0)
                    if t >= 2:
                        turn(t - 2)
                    if t == 7:
                        up(0)
                weigh(1)
                up(1)

            for n in range(2):
                pe.wait_ge(freed, U0[f"heads{n}"])
                with pe.Fori(0, 4) as j:
                    head_pair(j, f"pairs{n}")
                operand(f"pairs{n}", 4 * PAIR)
                units(f"wo{n}", 8, [(x_hi, x_lo)], K0[f"pairs{n}"])
            mlp(1)
            ple(1)

        @block.scalar
        def _(act):
            def fn(o, i, f, **kw):
                return nc.scalar.activation(o, i, f, **kw)

            def tick(name, i, r=0, per=0):
                u = U0[name] + i
                if isinstance(r, int):
                    u, r = u + per * r, 0
                    if u + RING >= UNITS:
                        return
                act.wait_ge(mm_done, r * per + (u + 1))
                act.wait_ge(loaded[u % RING], r * (16 * per // RING) + 16 * (u // RING + 2))
                fn(w_hi[:, u % RING, :], stage[:, u % RING, :], ACT.Copy).then_inc(rounded, 1)

            def closing(phase, norm, i, r=0, first=0):
                j = r * 4 + i
                act.wait_ge(freed, j + (U0[phase] + first + 1))
                act.wait_ge(sq_used, j + (Q0[norm] - 1))
                fn(sq[:, i % 2, :], blk(acc, j), ACT.Square).then_inc(sq_ready, 1)
                tick(phase, first + i, r, 4)

            def closing_ticks(phase, norm):
                with act.Fori(0, 2) as r:
                    for i in range(4):
                        closing(phase, norm, i, r)

            def ticks(name, n, group=RING, first=0):
                with act.Fori(first // group, (first + n) // group) as r:
                    for i in range(group):
                        tick(name, i, r, group)

            def root(name, n=NB, size=D, eps=RMS_EPS, o=std, b=7, first=0):
                if name in TOTALS:
                    act.wait_ge(totalled, TOTALS.index(name) + 1)
                else:
                    act.wait_ge(sq_used, Q0[name] + first + n)
                fn(o[:, :] if o is std else o, bank[b][:, :], ACT.Sqrt, bias=eps_col(eps),
                   scale=1.0 / size).then_inc(std_ready, 1)

            def eps_col(eps):
                return consts[:, 0:1] if eps == LN_EPS else consts[:, 1:2]

            def squares(name, src, ready, base, per=2, scale=1):
                def two(r):
                    for s in range(2):
                        act.wait_ge(ready, r * 2 * scale + (base + scale * (s + 1)))
                        if not isinstance(r, int) or Q0[name] + 2 * r + s >= 2:
                            act.wait_ge(sq_used, r * 2 + (Q0[name] + s - 1))
                        fn(sq[:, s, :], blk(src, r * 2 + s), ACT.Square).then_inc(sq_ready, 1)
                two(0)
                with act.Fori(1, 4) as r:
                    two(r)

            act.dma_start(hres[:, :, :], ins["x"]).then_inc(x_in, 16)
            act.dma_start(prm[:, :], ins["params"]).then_inc(consts_in, 16)
            act.dma_start(ident[:, :], ins["ident"]).then_inc(consts_in, 16)
            act.wait_ge(consts_in, 32)
            fn(sig[:, 0, 0:8], prm[:, COL["c"]:COL["c"] + NB], ACT.Sigmoid).then_inc(act_done, 1)
            for s in range(RING):
                act.wait_ge(loaded[s], 16)
                fn(w_hi[:, s, :], stage[:, s, :], ACT.Copy).then_inc(rounded, 1)
            act.wait_ge(lb_in, 1)
            fn(lbt[:, 0:24], lbt[:, 0:24], ACT.Exp).then_inc(lb_exp, 1)
            for i in range(8):
                tick("ada", i)
            squares("ln_in", acc, centred, 0)
            root("ln_in", eps=LN_EPS)
            for i in range(8, 16):
                tick("ada", i)
            with act.Fori(0, 4) as r:
                for s in range(2):
                    act.wait_ge(val_ready, r * 2 + (s + 1))
                    fn(blk(x_hi, r * 2 + s), blk(acc, r * 2 + s), ACT.Copy).then_inc(hi_ready, 1)

            def rounds(name, n, dst, src):
                for k in range(n):
                    act.wait_ge(val_ready, V0[name] + k + 1)
                    fn(dst(k), src(k), ACT.Copy).then_inc(hi_ready, 1)

            with act.Fori(0, NB) as j:
                for i in range(8):
                    act.wait_ge(mm_done, j * 8 + (U0["proj"] + i + 1))
                    if i in BRANCH_ACT:
                        part, func = BRANCH_ACT[i]
                        dst = {0: sig[:, 0, :], 2: mean[:, :], 4: sig[:, 1, :], 6: std[:, :], 7: rstd_pre[:, :]}[i]
                        fn(dst, bank[(U0["proj"] + i) % RING][:, :], func,
                           bias=prm_col("b_in", j + 8 * part)).then_inc(act_done, 1)
                    tick("proj", i, j, 8)
                act.wait_ge(val_ready, j + (V0["yb"] + 1))
                fn(blk(yb_hi, j), sq[:, 0, :], ACT.Copy).then_inc(hi_ready, 1)
            for half in range(2):
                for k in range(4):
                    tick("avp", 5 * half + k)
                    act.wait_ge(val_ready, V0["ya"] + 8 * half + k + 1)
                    fn(ya_hi[:, 4 * half + k, :], sig[:, k % 2, :], ACT.Copy).then_inc(hi_ready, 1)
                for k in range(4):
                    act.wait_ge(val_ready, V0["ya"] + 8 * half + 4 + k + 1)
                    fn(ya_hi[:, 4 * half + k, :], sig[:, k % 2, :], ACT.Copy).then_inc(hi_ready, 1)
                tick("avp", 5 * half + 4)

            def merge(i):
                name = f"merge{i}"
                with act.Fori(0, 4) as r:
                    for s in range(2 if i == 0 else 0):
                        act.wait_ge(ln_ready, r * 2 + (s + 1))
                        fn((mean, std)[s][:, :], blk(hres, r * 2 + s), ACT.Sigmoid, scale=prm_col("cf_ln_g", r * 2 + s),
                           bias=prm_col("cf_ln_b", r * 2 + s)).then_inc(act_done, 1)
                    for s in range(4):
                        if s % 2 == 0:
                            act.wait_ge(mm_done, r * 4 + (U0[name] + s + 1))
                            fn(sig[:, s // 2, :], bank[(U0[name] + s) % RING][:, :], ACT.Sigmoid,
                               bias=prm_col("b_in", r * 2 + (72 + 8 * i + s // 2))).then_inc(act_done, 1)
                        tick(name, s, r, 4)
                        if i == 2 and s % 2:
                            act.wait_ge(val_ready, r * 2 + (V0["m"] + s // 2 + 1))
                            fn(blk(ya_hi, r * 2 + s // 2), blk(acc, r * 2 + s // 2), ACT.Copy).then_inc(hi_ready, 1)
                        if i == 0 and s % 2:
                            act.wait_ge(val_ready, r * 2 + (V0["yc"] + s // 2 + 1))
                            fn(blk(yb_hi, r * 2 + s // 2), tmp[:, s // 2, :], ACT.Copy).then_inc(hi_ready, 1)

            squares("ln_c", hres, centred, 8)
            merge(1)
            root("ln_c", eps=LN_EPS)
            merge(0)
            act.wait_ge(lo_ready, K0["yc"] + 8)
            act.dma_start(hres[:, :, :], ins["x"]).then_inc(x_in, 16)
            merge(2)
            ticks("adag", 8)
            ticks("wout", 8)
            squares("ln_out", hres, centred, 16)
            root("ln_out", eps=LN_EPS)
            with act.Fori(0, 4) as r:
                for s in range(2):
                    act.wait_ge(ln_ready, r * 2 + (8 + s + 1))
                    fn(blk(hres, r * 2 + s), tmp[:, s, :], ACT.Identity, bias=prm_col("ln_b", r * 2 + s)
                       ).then_inc(h_ready, 1)
                    act.wait_ge(h_ready, r * 2 + (s + 1))
                    act.wait_ge(sq_used, r * 2 + (Q0["mix0"] + s - 1))
                    fn(blk(x_hi, r * 2 + s), blk(hres, r * 2 + s), ACT.Copy,
                       scale=prm_col("pre_mix", r * 2 + s)).then_inc(hi_ready, 1)
                    fn(sq[:, s, :], blk(hres, r * 2 + s), ACT.Square).then_inc(sq_ready, 1)
            root("mix0")

            act.dma_start(mask[:, :, :], ins["mask"]).then_inc(gla_in, 16)
            act.dma_start(reset[:, :], ins["reset"]).then_inc(gla_in, 16)

            def head_ticks(h):
                for i in range(4):
                    tick("hg", i, h, 4)

            def gates(h):
                for d in range(2):
                    act.wait_ge(freed, h * 4 + (U0["hg"] + d + 2))
                    fn(hf[:, d, :], hf[:, d, :], ACT.Sigmoid).then_inc(gla_act, 1)
                for d in range(2):
                    act.wait_ge(gla_dve, h * 6 + (d + 1))
                    fn(hg[:, d, :], hf[:, d, :], ACT.Ln).then_inc(gla_act, 1)
                for d in range(2):
                    act.wait_ge(gla_dve, h * 6 + (2 + d + 1))
                    fn(hE[:, d, :], hG[:, d, :], ACT.Exp).then_inc(gla_act, 1)
                    fn(hI[:, d, :], hG[:, d, :], ACT.Exp, scale=-1.0).then_inc(gla_act, 1)
                    act.wait_ge(gla_dve, h * 6 + (4 + d + 1))
                    fn(hg[:, d, :], hg[:, d, :], ACT.Exp).then_inc(gla_act, 1)

            def tokens(c):
                act.wait_ge(v_turned, c)
                fn(v_tok[:, :], bank[4][:, :], ACT.Copy).then_inc(tok_copied, 1)
                act.wait_ge(k_turned, c * 2 - 1)
                fn(k_tok[:, 0, :], bank[5][:, :], ACT.Copy).then_inc(tok_copied, 1)
                act.wait_ge(k_turned, c * 2)
                fn(k_tok[:, 1, :], bank[7][:, :], ACT.Copy).then_inc(tok_copied, 1)

            head_ticks(0)
            gates(0)
            with act.Fori(1, HEADS) as h:
                head_ticks(h)
                tokens(h)
                gates(h)
            tokens(HEADS)
            for h in range(HEADS):
                act.wait_ge(o_read, h + 2)
                if h >= 2:
                    act.wait_ge(sq_used, Q0["o"] + h - 1)
                fn(sq[:, h % 2, :], acc[:, h, :], ACT.Square).then_inc(sq_ready, 1)
                act.wait_ge(sq_used, Q0["o"] + h + 1)
                if h >= 2:
                    act.wait_ge(o_normed, h - 1)
                fn(sig[:, h % 2, :], bank[6 + h % 2][:, :], ACT.Ln, bias=consts[:, 1:2], scale=1.0 / P
                   ).then_inc(gla_act, 1)
                act.wait_ge(gla_act, 10 * HEADS + h + 1)
                fn(sig[:, h % 2, :], sig[:, h % 2, :], ACT.Exp, scale=-0.5).then_inc(o_rstd, 1)
            with act.Fori(0, 2) as r:
                for i in range(4):
                    tick("hggate", i, r, 4)
                    act.wait_ge(freed, r * 4 + (U0["hggate"] + i + 1))
                    fn(sig[:, i % 2, :], tmp[:, i % 2, :], ACT.Sigmoid).then_inc(gate_sig, 1)
                    act.wait_ge(val_ready, r * 4 + (V0["o"] + i + 1))
                    fn(blk(y_hi, r * 4 + i), tmp[:, i % 2, :], ACT.Copy).then_inc(hi_ready, 1)
            closing_ticks("hgout", "post_mix0")

            hblocks = {"mlp0": 1, "ple0": 2, "mix1": 3, "mlp1": 4, "ple1": 5, "end": 6}

            def next_operand(name, gain, layer, normed):
                with act.Fori(0, 4) as r:
                    for s in range(2):
                        act.wait_ge(h_ready, r * 2 + (8 * hblocks[name] + s + 1))
                        if normed:
                            act.wait_ge(sq_used, r * 2 + (Q0[name] + s - 1))
                        kw = dict(scale=prm_col(gain, r * 2 + (8 * layer + s))) if gain else {}
                        fn(blk(x_hi, r * 2 + s), blk(hres, r * 2 + s), ACT.Copy, **kw).then_inc(hi_ready, 1)
                        if normed:
                            fn(sq[:, s, :], blk(hres, r * 2 + s), ACT.Square).then_inc(sq_ready, 1)
                if normed:
                    root(name)

            def mlp(i):
                name = f"mlp{i}"
                act.dma_start(p_in[:, :, :], ins[f"p{i}"]).then_inc(p_arrived, 16)
                root(f"post_mix{i}")
                next_operand(name, "pre_mlp", i, True)
                def quarter(q):
                    for v in range(8):
                        s = v % 2
                        act.wait_ge(freed, q * 16 + (U0[name] + v + 1))
                        fn(tmp[:, s, :], tmp[:, s, :], ACT.Square).then_inc(squared, 1)
                        act.wait_ge(squared, q * 8 + (32 * i + v + 1))
                        fn(y_hi[:, v, :], tmp[:, s, :], ACT.Copy).then_inc(hi_ready, 1)
                        tick(name, v, q, 16)
                    if not isinstance(q, int):
                        for v in range(8, 16):
                            tick(name, v, q, 16)

                with act.Fori(0, 3) as q:
                    quarter(q)
                quarter(3)
                act.wait_ge(p_arrived, 16 * (i + 1))
                for k in range(2):
                    fn(p_hi[:, k, :], p_in[:, k, :], ACT.Copy).then_inc(hi_ready, 1)
                for v in range(8):
                    closing(name, f"post_mlp{i}", v, first=56)

            def ple(i):
                for e in range(2):
                    tick(f"plee{i}", e)
                root(f"post_mlp{i}", b=3)
                next_operand(f"ple{i}", None, 0, False)
                name = f"pleg{i}"

                def four(r):
                    for v in range(4):
                        if isinstance(r, int):
                            act.wait_ge(mm_done, r * 4 + U0[name] + v + 1)
                        else:
                            act.wait_ge(mm_done, r * 4 + (U0[name] + v + 1))
                        act.wait_ge(freed, r * 4 + (U0[name] + v - 1))
                        fn(sig[:, v % 2, :], bank[(U0[name] + v) % RING][:, :], ACT.Sigmoid).then_inc(ple_sig, 1)
                        closing(name, f"post_ple{i}", v, r)

                if U0[name] + 8 == UNITS:
                    four(0)
                    four(1)
                else:
                    with act.Fori(0, 2) as r:
                        four(r)
                root(f"post_ple{i}")

            mlp(0)
            ple(0)
            next_operand("mix1", "pre_mix", 1, True)

            act.dma_start(pos_i[:, :], ins["positions"].partition_broadcast(P)).then_inc(pos_in, 16)
            for i in range(2):
                act.wait_ge(trig_arg, i + 1)
                fn((sin, cos)[i][:, :], (sin, cos)[i][:, :], ACT.Sin).then_inc(trig, 1)
            for i in range(7):
                tick("mlain", i)
            for k in range(5):
                act.wait_ge(freed, U0["mlain"] + k + 1)
                if k >= 2:
                    act.wait_ge(sq_used, Q0["cqkv"] + k - 1)
                fn(sq[:, k % 2, :], acc[:, k, :], ACT.Square).then_inc(sq_ready, 1)
            root("cqkv", 3, 384, o=std, b=6)
            root("cqkv", 2, 256, o=sig[:, 0, :], b=7, first=3)
            rounds("cqkv", 5, lambda k: cq_hi[:, k, :] if k < 3 else ckv_hi[:, k - 3, :], lambda k: acc[:, k, :])
            rounds("kr", 1, lambda k: kr_hi[:, :], lambda k: sig[:, 1, :])
            act.wait_ge(ckt_mm, 1)
            for c in range(2):
                act.wait_ge(ckt_mm, c + 1)
                fn(ckt_hi[:, :, c * P:(c + 1) * P], bank[4 + c][:, :].rearrange("p (k n) -> p k n", n=P),
                   ACT.Copy).then_inc(hi_ready, 1)

            def head_pair(j, n):
                hp = j + 4 * n
                phase = f"heads{n}"

                def cut_bank(dst, b):
                    fn(dst, bank[b][:, :], ACT.Copy).then_inc(hi_ready, 1)

                act.wait_ge(q_mm, hp * 3 + 1)
                cut_bank(qn_hi[:, 0, :], 0)
                act.wait_ge(val_ready, j + (V0[f"pairs{n}"] + 1))
                fn(qr_hi[:, :], sig[:, 0, :], ACT.Copy).then_inc(hi_ready, 1)
                act.wait_ge(q_mm, hp * 3 + 3)
                cut_bank(qn_hi[:, 1, :], 3)
                for e in range(2):
                    act.wait_ge(mm_done, j * 4 + (U0[phase] + e + 1))
                    for c in range(2):
                        cut_bank(ql_hi[:, 2 * e + c, :], 2 * e + c)
                for e in range(2):
                    tick(phase, e, j, 4)

                def exp(i):
                    s = i % 2
                    act.wait_ge(mx_ready, hp * 8 + (i + 1))
                    if i >= 2:
                        act.wait_ge(pt_mm, hp * 8 + (i - 1))
                    fn(probs[:, s, :], bank[4 + s][:, :], ACT.Exp, bias=small[:, 4 * s + 1:4 * s + 2], scale=MLA_SCALE,
                       accum_out=small[:, 4 * s + 2:4 * s + 3]).then_inc(exp_done, 1)

                def pt(i):
                    qb = i % 4
                    act.wait_ge(pt_mm, hp * 8 + (i + 1))
                    if i == 4:
                        act.wait_ge(pv_mm, hp * 2 + 1)
                    fn(pt_hi[:, :, qb * P:(qb + 1) * P], bank[6 + i % 2][:, :].rearrange("p (k n) -> p k n", n=P),
                       ACT.Copy).then_inc(hi_ready, 1)

                def ol(e):
                    act.wait_ge(pv_mm, hp * 2 + (e + 1))
                    if e:
                        act.wait_ge(mm_done, j * 4 + (U0[phase] + 3))
                    for c in range(2):
                        cut_bank(ol_hi[:, c, :], c)

                def o(e):
                    act.wait_ge(mm_done, j * 4 + (U0[phase] + 3 + e))
                    cut_bank(blk(x_hi, j * 2 + e), 2 + e)

                for t in range(10):
                    if t < 8:
                        exp(t)
                    if t == 6:
                        ol(0)
                    if t >= 2:
                        pt(t - 2)
                    if t == 7:
                        o(0)
                        tick(phase, 2, j, 4)
                ol(1)
                o(1)
                tick(phase, 3, j, 4)

            for n in range(2):
                with act.Fori(0, 4) as j:
                    head_pair(j, n)
                if n == 0:
                    ticks("wo0", 8)
                else:
                    closing_ticks("wo1", "post_mix1")
            mlp(1)
            ple(1)

        @block.vector
        def _(dve):
            v = nc.vector
            chain = Steps(dve, step)

            def did(ins):
                chain.did(ins)
                chain.wait()

            def lo(dst, value, hi, name, k):
                dve.wait_ge(hi_ready, k + (K0[name] + 1))
                v.tensor_tensor(dst, value, hi.bitcast(F32), ALU.subtract).then_inc(lo_ready, 1)

            def bank_of(name, i):
                if name in ("mlp0", "mlp1", "mlain"):
                    return bank[i % 8][:, :]
                return bank[(U0[name] + i) % RING][:, :]

            def multiplied(name, i, r=0, per=0):
                dve.wait_ge(mm_done, r * per + (U0[name] + i + 1))

            def recip(name, o, i=None):
                dve.wait_ge(std_ready, STD0[name] + 1)
                did(v.reciprocal(o, std[:, :]))

            def centre(src, dst, nth):
                dve.wait_ge(sum_done, nth + 1)
                did(v.tensor_scalar(mean[:, :], bank[6][:, :], 1.0 / D, None, ALU.mult))
                with dve.Fori(0, NB) as k:
                    v.tensor_tensor(blk(dst, k), blk(src, k), mean[:, :], ALU.subtract).then_inc(centred, 1)

            def add_square(norm, r, i, per=4):
                k = r * per + i
                dve.wait_ge(sq_ready, k + (Q0[norm] + 1))
                dve.wait_ge(sq_used, k + Q0[norm])
                if isinstance(k, int) and k == 0:
                    v.tensor_copy(std[:, :], sq[:, 0, :]).then_inc(sq_used, 1)
                else:
                    v.tensor_tensor(std[:, :], std[:, :], sq[:, i % 2, :], ALU.add).then_inc(sq_used, 1)

            dve.wait_ge(consts_in, 32)
            v.memset(ones[:, :], 1.0).then_inc(consts_set, 1)
            v.memset(zpad[:, 0:TAPS - 1], 0.0).then_inc(hc_ready, 1)
            v.memset(qpad[:, 0:2], 0.0)
            v.memset(consts[:, 0:1], LN_EPS)
            did(v.memset(consts[:, 1:2], RMS_EPS))
            def spread_c(buf, value):
                return buf[:, 0:2, :].rearrange("p a (b n) -> p (a b) n", n=P), \
                    value.rearrange("p (k n) -> p k n", n=1).to_broadcast([P, NB, P])

            def cut_c():
                hi, value = spread_c(x_hi, small[:, :])
                rest, _ = spread_c(x_lo, small[:, :])
                did(v.tensor_copy(hi, value))
                v.tensor_tensor(rest, value, hi.bitcast(F32), ALU.subtract).then_inc(c_ready, 1)

            dve.wait_ge(act_done, 1)
            did(v.tensor_tensor(small[:, :], prm[:, COL["c"]:COL["c"] + NB], sig[:, 0, 0:NB], ALU.mult))
            cut_c()
            lg = [prm[:, COL["hg_lb"] + 8 * i:COL["hg_lb"] + 8 * i + 8] for i in range(3)]
            did(v.tensor_tensor(lbt[:, 24:32], lg[0], lg[1], ALU.max))
            did(v.tensor_tensor(lbt[:, 24:32], lbt[:, 24:32], lg[2], ALU.max))
            for i in range(3):
                last = v.tensor_tensor(lbt[:, 8 * i:8 * i + 8], lg[i], lbt[:, 24:32], ALU.subtract)
            last.then_inc(lb_in, 1)
            dve.wait_ge(lb_exp, 1)
            did(v.tensor_tensor(lbt[:, 24:32], lbt[:, 0:8], lbt[:, 8:16], ALU.add))
            did(v.tensor_tensor(lbt[:, 24:32], lbt[:, 24:32], lbt[:, 16:24], ALU.add))
            did(v.reciprocal(lbt[:, 32:40], lbt[:, 24:32]))
            did(v.tensor_tensor(lbt[:, 24:32], lbt[:, 0:8], lbt[:, 32:40], ALU.mult))
            did(v.tensor_scalar(lbt[:, 32:40], lbt[:, 24:32], -1.0, 1.0, ALU.mult, ALU.add))

            centre(hres, acc, 0)

            def columns_of(name, unit_, b, first):
                multiplied(name, unit_)
                for j in range(NB):
                    v.scalar_tensor_tensor(diag[:, j % 2, 0:P], cut(bank[b + j // 4], j % 4), 1.0, ident[:, :],
                                           ALU.mult, ALU.mult, accum_out=mod[:, first + j:first + j + 1]
                                           ).then_inc(step, 1)
                    chain.n += 1
                    chain.wait()
                part = mod[:, first:first + NB]
                did(v.tensor_tensor(part, part, prm[:, COL["b_ada"] + first:COL["b_ada"] + first + NB], ALU.add))
                dve.sem_inc(freed, 8)

            diag = sq
            recip("ln_in", rstd_pre[:, :])
            with chain.loop(NB, 1) as k:
                chain.did(v.tensor_tensor(blk(acc, k), blk(acc, k), rstd_pre[:, :], ALU.mult))
            columns_of("ada", 7, 0, 0)
            columns_of("ada", 15, 2, 8)
            did(v.tensor_scalar(mod[:, 8:16], mod[:, 8:16], 1.0, None, ALU.add))
            with dve.Fori(0, 4) as r:
                for s in range(2):
                    j = r * 2 + s
                    v.tensor_scalar(blk(acc, j), blk(acc, j), mod[:, bass.ds(j + 8, 1)], mod[:, bass.ds(j, 1)],
                                    ALU.mult, ALU.add).then_inc(val_ready, 1)
                for s in range(2):
                    lo(blk(x_lo, r * 2 + s), blk(acc, r * 2 + s), blk(x_hi, r * 2 + s), "u", r * 2 + s)

            def taps(j, first, last):
                for t in range(first, last):
                    z, w = zpad[:, t:t + T], prm_col("cf_w", j * TAPS + t)
                    h = blk(hres, j)
                    if t == 0:
                        did(v.tensor_scalar(h, z, w, prm_col("cf_b", j), ALU.mult, ALU.add))
                    elif t < TAPS - 1:
                        did(v.scalar_tensor_tensor(h, z, w, h, ALU.mult, ALU.add))
                    else:
                        v.scalar_tensor_tensor(h, z, w, h, ALU.mult, ALU.add).then_inc(hc_ready, 1)

            def biased(o, j, i, by):
                return v.scalar_tensor_tensor(o, bank_of("proj", i), prm_col("b_in", j + 8 * BRANCH_UNITS[i]), by,
                                              ALU.add, ALU.mult)

            with chain.loop(NB, 34) as j:
                dve.wait_ge(hc_ready, j + 1)
                multiplied("proj", 1, j, 8)
                dve.wait_ge(act_done, j * 5 + 2)
                biased(zpad[:, TAPS - 1:], j, 1, sig[:, 0, :]).then_inc(freed, 2)
                dve.wait_ge(freed, j * 8 + (U0["proj"] + 2))
                taps(j, 0, 10)
                multiplied("proj", 3, j, 8)
                dve.wait_ge(act_done, j * 5 + 3)
                biased(qpad[:, 2:], j, 3, mean[:, :]).then_inc(freed, 2)
                dve.wait_ge(freed, j * 8 + (U0["proj"] + 4))
                conv = rstd_post[:, :]
                did(v.tensor_scalar(conv, qpad[:, 0:T], prm_col("sc_w", j * 3), prm_col("sc_b", j), ALU.mult, ALU.add))
                for t in (1, 2):
                    did(v.scalar_tensor_tensor(conv, qpad[:, t:t + T], prm_col("sc_w", j * 3 + t), conv,
                                               ALU.mult, ALU.add))
                taps(j, 10, 18)
                dve.wait_ge(act_done, j * 5 + 4)
                biased(tmp[:, 0, :], j, 4, sig[:, 1, :]).then_inc(freed, 1)
                multiplied("proj", 5, j, 8)
                dve.wait_ge(freed, j * 8 + (U0["proj"] + 5))
                biased(tmp[:, 1, :], j, 5, tmp[:, 0, :]).then_inc(freed, 1)
                dve.wait_ge(freed, j * 8 + (U0["proj"] + 6))
                v.tensor_tensor(sq[:, 0, :], tmp[:, 1, :], conv, ALU.mult).then_inc(val_ready, 1)
                taps(j, 18, 25)
                dve.wait_ge(act_done, j * 5 + 5)
                biased(blk(acc, j), j, 6, std[:, :]).then_inc(freed, 1)
                dve.wait_ge(freed, j * 8 + (U0["proj"] + 7))
                did(v.tensor_scalar(blk(acc, j), blk(acc, j), prm_col("pool_scale", j), None, ALU.mult))
                dve.wait_ge(act_done, j * 5 + 6)
                biased(blk(gate_c, j), j, 7, rstd_pre[:, :]).then_inc(freed, 1)
                taps(j, 25, TAPS)
                lo(blk(yb_lo, j), sq[:, 0, :], blk(yb_hi, j), "yb", j)

            ping = tmp[:, :, :].rearrange("p a n -> p (a n)")
            pong = sq[:, :, :].rearrange("p a n -> p (a n)")
            for half in range(2):
                for k in range(4):
                    j = 4 * half + k
                    g = j // 2
                    w = POOLS[g]
                    front = w - 2
                    if j == 0:
                        dve.wait_ge(hc_ready, NB + 1)
                    multiplied("avp", 5 * half + k)
                    v.tensor_scalar(zpad[:, TAPS - 1:], bank_of("avp", 5 * half + k), prm_col("b_in", j), None,
                                    ALU.add).then_inc(freed, 1)
                    dve.wait_ge(freed, U0["avp"] + 5 * half + k + 1)
                    z0 = TAPS - 1
                    did(v.tensor_tensor(ping[:, 0:T + front], zpad[:, z0 - front:z0 + T],
                                        zpad[:, z0 - front - 1:z0 + T - 1], ALU.add))
                    src, dst, width, at = ping, pong, 2, front
                    while width < w:
                        rest = at - width
                        did(v.tensor_tensor(dst[:, 0:T + rest], src[:, width:width + T + rest], src[:, 0:T + rest],
                                            ALU.add))
                        src, dst, width, at = dst, src, 2 * width, rest
                    vals = sig[:, k % 2, :]
                    z = zpad[:, z0:z0 + T]
                    did(v.scalar_tensor_tensor(vals, src[:, 0:T], 1.0 / w, z, ALU.mult, ALU.subtract))
                    ic = COL["inv_count"] + 16 * g
                    did(v.tensor_tensor(vals[:, 0:w], src[:, 0:w], prm[:, ic:ic + w], ALU.mult))
                    v.tensor_tensor(vals[:, 0:w], vals[:, 0:w], z[:, 0:w], ALU.subtract).then_inc(val_ready, 1)
                    lo(ya_lo[:, j, :], vals, ya_hi[:, j, :], "ya", 8 * half + k)
                for k in range(4):
                    g, m = 2 * half + k // 2, k % 2
                    j = 4 * half + k
                    if k == 0:
                        dve.wait_ge(pool_mm, half + 1)
                    if k == 2:
                        multiplied("avp", 5 * half + 4)
                    vals = sig[:, k % 2, :]
                    v.tensor_tensor(vals, bank[4 + 2 * (g % 2) + m][:, :], acc[:, j, :], ALU.mult
                                    ).then_inc(val_ready, 1)
                    dve.wait_ge(hi_ready, K0["ya"] + 8 * half + 4 + k + 1)
                    v.tensor_tensor(ya_lo[:, j, :], vals, ya_hi[:, j, :].bitcast(F32), ALU.subtract
                                    ).then_inc(lo_ready, 1)
                dve.wait_ge(lo_ready, K0["ya"] + 8 * half + 8)
                dve.sem_inc(freed, 1)
            centre(hres, hres, 1)
            did(v.memset(std[:, :], 0.0))
            with dve.Fori(0, 4) as r:
                for i in range(2):
                    add_square("ln_c", r, i, 2)

            def merge(i):
                name = f"merge{i}"
                dve.wait_ge(freed, U0[name])
                with chain.loop(4, {1: 0, 0: 6, 2: 0}[i]) as r:
                    if i == 0:
                        for s in range(2):
                            v.tensor_tensor(blk(hres, r * 2 + s), blk(hres, r * 2 + s), rstd_post[:, :], ALU.mult
                                            ).then_inc(ln_ready, 1)
                        for s in range(2):
                            j = r * 2 + s
                            t = tmp[:, s, :]
                            dve.wait_ge(ln_ready, r * 2 + (s + 1))
                            did(v.tensor_scalar(t, blk(hres, j), prm_col("cf_ln_g", j), prm_col("cf_ln_b", j),
                                                ALU.mult, ALU.add))
                            dve.wait_ge(act_done, r * 4 + (A0[name] + s + 1))
                            did(v.tensor_tensor(t, t, (mean, std)[s][:, :], ALU.mult))
                            v.tensor_tensor(t, t, blk(gate_c, j), ALU.mult).then_inc(val_ready, 1)
                    for s in range(2):
                        j = r * 2 + s
                        multiplied(name, 2 * s + 1, r, 4)
                        product = (bank_of(name, 2 * s + 1), sig[:, s, :], ALU.mult)
                        if i == 0:
                            dve.wait_ge(act_done, r * 4 + (A0[name] + 2 + s + 1))
                        else:
                            dve.wait_ge(act_done, r * 2 + (A0[name] + s + 1))
                        if i == 1:
                            v.tensor_tensor(blk(acc, j), *product).then_inc(freed, 2)
                        if i == 0:
                            did(v.tensor_tensor(sig[:, s, :], *product))
                            v.tensor_tensor(blk(acc, j), blk(acc, j), sig[:, s, :], ALU.add).then_inc(freed, 2)
                            lo(blk(yb_lo, j), tmp[:, s, :], blk(yb_hi, j), "yc", j)
                        if i == 2:
                            v.tensor_tensor(sig[:, s, :], *product).then_inc(freed, 2)
                            dve.wait_ge(freed, r * 4 + (U0[name] + 2 * s + 2))
                            v.tensor_tensor(blk(acc, j), blk(acc, j), sig[:, s, :], ALU.add).then_inc(val_ready, 1)
                            lo(blk(ya_lo, j), blk(acc, j), blk(ya_hi, j), "m", j)

            merge(1)
            recip("ln_c", rstd_post[:, :])
            merge(0)
            merge(2)
            multiplied("merge2", 15)
            cut_c()
            columns_of("adag", 7, 0, 16)
            dve.wait_ge(x_in, 32)
            with chain.loop(2, 0) as r:
                for i in range(4):
                    j = r * 4 + i
                    multiplied("wout", i, r, 4)
                    t = (tmp, sig)[i // 2][:, i % 2, :]
                    v.tensor_scalar(t, bank_of("wout", i), mod[:, bass.ds(j + 16, 1)], None, ALU.mult
                                    ).then_inc(freed, 1)
                    dve.wait_ge(freed, r * 4 + (U0["wout"] + i + 1))
                    v.scalar_tensor_tensor(blk(hres, j), blk(hres, j), ALPHA, t, ALU.mult, ALU.add
                                           ).then_inc(r_ready, 1)
            centre(hres, hres, 2)
            recip("ln_out", rstd_post[:, :])
            with dve.Fori(0, 4) as r:
                for s in range(2):
                    j = r * 2 + s
                    v.scalar_tensor_tensor(tmp[:, s, :], blk(hres, j), prm_col("ln_g", j), rstd_post[:, :],
                                           ALU.mult, ALU.mult).then_inc(ln_ready, 1)
                for s in range(2):
                    j = r * 2 + s
                    dve.wait_ge(hi_ready, r * 2 + (K0["mix0"] + s + 1))
                    v.scalar_tensor_tensor(blk(x_lo, j), blk(hres, j), prm_col("pre_mix", j), blk(x_hi, j).bitcast(F32),
                                           ALU.mult, ALU.subtract).then_inc(lo_ready, 1)
            recip("mix0", rstd_pre[:, :])

            v.memset(attn[:, 0, :], 0.0).then_inc(o_read, 1)
            did(v.memset(attn[:, 1, :], 0.0))
            dve.wait_ge(gla_in, 32)

            def head(h):
                b = [bank_of("hg", i) for i in range(4)]
                multiplied("hg", 0, h, 4)
                v.scalar_tensor_tensor(hq[:, :], b[0], float(P) ** -0.5, rstd_pre[:, :], ALU.mult, ALU.mult
                                       ).then_inc(freed, 1)
                for d in range(2):
                    multiplied("hg", 1 + d, h, 4)
                    v.tensor_tensor(hf[:, d, :], b[1 + d], rstd_pre[:, :], ALU.mult).then_inc(freed, 1)
                multiplied("hg", 3, h, 4)
                v.tensor_tensor(hvT[:, :], b[3], rstd_pre[:, :], ALU.mult).then_inc(freed, 1)
                at = lambda first: lbt[:, bass.ds(h + first, 1)] if not isinstance(h, int) else lbt[:, first + h:first + h + 1]
                for d in range(2):
                    dve.wait_ge(gla_act, h * 10 + (d + 1))
                    v.tensor_scalar(hf[:, d, :], hf[:, d, :], at(32), at(24), ALU.mult, ALU.add).then_inc(gla_dve, 1)
                    dve.wait_ge(gla_dve, h * 6 + (d + 1))
                    chain.did(v.tensor_scalar(hk[:, d, :], hf[:, d, :], -1.0, 1.0, ALU.mult, ALU.add))
                for d in range(2):
                    way = (slice(None), d, slice(None, None, -1) if d else slice(None))
                    dve.wait_ge(gla_act, h * 10 + (2 + d + 1))
                    v.tensor_tensor_scan(hG[way], reset[:, :], hg[way], 0.0, ALU.mult, ALU.add).then_inc(gla_dve, 1)
                for d in range(2):
                    dve.wait_ge(gla_dve, h * 6 + (2 + d + 1))
                    G = hG[:, d, :].rearrange("p (c t) -> p c t", t=CH)
                    end = G[:, :, 0:1] if d else G[:, :, CH - 1:CH]
                    v.tensor_tensor(hg[:, d, :].rearrange("p (c t) -> p c t", t=CH), end.to_broadcast([P, NCH, CH]), G,
                                    ALU.subtract).then_inc(gla_dve, 1)
                for d in range(2):
                    dve.wait_ge(gla_act, h * 10 + (4 + 3 * d + 2))
                    chain.did(v.tensor_tensor(hf[:, d, :], hq[:, :], hE[:, d, :], ALU.mult))
                    chain.wait()
                    v.tensor_tensor(hI[:, d, :], hk[:, d, :], hI[:, d, :], ALU.mult).then_inc(decayed, 1)
                    dve.wait_ge(gla_act, h * 10 + (4 + 3 * d + 3))
                    v.tensor_tensor(hg[:, d, :], hk[:, d, :], hg[:, d, :], ALU.mult).then_inc(kend_ready, 1)

            def scans(c):
                for d in range(2):
                    dve.wait_ge(attn_mm, c * 2 - 1 + d)
                    v.memset(small[:, d:d + 1], 0.0)
                    v.copy_predicated(attn[:, d, :], mask[:, d, :], bank[7 - d][:, :]).then_inc(masked, 1)
                for d in range(2):
                    dve.wait_ge(kv_mm, c * 2 - 1 + d)
                    kv = lambda n: bank[4 + 2 * d + n % 2][:, n // 2 * P:(n // 2 + 1) * P]
                    order = list(range(NCH)) if d == 0 else list(range(NCH - 1, -1, -1))
                    for i in range(NCH - 1):
                        n, to = order[i], order[i + 1]
                        if i == 0:
                            ins_ = v.tensor_copy(state[:, d, to, :], kv(n))
                        else:
                            e = n * CH if d else n * CH + CH - 1
                            ins_ = v.scalar_tensor_tensor(state[:, d, to, :], state[:, d, n, :], hE[:, d, e:e + 1],
                                                          kv(n), ALU.mult, ALU.add)
                        if i == NCH - 2:
                            ins_.then_inc(states_done, 1)
                        else:
                            did(ins_)
                dve.wait_ge(o_mm, c)
                v.tensor_copy(blk(acc, c - 1), bank[4][:, :]).then_inc(o_read, 1)

            GLA_HEAD, GLA_SCAN = 4, 12
            head(0)
            with chain.loop(HEADS - 1, GLA_HEAD + GLA_SCAN) as r:
                h = r + 1
                scans(h)
                head(h)
            scans(HEADS)
            for h in range(HEADS):
                dve.wait_ge(o_rstd, h + 1)
                v.scalar_tensor_tensor(acc[:, h, :], acc[:, h, :], prm_col("o_norm", h), sig[:, h % 2, :],
                                       ALU.mult, ALU.mult).then_inc(o_normed, 1)
            dve.wait_ge(o_normed, HEADS)
            with chain.loop(2, 4) as r:
                for i in range(4):
                    t = tmp[:, i % 2, :]
                    dve.wait_ge(lo_ready, r * 4 + (K0["o"] + i))
                    multiplied("hggate", i, r, 4)
                    v.tensor_tensor(t, bank_of("hggate", i), rstd_pre[:, :], ALU.mult).then_inc(freed, 1)
                    dve.wait_ge(gate_sig, r * 4 + (i + 1))
                    did(v.tensor_tensor(t, t, sig[:, i % 2, :], ALU.mult))
                    v.tensor_tensor(t, t, blk(acc, r * 4 + i), ALU.mult).then_inc(val_ready, 1)
                    lo(blk(y_lo, r * 4 + i), t, blk(y_hi, r * 4 + i), "o", r * 4 + i)

            did(v.memset(std[:, :], 0.0))
            with dve.Fori(0, 2) as r:
                for i in range(4):
                    multiplied("hgout", i, r, 4)
                    v.tensor_copy(blk(acc, r * 4 + i), bank_of("hgout", i)).then_inc(freed, 1)
                    add_square("post_mix0", r, i)

            hblocks = {"mlp0": 1, "ple0": 2, "mix1": 3, "mlp1": 4, "ple1": 5, "end": 6}

            def residual(norm, gain, layer, name, next_gain, next_layer):
                recip(norm, rstd_post[:, :])
                if name != "end":
                    dve.wait_ge(lo_ready, K0[name])

                def two(r):
                    dve.wait_ge(h_ready, r * 2 + 8 * hblocks[name])
                    for s in range(2):
                        j = r * 2 + s
                        did(v.scalar_tensor_tensor(tmp[:, s, :], blk(acc, j), prm_col(gain, j + 8 * layer),
                                                   rstd_post[:, :], ALU.mult, ALU.mult))
                        v.tensor_tensor(blk(hres, j), blk(hres, j), tmp[:, s, :], ALU.add).then_inc(h_ready, 1)
                    for s in range(2):
                        j = r * 2 + s
                        if name == "end":
                            continue
                        dve.wait_ge(hi_ready, j + (K0[name] + 1))
                        if next_gain:
                            v.scalar_tensor_tensor(blk(x_lo, j), blk(hres, j), prm_col(next_gain, j + 8 * next_layer),
                                                   blk(x_hi, j).bitcast(F32), ALU.mult, ALU.subtract
                                                   ).then_inc(lo_ready, 1)
                        else:
                            v.tensor_tensor(blk(x_lo, j), blk(hres, j), blk(x_hi, j).bitcast(F32), ALU.subtract
                                            ).then_inc(lo_ready, 1)
                    if name in TOTALS:
                        for s in range(2):
                            add_square(name, r, s, 2)

                two(0)
                with chain.loop(3, 2) as r:
                    two(r + 1)

            def mlp(i):
                name = f"mlp{i}"
                residual(f"post_mix{i}", "post_mix", i, name, "pre_mlp", i)
                recip(name, rstd_pre[:, :])

                def quarter(q):
                    last = q == 3 if isinstance(q, int) else False
                    for u in range(8):
                        s = u % 2
                        dve.wait_ge(lo_ready, q * 8 + (K0[f"f{i}"] + u))
                        multiplied(name, u, q, 16)
                        v.scalar_tensor_tensor(tmp[:, s, :], bank_of(name, u), 0.0, rstd_pre[:, :], ALU.max, ALU.mult
                                               ).then_inc(freed, 1)
                        lo(y_lo[:, u, :], tmp[:, s, :], y_hi[:, u, :], f"f{i}", q * 8 + u)
                    if last:
                        dve.wait_ge(p_arrived, 16 * (i + 1))
                        for k in range(2):
                            lo(p_lo[:, k, :], p_in[:, k, :], p_hi[:, k, :], f"p{i}", k)
                    for u in range(8):
                        multiplied(name, 8 + u, q, 16)
                        if isinstance(q, int) and q == 0:
                            v.tensor_copy(acc[:, u, :], bank_of(name, 8 + u)).then_inc(freed, 1)
                            continue
                        v.tensor_tensor(acc[:, u, :], acc[:, u, :], bank_of(name, 8 + u), ALU.add).then_inc(freed, 1)
                        if last:
                            add_square(f"post_mlp{i}", 0, u)

                quarter(0)
                with dve.Fori(1, 3) as q:
                    quarter(q)
                quarter(3)

            def ple(i, nxt):
                for e in range(2):
                    multiplied(f"plee{i}", e)
                    for o in range(4):
                        last = v.tensor_copy(e_buf[:, 4 * e + o, :], bank[4 + o][:, :])
                    last.then_inc(freed, 1)
                residual(f"post_mlp{i}", "post_mlp", i, f"ple{i}", None, 0)
                name = f"pleg{i}"
                did(v.memset(std[:, :], 0.0))
                with dve.Fori(0, 2) as r:
                    for u in range(4):
                        j = r * 4 + u
                        dve.wait_ge(ple_sig, j + (8 * i + 1))
                        v.tensor_tensor(blk(acc, j), sig[:, u % 2, :], blk(e_buf, j), ALU.mult).then_inc(freed, 1)
                        add_square(f"post_ple{i}", r, u)
                residual(f"post_ple{i}", "ple_norm", i, nxt, "pre_mix", 1)

            mlp(0)
            ple(0, "mix1")
            recip("mix1", rstd_pre[:, :])

            dve.wait_ge(pos_in, 16)
            ang, n_turns = tmp[:, 0, :], tmp[:, 1, :]
            did(v.tensor_copy(ang, pos_i[:, :]))
            did(v.tensor_scalar(ang, ang, prm_col("inv_freq"), None, ALU.mult))
            for i, shift in enumerate((0.0, TWO_PI / 4)):
                o = (sin, cos)[i][:, :]
                did(v.tensor_scalar(n_turns, ang, 1.0 / TWO_PI, shift / TWO_PI, ALU.mult, ALU.add))
                did(v.tensor_scalar(n_turns, n_turns, ROUNDER, None, ALU.add))
                did(v.tensor_scalar(n_turns, n_turns, -ROUNDER, None, ALU.add))
                did(v.scalar_tensor_tensor(o, n_turns, -TWO_PI_PARTS[0], ang, ALU.mult, ALU.add))
                for part in TWO_PI_PARTS[1:]:
                    did(v.scalar_tensor_tensor(o, n_turns, -part, o, ALU.mult, ALU.add))
                did(v.tensor_scalar(o, o, shift, None, ALU.add))
                v.tensor_scalar(o, o, PI_LO, -PI_LO, ALU.min, ALU.max).then_inc(trig_arg, 1)
            for i in range(7):
                multiplied("mlain", i)
                v.tensor_tensor(acc[:, i, :], bank_of("mlain", i), rstd_pre[:, :], ALU.mult).then_inc(freed, 1)
            dve.wait_ge(std_ready, STD0["cqkv"] + 1)
            v.reciprocal(tmp[:, 0, :], std[:, :])
            dve.wait_ge(std_ready, STD0["cqkv"] + 2)
            did(v.reciprocal(tmp[:, 1, :], sig[:, 0, :]))
            for k in range(5):
                gain = prm_col("q_norm", k) if k < 3 else prm_col("kv_norm", k - 3)
                v.scalar_tensor_tensor(acc[:, k, :], acc[:, k, :], gain, tmp[:, 0 if k < 3 else 1, :],
                                       ALU.mult, ALU.mult).then_inc(val_ready, 1)
            for k in range(5):
                hi, lo_ = (cq_hi[:, k, :], cq_lo[:, k, :]) if k < 3 else (ckv_hi[:, k - 3, :], ckv_lo[:, k - 3, :])
                lo(lo_, acc[:, k, :], hi, "cqkv", k)
            dve.wait_ge(trig, 2)
            did(v.tensor_scalar(sin[:, :], sin[:, :], prm_col("rope_sign"), None, ALU.mult))
            did(v.tensor_tensor(tmp[:, 0, :], acc[:, 5, :], cos[:, :], ALU.mult))
            did(v.tensor_tensor(tmp[:, 1, :], acc[:, 6, :], sin[:, :], ALU.mult))
            v.tensor_tensor(sig[:, 1, :], tmp[:, 0, :], tmp[:, 1, :], ALU.add).then_inc(val_ready, 1)
            lo(kr_lo[:, :], sig[:, 1, :], kr_hi[:, :], "kr", 0)
            for c in range(2):
                dve.wait_ge(hi_ready, K0["ckt"] + c + 1)
                part = slice(c * P, (c + 1) * P)
                v.tensor_tensor(ckt_lo[:, :, part], bank[4 + c][:, :].rearrange("p (k n) -> p k n", n=P),
                                ckt_hi[:, :, part].bitcast(F32), ALU.subtract).then_inc(lo_ready, 1)

            def head_pair(j, n):
                hp = j + 4 * n
                name = f"pairs{n}"
                at = iter(range(PAIR))

                def rest(dst, b, hi):
                    dve.wait_ge(hi_ready, j * PAIR + (K0[name] + next(at) + 1))
                    ins_ = v.tensor_tensor(dst, b, hi.bitcast(F32), ALU.subtract)
                    ins_.then_inc(lo_ready, 1)

                rest(qn_lo[:, 0, :], bank[0][:, :], qn_hi[:, 0, :])
                dve.wait_ge(q_mm, hp * 3 + 2)
                chain.did(v.tensor_tensor(tmp[:, 0, :], bank[1][:, :], cos[:, :], ALU.mult))
                did(v.tensor_tensor(tmp[:, 1, :], bank[2][:, :], sin[:, :], ALU.mult))
                v.tensor_tensor(sig[:, 0, :], tmp[:, 0, :], tmp[:, 1, :], ALU.add).then_inc(val_ready, 1)
                rest(qr_lo[:, :], sig[:, 0, :], qr_hi[:, :])
                rest(qn_lo[:, 1, :], bank[3][:, :], qn_hi[:, 1, :])
                for e in range(2):
                    for c in range(2):
                        rest(ql_lo[:, 2 * e + c, :], bank[2 * e + c][:, :], ql_hi[:, 2 * e + c, :])

                def top(i):
                    s = i % 2
                    dve.wait_ge(sc_mm, hp * 8 + (i + 1))
                    did(v.tensor_reduce(small[:, 4 * s:4 * s + 1], bank[4 + s][:, :], AX_X, ALU.max))
                    v.tensor_scalar(small[:, 4 * s + 1:4 * s + 2], small[:, 4 * s:4 * s + 1], -MLA_SCALE, None,
                                    ALU.mult).then_inc(mx_ready, 1)

                def normed(i):
                    s = i % 2
                    dve.wait_ge(exp_done, hp * 8 + (i + 1))
                    did(v.reciprocal(small[:, 4 * s + 3:4 * s + 4], small[:, 4 * s + 2:4 * s + 3]))
                    v.tensor_scalar(probs[:, s, :], probs[:, s, :], small[:, 4 * s + 3:4 * s + 4], None,
                                    ALU.mult).then_inc(p_ready, 1)

                def pt(i):
                    part = slice(i % 4 * P, (i % 4 + 1) * P)
                    rest(pt_lo[:, :, part], bank[6 + i % 2][:, :].rearrange("p (k n) -> p k n", n=P),
                         pt_hi[:, :, part])

                def ol():
                    for c in range(2):
                        rest(ol_lo[:, c, :], bank[c][:, :], ol_hi[:, c, :])

                for t in range(10):
                    if t < 8:
                        top(t)
                    if 1 <= t < 9:
                        normed(t - 1)
                    if t == 6:
                        ol()
                    if t >= 2:
                        pt(t - 2)
                    if t == 7:
                        rest(blk(x_lo, j * 2), bank[2][:, :], blk(x_hi, j * 2))
                ol()
                rest(blk(x_lo, j * 2 + 1), bank[3][:, :], blk(x_hi, j * 2 + 1))

            for n in range(2):
                with chain.loop(4, 18) as j:
                    head_pair(j, n)
                dve.wait_ge(lo_ready, K0[f"pairs{n}"] + 4 * PAIR)
                dve.sem_inc(freed, 16)
                if n == 0:
                    with dve.Fori(0, 2) as r:
                        for i in range(4):
                            multiplied("wo0", i, r, 4)
                            v.tensor_copy(blk(acc, r * 4 + i), bank_of("wo0", i)).then_inc(freed, 1)
                else:
                    did(v.memset(std[:, :], 0.0))
                    with dve.Fori(0, 2) as r:
                        for i in range(4):
                            multiplied("wo1", i, r, 4)
                            v.tensor_tensor(blk(acc, r * 4 + i), blk(acc, r * 4 + i), bank_of("wo1", i), ALU.add
                                            ).then_inc(freed, 1)
                            add_square("post_mix1", r, i)
            mlp(1)
            ple(1, "end")


def blocks(w):
    k, n = w.shape
    return w.reshape(k // P, P, n // P, P).transpose(2, 1, 0, 3)


def as_units(w):
    b = blocks(w)
    return b.reshape(b.shape[0], P, UNIT)


def weight_stream(a):
    w_in = as_units(a["w_in"][0]).reshape(12, NB, P, UNIT)
    ada = a["w_ada"][0].reshape(NB, P, 3, D).transpose(2, 0, 1, 3).reshape(24, P, UNIT)
    parts = [ada[:16], np.stack([w_in[p] for p in BRANCH_UNITS], 1).reshape(64, P, UNIT)]
    pool = blocks(a["pool_w"][0].reshape(4 * 256, 256))
    pool = pool.reshape(2, P, 4, 2, P).transpose(2, 1, 3, 0, 4)
    for half in range(2):
        parts += [w_in[0][4 * half:4 * half + 4],
                  pool[2 * half:2 * half + 2].transpose(1, 0, 2, 3, 4).reshape(1, P, UNIT)]
    for i in (1, 0, 2):
        parts.append(np.stack([w_in[9 + i], as_units(a["w_branch"][0, i])], 1).reshape(16, P, UNIT))
    parts += [ada[16:], as_units(a["w_out"][0])]
    hg = as_units(a["hg_w_in_2"][0]).reshape(5, NB, P, UNIT)
    parts += [np.stack([hg[p] for p in range(4)], 1).reshape(32, P, UNIT), hg[4], as_units(a["hg_w_out_2"][0])]

    def mlp(i):
        w1 = as_units(a["w_mlp_in_2"][i]).reshape(4, 8, P, UNIT)
        w2 = np.stack([as_units(a["w_mlp_out_2"][i][q * D:(q + 1) * D]) for q in range(4)])
        e = blocks(a["w_ple_proj_2"][i]).reshape(2, 4, P, 2, P).transpose(0, 2, 1, 3, 4).reshape(2, P, UNIT)
        return [np.stack([w1, w2], 1).reshape(64, P, UNIT), e, as_units(a["w_ple_gate_2"][i])]

    parts += mlp(0)
    w = a["mla_w_in_2"][0]
    kr = w[:, 640:704]
    ks = np.concatenate([kr[:, 32:], kr[:, :32]], 1)
    parts.append(as_units(np.concatenate([w[:, :640], kr, kr, ks, ks], 1)))
    uq = a["mla_w_uq_2"][0].reshape(384, MH, 192)
    ukv = a["mla_w_ukv_2"][0].reshape(256, MH, 256)
    swap = np.concatenate([uq[:, :, 160:192], uq[:, :, 128:160]], 2)
    pad = np.zeros((P, 3, P), np.float32)
    wo = a["mla_w_o_2"][0]
    for half in range(2):
        for j in range(4):
            h = 8 * half + 2 * j
            cols = [blocks(uq[:, h + e, :128])[0] for e in range(2)]
            cols += [blocks(x.reshape(384, P))[0] for x in (uq[:, h:h + 2, 128:], swap[:, h:h + 2])]
            for e in range(2):
                uk = ukv[:, h + e, :128].T
                cols[e] = np.concatenate([cols[e], uk.reshape(P, 2, P), pad], 1)
                cols[2 + e] = np.concatenate([cols[2 + e], blocks(ukv[:, h + e, 128:])[0], pad], 1)
            parts.append(np.stack(cols).reshape(4, P, UNIT))
        parts.append(as_units(wo[half * D:(half + 1) * D]))
    parts += mlp(1)
    return np.ascontiguousarray(np.concatenate(parts))


def columns(v):
    return v.reshape(-1, P).T


def lay_out(a):
    f = {n: a[n + "_2"] for n in ("hg_lb", "o_norm") if n + "_2" in a}
    t = np.arange(16)
    inv = (1.0 / (np.float32(10000.0) ** (np.arange(0, 64, 2, dtype=np.float32) / np.float32(64)))).astype(np.float32)
    by_name = {
        "b_ada": columns(a["b_ada"]), "b_in": columns(a["b_in"]), "pool_scale": columns(a["pool_scale"]),
        "sc_w": a["sc_w"][0].reshape(3, NB, P).transpose(2, 1, 0).reshape(P, -1), "sc_b": columns(a["sc_b"]),
        "cf_w": a["cf_w"][0].reshape(TAPS, NB, P).transpose(2, 1, 0).reshape(P, -1), "cf_b": columns(a["cf_b"]),
        "cf_ln_g": columns(a["cf_ln_g"]), "cf_ln_b": columns(a["cf_ln_b"]), "ln_g": columns(a["ln_g"]),
        "ln_b": columns(a["ln_b"]), "pre_mix": columns(a["pre_mix_norm_2"]), "post_mix": columns(a["post_mix_norm_2"]),
        "pre_mlp": columns(a["pre_mlp_norm_2"]), "post_mlp": columns(a["post_mlp_norm_2"]),
        "ple_norm": columns(a["ple_norm_2"]), "hg_lb": columns(a["hg_lb_logits_2"]),
        "o_norm": columns(a["hg_o_norm_2"]), "q_norm": columns(a["mla_q_norm_2"]), "kv_norm": columns(a["mla_kv_norm_2"]),
        "inv_freq": np.tile(inv, 4)[:, None], "rope_sign": np.tile(np.repeat([-1.0, 1.0], 32), 2)[:, None],
        "c": columns(a["c"]),
        "inv_count": np.tile(np.concatenate([1.0 / np.minimum(t + 1, w) for w in POOLS]), (P, 1)),
    }
    params = np.concatenate([by_name[n].astype(np.float32) for n, _ in PARAMS], 1)
    assert params.shape == (P, NCOL)

    def turned(x):
        return np.ascontiguousarray(x.T.reshape(-1, P, T).transpose(1, 0, 2))

    tok = np.arange(P)
    same = tok[:, None] // CH == tok[None, :] // CH
    fwd = same & (tok[:, None] <= tok[None, :])
    bwd = same & (tok[:, None] >= tok[None, :])
    mask = np.stack([np.tile(fwd, (1, 4)), np.tile(bwd, (1, 4))], 1).astype(np.int32)
    return {
        "weights": weight_stream(a), "x": turned(a["x"][0]), "params": np.ascontiguousarray(params),
        "ident": np.eye(P, dtype=np.float32), "mask": mask,
        "reset": np.tile((np.arange(T) % CH != 0).astype(np.float32), (P, 1)),
        "p0": turned(a["p_2"][0, 0]), "p1": turned(a["p_2"][1, 0]), "positions": a["positions_2"].reshape(T),
    }


def kernel(**inputs):
    import concourse.bacc as _bacc
    from concourse.bass_utils import run_bass_kernel_spmd as _run

    arrays = lay_out({n: np.asarray(v) for n, v in inputs.items()})
    nc = _bacc.Bacc("TRN2", target_bir_lowering=False, num_devices=1, dynamic_dma_scratch_size=1024)
    ins = {n: nc.dram_tensor(f"{n}_dram", v.shape, mybir.dt.from_np(v.dtype), kind="ExternalInput").ap()
           for n, v in arrays.items()}
    out = nc.dram_tensor("out", (NB, P, T), F32, kind="ExternalOutput").ap()
    build(nc, ins, out)
    r = _run(nc, [{f"{n}_dram": v for n, v in arrays.items()}], core_ids=[0])
    return r.results[0]["out"].reshape(D, T).T.reshape(1, T, D)
```

```python
from contextlib import ExitStack

import numpy as np

import concourse.bass as bass
from concourse import mybir

F32 = mybir.dt.float32
F32R = mybir.dt.float32r
I32 = mybir.dt.int32
ALU = mybir.AluOpType
ACT = mybir.ActivationFunctionType
AX_X = mybir.AxisListType.X

P = 128
T = 512
D = 1024
NB = D // P
RING = 4
UNIT = 8 * P
TAPS = 31
POOLS = (2, 4, 8, 16)
ALPHA = 2.0 ** 0.25
LN_EPS = 1e-5
RMS_EPS = 1e-6
CH = 64
NCH = T // CH
HEADS = 8
MH = 16
MLA_SCALE = float(128 + 64) ** -0.5
TWO_PI = 6.283185307179586
PI_LO = 3.1415925

PARAMS = (("b_ada", 24), ("b_in", 96), ("pool_scale", 8), ("sc_w", 24), ("sc_b", 8), ("cf_w", 8 * TAPS),
          ("cf_b", 8), ("cf_ln_g", 8), ("cf_ln_b", 8), ("ln_g", 8), ("ln_b", 8), ("pre_mix", 16),
          ("post_mix", 16), ("pre_mlp", 16), ("post_mlp", 16), ("ple_norm", 16), ("hg_lb", 24),
          ("o_norm", 8), ("q_norm", 3), ("kv_norm", 2), ("inv_freq", 1), ("rope_sign", 1), ("c", 8), ("inv_count", 64))
COL = {}
_at = 0
for _name, _n in PARAMS:
    COL[_name] = _at
    _at += _n
NCOL = _at

BRANCH_UNITS = (7, 6, 3, 4, 5, 2, 1, 8)
BRANCH_ACT = {0: (7, ACT.Sigmoid), 2: (3, ACT.Identity), 4: (5, ACT.Sigmoid), 6: (1, ACT.Sigmoid), 7: (8, ACT.Sigmoid)}

STREAM = (("ada", 16), ("proj", 64), ("avp", 10), ("merge1", 16), ("merge0", 16), ("merge2", 16), ("adag", 8),
          ("wout", 8), ("hg", 32), ("hggate", 8), ("hgout", 8), ("mlp0", 64), ("plee0", 2), ("pleg0", 8),
          ("mlain", 7), ("heads0", 16), ("wo0", 8), ("heads1", 16), ("wo1", 8), ("mlp1", 64),
          ("plee1", 2), ("pleg1", 8))
U0 = {}
_at = 0
for _name, _n in STREAM:
    U0[_name] = _at
    _at += _n
UNITS = _at

PAIR = 17
AHEAD = ("qn0", "qn1", "qr", "K0", "K1")
CUTS = ("P0", "Va", "P1", "Vb", "P2", "qn0n", "P3", "K0n", "o0", "P4", "P5", "P6", "qn1n", "qrn", "P7", "K1n", "o1")
CUTS_LAST = tuple(c for c in CUTS if not c.endswith("n"))
SPLITS = (("u", 8, 1), ("yb", 8, 1), ("ya", 16, 1), ("yc", 8, 1), ("m", 8, 1), ("mix0", 8, 0), ("o", 8, 1),
          ("mlp0", 8, 0), ("f0", 32, 0), ("p0", 2, 0), ("ple0", 8, 0), ("mix1", 8, 0), ("cqkv", 5, 1),
          ("kr", 1, 1), ("pairs0", 4 * PAIR, 0.5), ("pairs1", 4 * PAIR, 0.5), ("mlp1", 8, 0), ("f1", 32, 0),
          ("p1", 2, 0), ("ple1", 8, 0))
K0, V0 = {}, {}
_at = _val = 0
for _name, _n, _has in SPLITS:
    K0[_name], V0[_name] = _at, _val
    _at += _n
    _val += {1: _n, 0: 0, 0.5: 4}[_has]

NORMS = (("ln_in", 8), ("ln_c", 8), ("ln_out", 8), ("mix0", 8), ("o", 8), ("post_mix0", 8), ("mlp0", 8),
         ("post_mlp0", 8), ("post_ple0", 8), ("mix1", 8), ("cqkv", 5), ("post_mix1", 8), ("mlp1", 8),
         ("post_mlp1", 8), ("post_ple1", 8))
Q0 = {}
_at = 0
for _name, _n in NORMS:
    Q0[_name] = _at
    _at += _n


A0 = {"proj": 1, "merge1": 1 + 5 * NB, "merge0": 1 + 6 * NB, "merge2": 1 + 8 * NB}
TOTALS = ("ln_in", "ln_c", "mix0", "post_mix0", "mlp0", "post_mlp0", "post_ple0", "mix1", "post_mix1", "mlp1",
          "post_mlp1", "post_ple1")
STD0 = {n: i for i, n in enumerate(("ln_in", "ln_c", "ln_out", "mix0", "post_mix0", "mlp0", "post_mlp0", "post_ple0",
                                    "mix1", "cqkv", "cqkv_second", "post_mix1", "mlp1", "post_mlp1", "post_ple1"))}
ROUNDER = 12582912.0
TWO_PI_PARTS = (6.28125, 0.0019350051879882812, 3.0199159819567e-07)


class Steps:

    def __init__(self, eng, sem):
        self.eng, self.sem, self.base, self.n = eng, sem, 0, 0

    def did(self, ins):
        ins.then_inc(self.sem, 1)
        self.n += 1

    def wait(self):
        self.eng.wait_ge(self.sem, self.base + self.n)

    def loop(self, rounds, per):
        return _Loop(self, rounds, per)


class _Loop:
    def __init__(self, steps, rounds, per):
        self.steps, self.rounds, self.per = steps, rounds, per

    def __enter__(self):
        k = self.steps
        self.before = k.base + k.n
        self.fori = k.eng.Fori(0, self.rounds)
        r = self.fori.__enter__()
        k.base, k.n = r * self.per + self.before, 0
        return r

    def __exit__(self, *exc):
        k = self.steps
        assert exc[0] or k.n == self.per, f"the loop signals {k.n} times a round, not {self.per}"
        k.base, k.n = self.before + self.rounds * self.per, 0
        return self.fori.__exit__(*exc)


def blk(buf, j):
    if isinstance(j, int):
        return buf[:, j, :]
    return buf[:, bass.ds(j, 1), :].rearrange("p a n -> p (a n)")


def cut(t, i):
    return t[:, i * P:(i + 1) * P]


def build(nc, ins, out):
    ctx = ExitStack()
    with ctx:
        def sb(name, shape, dt=F32, stack=ctx):
            return stack.enter_context(nc.sbuf_tensor(name, shape, dt))

        def sem(name):
            return ctx.enter_context(nc.semaphore(name))

        stage = sb("stage", [P, RING, UNIT])
        w_hi = sb("w_hi", [P, RING, UNIT], F32R)
        w_lo = sb("w_lo", [P, RING, UNIT], F32R)
        x_hi = sb("x_hi", [P, NB, T], F32R)
        x_lo = sb("x_lo", [P, NB, T], F32R)
        hres = sb("hres", [P, NB, T])
        acc = sb("acc", [P, NB, T])
        prm = sb("prm", [P, NCOL])
        ones = sb("ones", [P, P])
        ident = sb("ident", [P, P])
        mod = sb("mod", [P, 24])
        mean = sb("mean", [P, T])
        std = sb("std", [P, T])
        rstd_pre = sb("rstd_pre", [P, T])
        rstd_post = sb("rstd_post", [P, T])
        sq = sb("sq", [P, 2, T])
        tmp = sb("tmp", [P, 2, T])
        sig = sb("sig", [P, 2, T])
        consts = sb("consts", [P, 2])
        lbt = sb("lbt", [P, 40])
        small = sb("small", [P, 8])
        with ExitStack() as own:
            ya_hi = sb("ya_hi", [P, NB, T], F32R, own)
            ya_lo = sb("ya_lo", [P, NB, T], F32R, own)
            yb_hi = sb("yb_hi", [P, NB, T], F32R, own)
            yb_lo = sb("yb_lo", [P, NB, T], F32R, own)
            gate_c = sb("gate_c", [P, NB, T], F32, own)
            zpad = sb("zpad", [P, TAPS - 1 + T], F32, own)
            qpad = sb("qpad", [P, 2 + T], F32, own)
        with ExitStack() as own:
            y_hi = sb("y_hi", [P, NB, T], F32R, own)
            y_lo = sb("y_lo", [P, NB, T], F32R, own)
            with ExitStack() as own2:
                p_in = sb("p_in", [P, 2, T], F32, own2)
                p_hi = sb("p_hi", [P, 2, T], F32R, own2)
                p_lo = sb("p_lo", [P, 2, T], F32R, own2)
                e_buf = sb("e_buf", [P, NB, T], F32, own2)
            with ExitStack() as own2:
                hq = sb("hq", [P, T], F32, own2)
                hvT = sb("hvT", [P, T], F32, own2)
                hf = sb("hf", [P, 2, T], F32, own2)
                hk = sb("hk", [P, 2, T], F32, own2)
                hg = sb("hg", [P, 2, T], F32, own2)
                hG = sb("hG", [P, 2, T], F32, own2)
                hE = sb("hE", [P, 2, T], F32, own2)
                hI = sb("hI", [P, 2, T], F32, own2)
                v_tok = sb("v_tok", [P, T], F32, own2)
                k_tok = sb("k_tok", [P, 2, T], F32, own2)
                attn = sb("attn", [P, 2, T], F32, own2)
                state = sb("state", [P, 2, NCH, P], F32, own2)
                mask = sb("mask", [P, 2, T], I32, own2)
                reset = sb("reset", [P, T], F32, own2)
        with ExitStack() as own:
            ckv_hi = sb("ckv_hi", [P, 2, T], F32R, own)
            ckv_lo = sb("ckv_lo", [P, 2, T], F32R, own)
            K_hi = sb("K_hi", [P, 2, T], F32R, own)
            K_lo = sb("K_lo", [P, 2, T], F32R, own)
            V_hi = sb("V_hi", [P, 4, 2 * P], F32R, own)
            V_lo = sb("V_lo", [P, 4, 2 * P], F32R, own)
            kr_hi = sb("kr_hi", [P, T], F32R, own)
            kr_lo = sb("kr_lo", [P, T], F32R, own)
            cq_hi = sb("cq_hi", [P, 3, T], F32R, own)
            cq_lo = sb("cq_lo", [P, 3, T], F32R, own)
            qn_hi = sb("qn_hi", [P, 2, T], F32R, own)
            qn_lo = sb("qn_lo", [P, 2, T], F32R, own)
            qr_hi = sb("qr_hi", [P, T], F32R, own)
            qr_lo = sb("qr_lo", [P, T], F32R, own)
            pt_hi = sb("pt_hi", [P, 4, T], F32R, own)
            pt_lo = sb("pt_lo", [P, 4, T], F32R, own)
            pos_i = sb("pos_i", [P, T], I32, own)
        o_scale = [hf[:, 0, :], hf[:, 1, :], hg[:, 0, :], hg[:, 1, :], hI[:, 0, :], hI[:, 1, :], v_tok[:, :], k_tok[:, 0, :]]
        gate_o = [hk[:, 0, :], hk[:, 1, :], hG[:, 0, :], hG[:, 1, :], hq[:, :], hvT[:, :], attn[:, 0, :], attn[:, 1, :]]
        gate_s = [sig[:, 0, :], sig[:, 1, :], mean[:, :], std[:, :]]
        o_bank = (6, 7, 5, 4)
        probs = sq
        cos, sin = mean, rstd_post

        bank = [ctx.enter_context(nc.psum_tensor(f"bank{i}", [P, T], F32)) for i in range(8)]

        loaded = [sem(f"unit_loaded{i}") for i in range(RING)]
        rounded = sem("unit_rounded")
        split = sem("unit_split")
        mm_done = sem("unit_multiplied")
        freed = sem("bank_freed")

        consts_in = sem("consts_in")
        x_in = sem("x_in")
        consts_set = sem("consts_set")
        out_sent = sem("out_sent")

        def c_rep(k):
            return gate_c[:, k // 4, k % 4 * P:(k % 4 + 1) * P]

        def prm_col(name, j=0):
            if isinstance(j, int):
                return prm[:, COL[name] + j:COL[name] + j + 1]
            return prm[:, bass.ds(j + COL[name], 1)]

        sq_ready = sem("square_ready")
        sq_used = sem("square_summed")
        totalled = sem("squares_totalled")
        std_ready = sem("std_ready")
        sum_done = sem("sum_done")
        centred = sem("centred")

        block = ctx.enter_context(nc.Block())

        c_ready = sem("c_ready")
        act_done = sem("branch_act_done")
        hc_ready = sem("conv_ready")
        pool_mm = sem("pool_multiplied")
        r_ready = sem("rows_summed")
        val_ready = sem("value_ready")
        hi_ready = sem("hi_ready")
        lo_ready = sem("lo_ready")
        h_ready = sem("h_ready")
        ln_ready = sem("ln_ready")
        step = sem("dve_step")
        lb_exp = sem("lb_exp")
        lb_in = sem("lb_in")

        gla_in = sem("gla_consts_in")
        gla_act = sem("gla_act")
        gla_dve = sem("gla_dve")
        decayed = sem("decayed")
        kend_ready = sem("kend_ready")
        masked = sem("masked")
        states_done = sem("states_done")
        attn_mm = sem("attn_mm")
        v_turned = sem("v_turned")
        k_turned = sem("k_turned")
        kv_mm = sem("kv_mm")
        o_mm = sem("o_mm")
        o_read = sem("o_read")
        tok_copied = sem("tok_copied")
        o_rstd = sem("o_rstd")
        o_normed = sem("o_normed")
        gate_sig = sem("gate_sig")
        gate_ready = sem("gate_ready")

        squared = sem("squared")
        p_arrived = sem("p_arrived")
        ple_sig = sem("ple_sig")

        pos_in = sem("pos_in")
        trig_arg = sem("trig_arg")
        trig = sem("trig")
        q_mm = sem("query_mm")
        sc_mm = sem("score_mm")
        mx_ready = sem("max_ready")
        exp_done = sem("exp_done")
        p_ready = sem("prob_ready")
        pt_mm = sem("prob_turned")
        pv_mm = sem("pv_mm")

        @block.sync
        def _(sp):
            units = ins["weights"]

            def load(s, src):
                sp.dma_start(stage[:, s, :], src).then_inc(loaded[s], 16)

            sp.dma_start(hres[:, :, :], ins["x"]).then_inc(x_in, 16)
            for s in range(RING):
                load(s, units[s])
            with sp.Fori(1, UNITS // RING) as r:
                for s in range(RING):
                    sp.wait_ge(split, r * RING + (s - RING + 1))
                    load(s, units[bass.ds(r * RING + s, 1)].rearrange("a p n -> p (a n)"))
            for u in range(UNITS // RING * RING, UNITS):
                sp.wait_ge(split, u - RING + 1)
                load(u % RING, units[u])
            for j in range(NB):
                sp.wait_ge(h_ready, 8 * 6 + j + 1)
                sp.dma_start(out[j], hres[:, j, :]).then_inc(out_sent, 16)
            sp.wait_ge(out_sent, 16 * NB)

        @block.gpsimd
        def _(pool):
            def lo(u, s):
                pool.wait_ge(rounded, u + 1)
                nc.gpsimd.tensor_tensor(w_lo[:, s, :], stage[:, s, :], w_hi[:, s, :].bitcast(F32),
                                        ALU.subtract).then_inc(split, 1)

            def passed(first, n):
                for u in range(first, first + n):
                    pool.wait_ge(rounded, u + 1)
                    pool.wait_ge(mm_done, u + 1)
                    pool.sem_inc(split, 1)

            def los(first, end):
                front, back = -(-first // RING), end // RING
                for u in range(first, front * RING):
                    lo(u, u % RING)
                with pool.Fori(front, back) as r:
                    for s in range(RING):
                        lo(r * RING + s, s)
                for u in range(back * RING, end):
                    lo(u, u % RING)

            passed(U0["ada"], 16)
            los(U0["proj"], U0["adag"])
            passed(U0["adag"], 8)
            los(U0["wout"], UNITS)

        @block.tensor
        def _(pe):
            def mm3(o, wh, wl, xh, xl, start, stop):
                nc.tensor.matmul(o, wh, xh, start=start, stop=False)
                nc.tensor.matmul(o, wh, xl, start=False, stop=False)
                return nc.tensor.matmul(o, wl, xh, start=False, stop=stop)

            def unit(u, s, xh, xl, ready=None, b=None):
                pe.wait_ge(split, u + 1)
                if b is None:
                    pe.wait_ge(freed, u - (RING - 1))
                else:
                    pe.wait_ge(freed, u - 7)
                for k in range(8):
                    if ready is not None:
                        pe.wait_ge(lo_ready, ready + (k + 1))
                    last = mm3(bank[s if b is None else b][:, :], cut(w_hi[:, s, :], k), cut(w_lo[:, s, :], k),
                               xh[:, k, :], xl[:, k, :], k == 0, k == 7)
                last.then_inc(mm_done, 1)

            def quad(u, s, xs, ready, wide=False):
                for k in range(8):
                    pe.wait_ge(lo_ready, ready + (k + 1))
                    for i in range(RING):
                        slot, (xh, xl) = (s + i) % RING, xs[i % len(xs)]
                        if k == 0:
                            pe.wait_ge(split, u + (i + 1))
                            pe.wait_ge(freed, u + (i - RING + 1))
                        last = mm3(bank[i if wide else slot][:, :], cut(w_hi[:, slot, :], k), cut(w_lo[:, slot, :], k),
                                   xh[:, k, :], xl[:, k, :], k == 0, k == 7)
                        if k == 7:
                            last.then_inc(mm_done, 1)

            def units(name, n, xs, ready, slow=False, then=lambda: None):
                if slow:
                    quad(U0[name], U0[name] % RING, xs, ready)
                else:
                    for i in range(RING):
                        unit(U0[name] + i, (U0[name] + i) % RING, *xs[i % len(xs)],
                             ready=ready if i == len(xs) - 1 else None)
                then()
                if n == 2 * RING:
                    for i in range(RING, n):
                        unit(U0[name] + i, (U0[name] + i) % RING, *xs[i % len(xs)])
                    return
                with pe.Fori(1, n // RING) as r:
                    for i in range(RING):
                        unit(r * RING + (U0[name] + i), (U0[name] + i) % RING, *xs[i % len(xs)])

            def sum_features(src, ready, base):
                for k in range(NB):
                    pe.wait_ge(ready, base(k))
                    last = nc.tensor.matmul(bank[6][:, :], ones[:, :], src[:, k, :], start=k == 0, stop=k == NB - 1)
                last.then_inc(sum_done, 1)

            def sum_squares(name, n=NB, b=7, first=0, size=None):
                for k in range(n):
                    pe.wait_ge(sq_ready, Q0[name] + first + k + 1)
                    nc.tensor.matmul(bank[b][:, :], ones[:, :], sq[:, (first + k) % 2, :],
                                     start=k == 0, stop=k == n - 1).then_inc(sq_used, 1)

            def sum_total(name, b=7):
                pe.wait_ge(sq_used, Q0[name] + NB)
                nc.tensor.matmul(bank[b][:, :], ones[:, :], std[:, :], start=True, stop=True).then_inc(totalled, 1)

            def operand(name, n):
                pe.wait_ge(lo_ready, K0[name] + n)

            def modulation(name, first, b, between=lambda: None):
                pe.wait_ge(c_ready, 1 if name == "ada" else 2)
                if name == "adag":
                    pe.wait_ge(freed, U0[name])
                for k in range(8):
                    if k == 2:
                        between()
                    u = U0[name] + first + k
                    s = u % RING
                    pe.wait_ge(rounded, u + 1)
                    for n in range(2):
                        last = nc.tensor.matmul(bank[b + n][:, :], c_rep(k), stage[:, s, n * T:(n + 1) * T],
                                                start=k == 0, stop=k == 7)
                    last.then_inc(mm_done, 1)

            pe.wait_ge(consts_set, 1)
            pe.wait_ge(x_in, 16)
            sum_features(hres, x_in, lambda k: 16)
            modulation("ada", 0, 0)
            modulation("ada", 8, 2, lambda: sum_total("ln_in"))
            units("proj", 64, [(x_hi, x_lo)], K0["u"], slow=True)
            a0 = U0["avp"]
            for i in range(NB):
                unit(a0 + i, (a0 + i) % RING, x_hi, x_lo)
            for g in range(4):
                half = g // 2
                s = (a0 + NB + half) % RING
                pe.wait_ge(split, a0 + NB + half + 1)
                operand("ya", 2 * g + 2)
                if half:
                    operand("ya", NB + 2 * (g - 2) + 2)
                for m in range(2):
                    o = bank[4 + 2 * (g % 2) + m][:, :]
                    for k in range(2):
                        i = 4 * (g % 2) + 2 * k + m
                        last = mm3(o, cut(w_hi[:, s, :], i), cut(w_lo[:, s, :], i),
                                   ya_hi[:, 2 * g + k, :], ya_lo[:, 2 * g + k, :], k == 0, k == 1)
                last.then_inc(mm_done if g % 2 else pool_mm, 1)
            operand("ya", 16)
            sum_features(hres, hc_ready, lambda k: k + 2)
            units("merge1", 16, [(x_hi, x_lo), (yb_hi, yb_lo)], K0["yb"], then=lambda: sum_total("ln_c"))
            units("merge0", 16, [(x_hi, x_lo), (ya_hi, ya_lo)], K0["ya"] + 8)
            units("merge2", 16, [(x_hi, x_lo), (yb_hi, yb_lo)], K0["yc"])
            modulation("adag", 0, 0)
            units("wout", 8, [(ya_hi, ya_lo)], K0["m"])
            pe.wait_ge(r_ready, NB + 1)
            nc.tensor.matmul(bank[6][:, :], ones[:, :], std[:, :], start=True, stop=True).then_inc(sum_done, 1)
            sum_squares("ln_out")

            def head_units(h, part):
                for i in part:
                    unit(h * 4 + (U0["hg"] + i), (U0["hg"] + i) % RING, x_hi, x_lo)

            def pairs(t, p):
                return t[:, p * P:(p + 1) * P]

            def gla_scores(c):
                pe.wait_ge(decayed, c * 2 - 1)
                for p in range(4):
                    last = nc.tensor.matmul(pairs(bank[7], p), pairs(hI[:, 0, :], p), pairs(hf[:, 0, :], p),
                                            start=True, stop=True)
                last.then_inc(attn_mm, 1)
                pe.wait_ge(freed, c * 4 + U0["hg"])
                pe.wait_ge(o_read, c)
                for p in range(4):
                    last = nc.tensor.transpose(pairs(bank[4], p), pairs(hvT[:, :], p), ident[:, :])
                last.then_inc(v_turned, 1)
                pe.wait_ge(kend_ready, c * 2 - 1)
                for p in range(4):
                    last = nc.tensor.transpose(pairs(bank[5], p), pairs(hg[:, 0, :], p), ident[:, :])
                last.then_inc(k_turned, 1)
                pe.wait_ge(decayed, c * 2)
                for p in range(4):
                    last = nc.tensor.matmul(pairs(bank[6], p), pairs(hI[:, 1, :], p), pairs(hf[:, 1, :], p),
                                            start=True, stop=True)
                last.then_inc(attn_mm, 1)
                pe.wait_ge(kend_ready, c * 2)
                pe.wait_ge(masked, c * 2 - 1)
                for p in range(4):
                    last = nc.tensor.transpose(pairs(bank[7], p), pairs(hg[:, 1, :], p), ident[:, :])
                last.then_inc(k_turned, 1)

                def chunk_kv(d, n):
                    half, p = 64 * (n % 2), n // 2
                    return nc.tensor.matmul(pairs(bank[4 + 2 * d + n % 2], n // 2),
                                            k_tok[half:half + CH, d, p * P:(p + 1) * P],
                                            v_tok[half:half + CH, p * P:(p + 1) * P], start=True, stop=True)

                pe.wait_ge(tok_copied, c * 3 - 1)
                for n in range(NCH - 1):
                    last = chunk_kv(0, n)
                last.then_inc(kv_mm, 1)
                pe.wait_ge(tok_copied, c * 3)
                pe.wait_ge(masked, c * 2)
                for n in range(NCH - 1, 0, -1):
                    last = chunk_kv(1, n)
                last.then_inc(kv_mm, 1)
            def gla_outputs(c):
                pe.wait_ge(states_done, c * 2 - 1)
                for d in range(2):
                    if d:
                        pe.wait_ge(states_done, c * 2)
                    for p in range(4):
                        nc.tensor.matmul(pairs(bank[4], p), pairs(v_tok[:, :], p), pairs(attn[:, d, :], p),
                                         start=d == 0 and p == 0, stop=False, skip_group_check=True)
                    for n in range(1 - d, NCH - d):
                        last = nc.tensor.matmul(bank[4][:, n * CH:(n + 1) * CH], state[:, d, n, :],
                                                hf[:, d, n * CH:(n + 1) * CH], start=False,
                                                stop=d == 1 and n == NCH - 2, skip_group_check=True)
                last.then_inc(o_mm, 1)

            quad(U0["hg"], U0["hg"] % RING, [(x_hi, x_lo)], K0["mix0"])
            sum_total("mix0")
            with pe.Fori(1, HEADS) as h:
                head_units(h, (0, 1))
                gla_scores(h)
                head_units(h, (2, 3))
                gla_outputs(h)
            for i in range(4):
                if i == 2:
                    gla_scores(HEADS)
                unit(U0["hggate"] + i, (U0["hggate"] + i) % RING, x_hi, x_lo)
            gla_outputs(HEADS)
            for i in range(4):
                for h in (2 * i, 2 * i + 1):
                    pe.wait_ge(sq_ready, Q0["o"] + h + 1)
                    if h == 3:
                        pe.wait_ge(o_read, HEADS + 1)
                    if h >= 4:
                        pe.wait_ge(gla_act, 10 * HEADS + h - 3)
                    nc.tensor.matmul(bank[o_bank[h % 4]][:, :], ones[:, :], sq[:, h % 2, :],
                                     start=True, stop=True).then_inc(sq_used, 1)
                unit(U0["hggate"] + 4 + i, (U0["hggate"] + i) % RING, x_hi, x_lo)
            units("hgout", 8, [(y_hi, y_lo)], K0["o"])

            def mlp(i):
                sum_total(f"post_mix{i}")
                name = f"mlp{i}"

                def quarter(q):
                    for v in range(8):
                        if v or not isinstance(q, int):
                            if not isinstance(q, int) or v >= 4:
                                if v == 7 and isinstance(q, int):
                                    pe.wait_ge(std_ready, STD0[name] + 1)
                                unit(q * 16 + (U0[name] + v), (U0[name] + v) % RING, x_hi, x_lo, b=v)
                        else:
                            quad(U0[name], U0[name] % RING, [(x_hi, x_lo)], K0[name], wide=True)
                            sum_total(name)
                    for v in range(8, 16):
                        unit(q * 16 + (U0[name] + v), (U0[name] + v) % RING, y_hi, y_lo,
                             ready=q * 8 + K0[f"f{i}"] if v == 8 else None, b=v - 8)

                quarter(0)
                with pe.Fori(1, 4) as q:
                    quarter(q)

            def ple(i):
                pe.wait_ge(freed, U0[f"plee{i}"])
                sum_total(f"post_mlp{i}", 3)
                operand(f"p{i}", 2)
                for e in range(2):
                    u = U0[f"plee{i}"] + e
                    pe.wait_ge(split, u + 1)
                    if e:
                        pe.wait_ge(freed, u)
                    for o in range(4):
                        for k in range(2):
                            w = 2 * o + k
                            last = mm3(bank[4 + o][:, :], cut(w_hi[:, u % RING, :], w), cut(w_lo[:, u % RING, :], w),
                                       p_hi[:, k, :], p_lo[:, k, :], k == 0, k == 1)
                    last.then_inc(mm_done, 1)
                units(f"pleg{i}", 8, [(x_hi, x_lo)], K0[f"ple{i}"], slow=True)
                sum_total(f"post_ple{i}")

            mlp(0)
            ple(0)

            quad(U0["mlain"], U0["mlain"] % RING, [(x_hi, x_lo)], K0["mix1"], wide=True)
            sum_total("mix1")
            unit(U0["mlain"] + 4, (U0["mlain"] + 4) % RING, x_hi, x_lo, b=4)
            pe.wait_ge(std_ready, STD0["mix1"] + 1)
            sum_squares("cqkv", 3, 7)
            unit(U0["mlain"] + 5, (U0["mlain"] + 5) % RING, x_hi, x_lo, b=5)
            pe.wait_ge(freed, U0["mlain"] + 1)
            sum_squares("cqkv", 2, 0, 3)
            unit(U0["mlain"] + 6, (U0["mlain"] + 6) % RING, x_hi, x_lo, b=6)

            def slot(n, i):
                return (U0[f"heads{n}"] + i) % RING

            def w(s, i):
                return cut(w_hi[:, s, :], i), cut(w_lo[:, s, :], i)

            def down(b, s, first):
                for k in range(3):
                    last = mm3(bank[b][:, :], *w(s, first + k), cq_hi[:, k, :], cq_lo[:, k, :], k == 0, k == 2)
                return last

            def keys(e, b, s):
                for c in range(2):
                    last = mm3(bank[b][:, :], *w(s, 2 * e + c), ckv_hi[:, c, :], ckv_lo[:, c, :], c == 0, c == 1)
                return last

            def values(half, s):
                for k in (2 * half, 2 * half + 1):
                    o = bank[half][:, k % 2 * 2 * P:(k % 2 + 1) * 2 * P]
                    for c in range(2):
                        part = slice(2 * c * P, 2 * (c + 1) * P)
                        last = mm3(o, ckv_hi[:, c, k * P:(k + 1) * P], ckv_lo[:, c, k * P:(k + 1) * P],
                                   w_hi[:, s, part], w_lo[:, s, part], c == 0, c == 1)
                return last

            def scores(hp, i):
                e, qb = i // 4, i % 4
                if not isinstance(hp, int) or hp * 8 + i >= 2:
                    pe.wait_ge(exp_done, hp * 8 + (i - 1))
                o = bank[4 + i % 2][:, :]
                q = slice(qb * P, (qb + 1) * P)
                mm3(o, qn_hi[:, e, q], qn_lo[:, e, q], K_hi[:, e, :], K_lo[:, e, :], True, False)
                r = slice(64 * e, 64 * e + 64)
                mm3(o, qr_hi[r, q], qr_lo[r, q], kr_hi[r, :], kr_lo[r, :], False, True).then_inc(sc_mm, 1)

            def first_queries(n):
                u = U0[f"heads{n}"]
                pe.wait_ge(split, u + 3)
                if n == 0:
                    operand("cqkv", 3)
                down(0, slot(n, 1), 0).then_inc(q_mm, 1)
                down(2, slot(n, 0), 0)
                down(3, slot(n, 0), 3).then_inc(mm_done, 1)
                down(1, slot(n, 1), 3).then_inc(mm_done, 1)
                if n == 0:
                    operand("cqkv", 5)
                keys(0, 4, slot(n, 2)).then_inc(q_mm, 1)
                keys(1, 5, slot(n, 2)).then_inc(mm_done, 1)
                pe.wait_ge(lo_ready, K0[f"pairs{n}"] + len(AHEAD))
                for i in range(2):
                    scores(4 * n, i)

            def head_pair(j, n, last_pair=False):
                hp = j + 4 * n
                cuts = j * PAIR + (K0[f"pairs{n}"] + len(AHEAD))
                order = CUTS_LAST if last_pair else CUTS
                nxt = not last_pair
                u = j * 4 + (U0[f"heads{n}"] + 3)
                at = {"C": 0, "B": 1, "A": 2, "D": 3}
                sl = {x: slot(n, 3 + i) for x, i in at.items()}

                def was_cut(name):
                    pe.wait_ge(lo_ready, cuts + (order.index(name) + 1))

                def weights(x):
                    pe.wait_ge(split, u + (at[x] + 1))

                def turn(i):
                    pe.wait_ge(p_ready, hp * 8 + (i + 1))
                    if i >= 2:
                        was_cut(f"P{i - 2}")
                    for k in range(4):
                        last = nc.tensor.transpose(pairs(bank[6 + i % 2], k), pairs(probs[:, i % 2, :], k), ident[:, :])
                    last.then_inc(pt_mm, 1)

                def weigh(e):
                    was_cut(f"P{4 * e + 3}")
                    for k in range(4):
                        last = mm3(bank[2 * e][:, :], V_hi[:, k, e * P:(e + 1) * P], V_lo[:, k, e * P:(e + 1) * P],
                                   pt_hi[:, k, :], pt_lo[:, k, :], k == 0, k == 3)
                    last.then_inc(pv_mm, 1)

                scores(hp, 2)
                turn(0)
                weights("C")
                pe.wait_ge(lo_ready, cuts - 1)
                values(0, sl["C"]).then_inc(q_mm, 1)
                scores(hp, 3)
                turn(1)
                values(1, sl["C"]).then_inc(mm_done, 1)
                scores(hp, 4)
                turn(2)
                if nxt:
                    weights("A")
                    down(2, sl["A"], 0).then_inc(q_mm, 1)
                scores(hp, 5)
                turn(3)
                if nxt:
                    weights("D")
                    keys(0, 3, sl["D"]).then_inc(q_mm, 1)
                scores(hp, 6)
                turn(4)
                scores(hp, 7)
                weigh(0)
                turn(5)
                if nxt:
                    was_cut("K0n")
                    weights("B")
                    down(2, sl["B"], 0)
                    down(3, sl["B"], 3).then_inc(mm_done, 1)
                turn(6)
                if nxt:
                    down(1, sl["A"], 3).then_inc(mm_done, 1)
                turn(7)
                if nxt:
                    was_cut("o0")
                    keys(1, 0, sl["D"]).then_inc(mm_done, 1)
                if nxt:
                    pe.wait_ge(val_ready, j + (V0[f"pairs{n}"] + 2))
                weigh(1)
                if nxt:
                    scores(hp + 1, 0)
                    scores(hp + 1, 1)

            for n in range(2):
                pe.wait_ge(freed, U0[f"heads{n}"])
                first_queries(n)
                with pe.Fori(0, 3) as j:
                    head_pair(j, n)
                head_pair(3, n, last_pair=True)
                operand(f"pairs{n}", 4 * PAIR)
                units(f"wo{n}", 8, [(x_hi, x_lo)], K0[f"pairs{n}"])
            mlp(1)
            ple(1)

        @block.scalar
        def _(act):
            def fn(o, i, f, **kw):
                return nc.scalar.activation(o, i, f, **kw)

            def tick(name, i, r=0, per=0):
                u = U0[name] + i
                if isinstance(r, int):
                    u, r = u + per * r, 0
                    if u + RING >= UNITS:
                        return
                act.wait_ge(mm_done, r * per + (u + 1))
                act.wait_ge(loaded[u % RING], r * (16 * per // RING) + 16 * (u // RING + 2))
                fn(w_hi[:, u % RING, :], stage[:, u % RING, :], ACT.Copy).then_inc(rounded, 1)

            def closing(phase, norm, i, r=0, first=0, tick_first=False):
                j = r * 4 + i
                if tick_first:
                    tick(phase, first + i, r, 4)
                act.wait_ge(freed, j + (U0[phase] + first + 1))
                act.wait_ge(sq_used, j + (Q0[norm] - 1))
                fn(sq[:, i % 2, :], blk(acc, j), ACT.Square).then_inc(sq_ready, 1)
                if not tick_first:
                    tick(phase, first + i, r, 4)

            def closing_ticks(phase, norm):
                with act.Fori(0, 2) as r:
                    for i in range(4):
                        closing(phase, norm, i, r)

            def ticks(name, n, group=RING, first=0):
                with act.Fori(first // group, (first + n) // group) as r:
                    for i in range(group):
                        tick(name, i, r, group)

            def root(name, n=NB, size=D, eps=RMS_EPS, o=std, b=7, first=0):
                if name in TOTALS:
                    act.wait_ge(totalled, TOTALS.index(name) + 1)
                else:
                    act.wait_ge(sq_used, Q0[name] + first + n)
                fn(o[:, :] if o is std else o, bank[b][:, :], ACT.Sqrt, bias=eps_col(eps),
                   scale=1.0 / size).then_inc(std_ready, 1)

            def eps_col(eps):
                return consts[:, 0:1] if eps == LN_EPS else consts[:, 1:2]

            def squares(name, src, ready, base, per=2, scale=1):
                def two(r):
                    for s in range(2):
                        act.wait_ge(ready, r * 2 * scale + (base + scale * (s + 1)))
                        if not isinstance(r, int) or Q0[name] + 2 * r + s >= 2:
                            act.wait_ge(sq_used, r * 2 + (Q0[name] + s - 1))
                        fn(sq[:, s, :], blk(src, r * 2 + s), ACT.Square).then_inc(sq_ready, 1)
                two(0)
                with act.Fori(1, 4) as r:
                    two(r)

            act.dma_start(prm[:, :], ins["params"]).then_inc(consts_in, 16)
            act.dma_start(ident[:, :], ins["ident"]).then_inc(consts_in, 16)
            act.wait_ge(consts_in, 32)
            fn(sig[:, 0, 0:8], prm[:, COL["c"]:COL["c"] + NB], ACT.Sigmoid).then_inc(act_done, 1)
            for s in range(RING):
                act.wait_ge(loaded[s], 16)
                fn(w_hi[:, s, :], stage[:, s, :], ACT.Copy).then_inc(rounded, 1)
            act.wait_ge(lb_in, 1)
            fn(lbt[:, 0:24], lbt[:, 0:24], ACT.Exp).then_inc(lb_exp, 1)
            for i in range(8):
                tick("ada", i)
                act.wait_ge(centred, i + 1)
                if i >= 2:
                    act.wait_ge(sq_used, i - 1)
                fn(sq[:, i % 2, :], acc[:, i, :], ACT.Square).then_inc(sq_ready, 1)
            for i in (8, 9):
                tick("ada", i)
            root("ln_in", eps=LN_EPS)
            for i in range(10, 16):
                tick("ada", i)
            with act.Fori(0, 4) as r:
                for s in range(2):
                    act.wait_ge(val_ready, r * 2 + (s + 1))
                    fn(blk(x_hi, r * 2 + s), blk(acc, r * 2 + s), ACT.Copy).then_inc(hi_ready, 1)

            def rounds(name, n, dst, src):
                for k in range(n):
                    act.wait_ge(val_ready, V0[name] + k + 1)
                    fn(dst(k), src(k), ACT.Copy).then_inc(hi_ready, 1)

            with act.Fori(0, NB) as j:
                for i in range(8):
                    act.wait_ge(mm_done, j * 8 + (U0["proj"] + i + 1))
                    if i in BRANCH_ACT:
                        part, func = BRANCH_ACT[i]
                        dst = {0: sig[:, 0, :], 2: mean[:, :], 4: sig[:, 1, :], 6: std[:, :], 7: rstd_pre[:, :]}[i]
                        fn(dst, bank[(U0["proj"] + i) % RING][:, :], func,
                           bias=prm_col("b_in", j + 8 * part)).then_inc(act_done, 1)
                    tick("proj", i, j, 8)
                act.wait_ge(val_ready, j + (V0["yb"] + 1))
                fn(blk(yb_hi, j), sq[:, 0, :], ACT.Copy).then_inc(hi_ready, 1)
            for j in range(NB):
                tick("avp", j)
                act.wait_ge(val_ready, V0["ya"] + j + 1)
                fn(ya_hi[:, j, :], sig[:, j % 2, :], ACT.Copy).then_inc(hi_ready, 1)
            for j in range(NB):
                act.wait_ge(val_ready, V0["ya"] + NB + j + 1)
                fn(ya_hi[:, j, :], sig[:, j % 2, :], ACT.Copy).then_inc(hi_ready, 1)
                if j % 4 == 3:
                    tick("avp", NB + j // 4)

            def merge(i):
                name = f"merge{i}"
                with act.Fori(0, 4) as r:
                    for s in range(2 if i == 0 else 0):
                        act.wait_ge(ln_ready, r * 2 + (s + 1))
                        fn((mean, std)[s][:, :], blk(hres, r * 2 + s), ACT.Sigmoid, scale=prm_col("cf_ln_g", r * 2 + s),
                           bias=prm_col("cf_ln_b", r * 2 + s)).then_inc(act_done, 1)
                    for s in range(4):
                        if s % 2 == 0:
                            act.wait_ge(mm_done, r * 4 + (U0[name] + s + 1))
                            fn(sig[:, s // 2, :], bank[(U0[name] + s) % RING][:, :], ACT.Sigmoid,
                               bias=prm_col("b_in", r * 2 + (72 + 8 * i + s // 2))).then_inc(act_done, 1)
                        tick(name, s, r, 4)
                        if i == 2 and s % 2:
                            act.wait_ge(val_ready, r * 2 + (V0["m"] + s // 2 + 1))
                            fn(blk(ya_hi, r * 2 + s // 2), blk(acc, r * 2 + s // 2), ACT.Copy).then_inc(hi_ready, 1)
                        if i == 0 and s % 2:
                            act.wait_ge(val_ready, r * 2 + (V0["yc"] + s // 2 + 1))
                            fn(blk(yb_hi, r * 2 + s // 2), tmp[:, s // 2, :], ACT.Copy).then_inc(hi_ready, 1)

            squares("ln_c", hres, centred, 8)
            merge(1)
            root("ln_c", eps=LN_EPS)
            merge(0)
            act.wait_ge(lo_ready, K0["yc"] + 8)
            act.dma_start(hres[:, :, :], ins["x"]).then_inc(x_in, 16)
            merge(2)
            ticks("adag", 8)
            ticks("wout", 8)
            squares("ln_out", hres, centred, 16)
            root("ln_out", eps=LN_EPS)
            with act.Fori(0, 4) as r:
                for s in range(2):
                    act.wait_ge(ln_ready, r * 2 + (8 + s + 1))
                    fn(blk(hres, r * 2 + s), tmp[:, s, :], ACT.Identity, bias=prm_col("ln_b", r * 2 + s)
                       ).then_inc(h_ready, 1)
                    act.wait_ge(h_ready, r * 2 + (s + 1))
                    act.wait_ge(sq_used, r * 2 + (Q0["mix0"] + s - 1))
                    fn(blk(x_hi, r * 2 + s), blk(hres, r * 2 + s), ACT.Copy,
                       scale=prm_col("pre_mix", r * 2 + s)).then_inc(hi_ready, 1)
                    fn(sq[:, s, :], blk(hres, r * 2 + s), ACT.Square).then_inc(sq_ready, 1)
            tick("hg", 0)
            root("mix0")
            for i in range(1, 4):
                tick("hg", i)

            act.dma_start(mask[:, :, :], ins["mask"]).then_inc(gla_in, 16)
            act.dma_start(reset[:, :], ins["reset"]).then_inc(gla_in, 16)

            def gates(h):
                for d in range(2):
                    act.wait_ge(freed, h * 4 + (U0["hg"] + d + 2))
                    fn(hf[:, d, :], hf[:, d, :], ACT.Sigmoid).then_inc(gla_act, 1)
                for d in range(2):
                    act.wait_ge(gla_dve, h * 6 + (d + 1))
                    fn(hg[:, d, :], hf[:, d, :], ACT.Ln).then_inc(gla_act, 1)
                for d in range(2):
                    act.wait_ge(gla_dve, h * 6 + (2 + d + 1))
                    fn(hE[:, d, :], hG[:, d, :], ACT.Exp).then_inc(gla_act, 1)
                    fn(hI[:, d, :], hG[:, d, :], ACT.Exp, scale=-1.0).then_inc(gla_act, 1)
                    act.wait_ge(gla_dve, h * 6 + (4 + d + 1))
                    fn(hg[:, d, :], hg[:, d, :], ACT.Exp).then_inc(gla_act, 1)

            def tokens(c):
                act.wait_ge(v_turned, c)
                fn(v_tok[:, :], bank[4][:, :], ACT.Copy).then_inc(tok_copied, 1)
                act.wait_ge(k_turned, c * 2 - 1)
                fn(k_tok[:, 0, :], bank[5][:, :], ACT.Copy).then_inc(tok_copied, 1)
                act.wait_ge(k_turned, c * 2)
                fn(k_tok[:, 1, :], bank[7][:, :], ACT.Copy).then_inc(tok_copied, 1)

            gates(0)
            with act.Fori(1, HEADS) as h:
                for i in range(4):
                    if i == 2:
                        tokens(h)
                    tick("hg", i, h, 4)
                gates(h)

            def gate_sigmoid(i):
                act.wait_ge(freed, U0["hggate"] + i + 1)
                if i >= 4:
                    act.wait_ge(gate_ready, i - 3)
                fn(gate_s[i % 4], gate_o[i], ACT.Sigmoid).then_inc(gate_sig, 1)

            def round_o(h):
                act.wait_ge(val_ready, V0["o"] + h + 1)
                fn(y_hi[:, h, :], acc[:, h, :], ACT.Copy).then_inc(hi_ready, 1)

            def square_o(h):
                act.wait_ge(o_read, h + 2)
                act.wait_ge(sq_used, Q0["o"] + h - 1)
                fn(sq[:, h % 2, :], acc[:, h, :], ACT.Square).then_inc(sq_ready, 1)

            for i in range(4):
                if i == 2:
                    tokens(HEADS)
                tick("hggate", i)
            for i in range(4):
                gate_sigmoid(i)
            square_o(0)
            square_o(1)
            for i in range(4):
                for h in (2 * i, 2 * i + 1):
                    act.wait_ge(sq_used, Q0["o"] + h + 1)
                    fn(o_scale[h], bank[o_bank[h % 4]][:, :], ACT.Ln, bias=consts[:, 1:2], scale=1.0 / P
                       ).then_inc(gla_act, 1)
                for h in (2 * i, 2 * i + 1):
                    act.wait_ge(gla_act, 10 * HEADS + h + 1)
                    fn(o_scale[h], o_scale[h], ACT.Exp, scale=-0.5).then_inc(o_rstd, 1)
                if i < 3:
                    square_o(2 * i + 2)
                    square_o(2 * i + 3)
                    tick("hggate", 4 + i)
                if i in (1, 2):
                    round_o(2 * i - 2)
                    round_o(2 * i - 1)
            for i in (4, 5, 6):
                gate_sigmoid(i)
            for h in (4, 5, 6):
                round_o(h)
            tick("hggate", 7)
            gate_sigmoid(7)
            round_o(7)
            closing_ticks("hgout", "post_mix0")

            hblocks = {"mlp0": 1, "ple0": 2, "mix1": 3, "mlp1": 4, "ple1": 5, "end": 6}

            def next_operand(name, gain, layer, normed, phase=None, beside=lambda: None):
                def two(r):
                    for s in range(2):
                        act.wait_ge(h_ready, r * 2 + (8 * hblocks[name] + s + 1))
                        if normed:
                            act.wait_ge(sq_used, r * 2 + (Q0[name] + s - 1))
                        kw = dict(scale=prm_col(gain, r * 2 + (8 * layer + s))) if gain else {}
                        fn(blk(x_hi, r * 2 + s), blk(hres, r * 2 + s), ACT.Copy, **kw).then_inc(hi_ready, 1)
                        if normed:
                            fn(sq[:, s, :], blk(hres, r * 2 + s), ACT.Square).then_inc(sq_ready, 1)

                two(0)
                beside()
                with act.Fori(1, 4) as r:
                    two(r)
                if normed:
                    tick(phase, 0)
                    root(name)
                    for i in range(1, 4):
                        tick(phase, i)

            def mlp(i):
                name = f"mlp{i}"
                act.dma_start(p_in[:, :, :], ins[f"p{i}"]).then_inc(p_arrived, 16)
                root(f"post_mix{i}")
                next_operand(name, "pre_mlp", i, True, name)
                def quarter(q):
                    for v in range(8):
                        s = v % 2
                        act.wait_ge(freed, q * 16 + (U0[name] + v + 1))
                        fn(tmp[:, s, :], tmp[:, s, :], ACT.Square).then_inc(squared, 1)
                        act.wait_ge(squared, q * 8 + (32 * i + v + 1))
                        fn(y_hi[:, v, :], tmp[:, s, :], ACT.Copy).then_inc(hi_ready, 1)
                        if v >= RING or not isinstance(q, int) or q:
                            tick(name, v, q, 16)
                    if not isinstance(q, int) or q == 0:
                        for v in range(8, 16):
                            tick(name, v, q, 16)

                quarter(0)
                with act.Fori(1, 3) as q:
                    quarter(q)
                quarter(3)
                act.wait_ge(p_arrived, 16 * (i + 1))
                for k in range(2):
                    fn(p_hi[:, k, :], p_in[:, k, :], ACT.Copy).then_inc(hi_ready, 1)
                for v in range(8):
                    closing(name, f"post_mlp{i}", v, first=56)

            def ple(i):
                root(f"post_mlp{i}", b=3)
                tick(f"plee{i}", 0)
                next_operand(f"ple{i}", None, 0, False, beside=lambda: tick(f"plee{i}", 1))
                name = f"pleg{i}"

                for v in range(8):
                    act.wait_ge(mm_done, U0[name] + v + 1)
                    act.wait_ge(freed, U0[name] + v - 1)
                    fn(sig[:, v % 2, :], bank[(U0[name] + v) % RING][:, :], ACT.Sigmoid).then_inc(ple_sig, 1)
                    closing(name, f"post_ple{i}", v, tick_first=v < RING)
                root(f"post_ple{i}")

            mlp(0)
            ple(0)
            next_operand("mix1", "pre_mix", 1, True, "mlain")

            act.dma_start(pos_i[:, :], ins["positions"].partition_broadcast(P)).then_inc(pos_in, 16)
            def latent_square(k):
                act.wait_ge(freed, U0["mlain"] + k + 1)
                act.wait_ge(sq_used, Q0["cqkv"] + k - 1)
                fn(sq[:, k % 2, :], acc[:, k, :], ACT.Square).then_inc(sq_ready, 1)

            latent_square(0)
            latent_square(1)
            tick("mlain", 4)
            latent_square(2)
            latent_square(3)
            root("cqkv", 3, 384, o=std, b=7)
            tick("mlain", 5)
            latent_square(4)
            root("cqkv", 2, 256, o=sig[:, 0, :], b=0, first=3)
            for i in range(2):
                act.wait_ge(trig_arg, i + 1)
                fn((sin, cos)[i][:, :], (sin, cos)[i][:, :], ACT.Sin).then_inc(trig, 1)

            def latent_round(k):
                act.wait_ge(val_ready, V0["cqkv"] + k + 1)
                fn(cq_hi[:, k, :] if k < 3 else ckv_hi[:, k - 3, :], acc[:, k, :], ACT.Copy).then_inc(hi_ready, 1)

            for k in range(3):
                latent_round(k)
            tick("mlain", 6)
            latent_round(3)
            latent_round(4)
            rounds("kr", 1, lambda k: kr_hi[:, :], lambda k: sig[:, 1, :])

            def cut_bank(dst, b):
                fn(dst, bank[b][:, :], ACT.Copy).then_inc(hi_ready, 1)

            def exp(hp, i):
                s = i % 2
                act.wait_ge(mx_ready, hp * 8 + (i + 1))
                if not isinstance(hp, int) or hp * 8 + i >= 2:
                    act.wait_ge(pt_mm, hp * 8 + (i - 1))
                fn(probs[:, s, :], bank[4 + s][:, :], ACT.Exp, bias=small[:, 4 * s + 1:4 * s + 2], scale=MLA_SCALE,
                   accum_out=small[:, 4 * s + 2:4 * s + 3]).then_inc(exp_done, 1)

            def cut_K(e, b):
                cut_bank(K_hi[:, e, :], b)

            def cut_qr(n, j):
                act.wait_ge(val_ready, j + (V0[f"pairs{n}"] + 1))
                fn(qr_hi[:, :], sig[:, 0, :], ACT.Copy).then_inc(hi_ready, 1)

            def first_queries(n):
                u = U0[f"heads{n}"]
                act.wait_ge(q_mm, 12 * n + 1)
                cut_bank(qn_hi[:, 0, :], 0)
                act.wait_ge(mm_done, u + 2)
                cut_bank(qn_hi[:, 1, :], 1)
                cut_qr(n, 0)
                act.wait_ge(q_mm, 12 * n + 2)
                cut_K(0, 4)
                act.wait_ge(mm_done, u + 3)
                cut_K(1, 5)
                for i in range(2):
                    exp(4 * n, i)
                    tick(f"heads{n}", i)
                tick(f"heads{n}", 2)

            def head_pair(j, n, last_pair=False):
                hp = j + 4 * n
                phase = f"heads{n}"
                nxt = not last_pair
                u = j * 4 + (U0[phase] + 3)
                at = {"C": 0, "B": 1, "A": 2, "D": 3}
                q = j * 3 + (12 * n + 2)

                def pt(i):
                    qb = i % 4
                    act.wait_ge(pt_mm, hp * 8 + (i + 1))
                    if i == 4:
                        act.wait_ge(pv_mm, hp * 2 + 1)
                    fn(pt_hi[:, :, qb * P:(qb + 1) * P], bank[6 + i % 2][:, :].rearrange("p (k n) -> p k n", n=P),
                       ACT.Copy).then_inc(hi_ready, 1)

                def o(e):
                    act.wait_ge(pv_mm, hp * 2 + (e + 1))
                    cut_bank(blk(x_hi, j * 2 + e), 2 * e)

                def multiplied(x):
                    act.wait_ge(mm_done, u + (at[x] + 1))

                def done(x):
                    tick(phase, 3 + at[x], j, 4)

                def cut_V(half):
                    fn(V_hi[:, 2 * half:2 * half + 2, :], bank[half][:, :].rearrange("p (k n) -> p k n", n=2 * P),
                       ACT.Copy).then_inc(hi_ready, 1)

                exp(hp, 2)
                pt(0)
                act.wait_ge(q_mm, q + 1)
                cut_V(0)
                exp(hp, 3)
                pt(1)
                multiplied("C")
                cut_V(1)
                exp(hp, 4)
                done("C")
                pt(2)
                if nxt:
                    act.wait_ge(q_mm, q + 2)
                    cut_bank(qn_hi[:, 0, :], 2)
                exp(hp, 5)
                pt(3)
                if nxt:
                    act.wait_ge(q_mm, q + 3)
                    cut_K(0, 3)
                exp(hp, 6)
                o(0)
                pt(4)
                exp(hp, 7)
                pt(5)
                pt(6)
                if nxt:
                    multiplied("A")
                    cut_bank(qn_hi[:, 1, :], 1)
                    cut_qr(n, j + 1)
                pt(7)
                if nxt:
                    multiplied("D")
                    cut_K(1, 0)
                    done("B")
                o(1)
                if nxt:
                    exp(hp + 1, 0)
                    done("A")
                    exp(hp + 1, 1)
                    done("D")

            for n in range(2):
                first_queries(n)
                with act.Fori(0, 3) as j:
                    head_pair(j, n)
                head_pair(3, n, last_pair=True)
                if n == 0:
                    ticks("wo0", 8)
                else:
                    closing_ticks("wo1", "post_mix1")
            mlp(1)
            ple(1)

        @block.vector
        def _(dve):
            v = nc.vector
            chain = Steps(dve, step)

            def did(ins):
                chain.did(ins)
                chain.wait()

            def lo(dst, value, hi, name, k):
                dve.wait_ge(hi_ready, k + (K0[name] + 1))
                v.tensor_tensor(dst, value, hi.bitcast(F32), ALU.subtract).then_inc(lo_ready, 1)

            def bank_of(name, i):
                if name in ("mlp0", "mlp1", "mlain"):
                    return bank[i % 8][:, :]
                return bank[(U0[name] + i) % RING][:, :]

            def multiplied(name, i, r=0, per=0):
                dve.wait_ge(mm_done, r * per + (U0[name] + i + 1))

            def recip(name, o, i=None):
                dve.wait_ge(std_ready, STD0[name] + 1)
                did(v.reciprocal(o, std[:, :]))

            def centre(src, dst, nth):
                dve.wait_ge(sum_done, nth + 1)
                did(v.tensor_scalar(mean[:, :], bank[6][:, :], 1.0 / D, None, ALU.mult))
                with dve.Fori(0, NB) as k:
                    v.tensor_tensor(blk(dst, k), blk(src, k), mean[:, :], ALU.subtract).then_inc(centred, 1)

            def add_square(norm, r, i, per=4):
                k = r * per + i
                dve.wait_ge(sq_ready, k + (Q0[norm] + 1))
                dve.wait_ge(sq_used, k + Q0[norm])
                if isinstance(k, int) and k == 0:
                    v.tensor_copy(std[:, :], sq[:, 0, :]).then_inc(sq_used, 1)
                else:
                    v.tensor_tensor(std[:, :], std[:, :], sq[:, i % 2, :], ALU.add).then_inc(sq_used, 1)

            v.memset(ones[:, :], 1.0).then_inc(consts_set, 1)
            v.memset(zpad[:, 0:TAPS - 1], 0.0).then_inc(hc_ready, 1)
            v.memset(qpad[:, 0:2], 0.0)
            v.memset(consts[:, 0:1], LN_EPS)
            did(v.memset(consts[:, 1:2], RMS_EPS))
            dve.wait_ge(consts_in, 32)
            def spread_c():
                v.tensor_copy(gate_c[:, 0:2, :].rearrange("p a (b n) -> p (a b) n", n=P),
                              small[:, :].rearrange("p (k n) -> p k n", n=1).to_broadcast([P, NB, P])
                              ).then_inc(c_ready, 1)

            dve.wait_ge(act_done, 1)
            did(v.tensor_tensor(small[:, :], prm[:, COL["c"]:COL["c"] + NB], sig[:, 0, 0:NB], ALU.mult))
            spread_c()
            lg = [prm[:, COL["hg_lb"] + 8 * i:COL["hg_lb"] + 8 * i + 8] for i in range(3)]
            did(v.tensor_tensor(lbt[:, 24:32], lg[0], lg[1], ALU.max))
            did(v.tensor_tensor(lbt[:, 24:32], lbt[:, 24:32], lg[2], ALU.max))
            for i in range(3):
                last = v.tensor_tensor(lbt[:, 8 * i:8 * i + 8], lg[i], lbt[:, 24:32], ALU.subtract)
            last.then_inc(lb_in, 1)
            dve.wait_ge(lb_exp, 1)
            did(v.tensor_tensor(lbt[:, 24:32], lbt[:, 0:8], lbt[:, 8:16], ALU.add))
            did(v.tensor_tensor(lbt[:, 24:32], lbt[:, 24:32], lbt[:, 16:24], ALU.add))
            did(v.reciprocal(lbt[:, 32:40], lbt[:, 24:32]))
            did(v.tensor_tensor(lbt[:, 24:32], lbt[:, 0:8], lbt[:, 32:40], ALU.mult))
            did(v.tensor_scalar(lbt[:, 32:40], lbt[:, 24:32], -1.0, 1.0, ALU.mult, ALU.add))

            centre(hres, acc, 0)
            for k in range(NB):
                add_square("ln_in", 0, k)

            def columns_of(name, unit_, b, first):
                multiplied(name, unit_)
                for j in range(NB):
                    v.scalar_tensor_tensor(diag[:, j % 2, 0:P], cut(bank[b + j // 4], j % 4), 1.0, ident[:, :],
                                           ALU.mult, ALU.mult, accum_out=mod[:, first + j:first + j + 1]
                                           ).then_inc(step, 1)
                    chain.n += 1
                    chain.wait()
                part = mod[:, first:first + NB]
                did(v.tensor_tensor(part, part, prm[:, COL["b_ada"] + first:COL["b_ada"] + first + NB], ALU.add))
                dve.sem_inc(freed, 8)

            diag = sq
            columns_of("ada", 7, 0, 0)
            recip("ln_in", rstd_pre[:, :])
            with chain.loop(NB, 1) as k:
                chain.did(v.tensor_tensor(blk(acc, k), blk(acc, k), rstd_pre[:, :], ALU.mult))
            columns_of("ada", 15, 2, 8)
            did(v.tensor_scalar(mod[:, 8:16], mod[:, 8:16], 1.0, None, ALU.add))
            with dve.Fori(0, 4) as r:
                for s in range(2):
                    j = r * 2 + s
                    v.tensor_scalar(blk(acc, j), blk(acc, j), mod[:, bass.ds(j + 8, 1)], mod[:, bass.ds(j, 1)],
                                    ALU.mult, ALU.add).then_inc(val_ready, 1)
                for s in range(2):
                    lo(blk(x_lo, r * 2 + s), blk(acc, r * 2 + s), blk(x_hi, r * 2 + s), "u", r * 2 + s)

            def taps(j, first, last):
                for t in range(first, last):
                    z, w = zpad[:, t:t + T], prm_col("cf_w", j * TAPS + t)
                    h = blk(hres, j)
                    if t == 0:
                        did(v.tensor_scalar(h, z, w, prm_col("cf_b", j), ALU.mult, ALU.add))
                    elif t < TAPS - 1:
                        did(v.scalar_tensor_tensor(h, z, w, h, ALU.mult, ALU.add))
                    else:
                        v.scalar_tensor_tensor(h, z, w, h, ALU.mult, ALU.add).then_inc(hc_ready, 1)

            def biased(o, j, i, by):
                return v.scalar_tensor_tensor(o, bank_of("proj", i), prm_col("b_in", j + 8 * BRANCH_UNITS[i]), by,
                                              ALU.add, ALU.mult)

            with chain.loop(NB, 34) as j:
                dve.wait_ge(hc_ready, j + 1)
                multiplied("proj", 1, j, 8)
                dve.wait_ge(act_done, j * 5 + 2)
                biased(zpad[:, TAPS - 1:], j, 1, sig[:, 0, :]).then_inc(freed, 2)
                dve.wait_ge(freed, j * 8 + (U0["proj"] + 2))
                taps(j, 0, 10)
                multiplied("proj", 3, j, 8)
                dve.wait_ge(act_done, j * 5 + 3)
                biased(qpad[:, 2:], j, 3, mean[:, :]).then_inc(freed, 2)
                dve.wait_ge(freed, j * 8 + (U0["proj"] + 4))
                conv = rstd_post[:, :]
                did(v.tensor_scalar(conv, qpad[:, 0:T], prm_col("sc_w", j * 3), prm_col("sc_b", j), ALU.mult, ALU.add))
                for t in (1, 2):
                    did(v.scalar_tensor_tensor(conv, qpad[:, t:t + T], prm_col("sc_w", j * 3 + t), conv,
                                               ALU.mult, ALU.add))
                taps(j, 10, 18)
                dve.wait_ge(act_done, j * 5 + 4)
                biased(tmp[:, 0, :], j, 4, sig[:, 1, :]).then_inc(freed, 1)
                multiplied("proj", 5, j, 8)
                dve.wait_ge(freed, j * 8 + (U0["proj"] + 5))
                biased(tmp[:, 1, :], j, 5, tmp[:, 0, :]).then_inc(freed, 1)
                dve.wait_ge(freed, j * 8 + (U0["proj"] + 6))
                v.tensor_tensor(sq[:, 0, :], tmp[:, 1, :], conv, ALU.mult).then_inc(val_ready, 1)
                taps(j, 18, 25)
                dve.wait_ge(act_done, j * 5 + 5)
                biased(blk(acc, j), j, 6, std[:, :]).then_inc(freed, 1)
                dve.wait_ge(freed, j * 8 + (U0["proj"] + 7))
                did(v.tensor_scalar(blk(acc, j), blk(acc, j), prm_col("pool_scale", j), None, ALU.mult))
                dve.wait_ge(act_done, j * 5 + 6)
                biased(blk(gate_c, j), j, 7, rstd_pre[:, :]).then_inc(freed, 1)
                taps(j, 25, TAPS)
                lo(blk(yb_lo, j), sq[:, 0, :], blk(yb_hi, j), "yb", j)

            ping = tmp[:, :, :].rearrange("p a n -> p (a n)")
            pong = sq[:, :, :].rearrange("p a n -> p (a n)")
            for j in range(NB):
                g = j // 2
                w = POOLS[g]
                front = w - 2
                if j == 0:
                    dve.wait_ge(hc_ready, NB + 1)
                multiplied("avp", j)
                v.tensor_scalar(zpad[:, TAPS - 1:], bank_of("avp", j), prm_col("b_in", j), None,
                                ALU.add).then_inc(freed, 1)
                dve.wait_ge(freed, U0["avp"] + j + 1)
                z0 = TAPS - 1
                did(v.tensor_tensor(ping[:, 0:T + front], zpad[:, z0 - front:z0 + T],
                                    zpad[:, z0 - front - 1:z0 + T - 1], ALU.add))
                src, dst, width, at = ping, pong, 2, front
                while width < w:
                    rest = at - width
                    did(v.tensor_tensor(dst[:, 0:T + rest], src[:, width:width + T + rest], src[:, 0:T + rest],
                                        ALU.add))
                    src, dst, width, at = dst, src, 2 * width, rest
                vals = sig[:, j % 2, :]
                z = zpad[:, z0:z0 + T]
                did(v.scalar_tensor_tensor(vals, src[:, 0:T], 1.0 / w, z, ALU.mult, ALU.subtract))
                ic = COL["inv_count"] + 16 * g
                did(v.tensor_tensor(vals[:, 0:w], src[:, 0:w], prm[:, ic:ic + w], ALU.mult))
                v.tensor_tensor(vals[:, 0:w], vals[:, 0:w], z[:, 0:w], ALU.subtract).then_inc(val_ready, 1)
                lo(ya_lo[:, j, :], vals, ya_hi[:, j, :], "ya", j)
            for j in range(NB):
                half, g, m = j // 4, j // 2, j % 2
                if j % 4 == 0:
                    dve.wait_ge(pool_mm, half + 1)
                if j % 4 == 2:
                    multiplied("avp", NB + half)
                vals = sig[:, j % 2, :]
                v.tensor_tensor(vals, bank[4 + 2 * (g % 2) + m][:, :], acc[:, j, :], ALU.mult).then_inc(val_ready, 1)
                lo(ya_lo[:, j, :], vals, ya_hi[:, j, :], "ya", NB + j)
                if j % 4 == 3:
                    dve.wait_ge(lo_ready, K0["ya"] + NB + j + 1)
                    dve.sem_inc(freed, 1)
            centre(hres, hres, 1)
            did(v.memset(std[:, :], 0.0))
            with dve.Fori(0, 4) as r:
                for i in range(2):
                    add_square("ln_c", r, i, 2)

            def merge(i):
                name = f"merge{i}"
                dve.wait_ge(freed, U0[name])
                with chain.loop(4, {1: 0, 0: 6, 2: 0}[i]) as r:
                    if i == 0:
                        for s in range(2):
                            v.tensor_tensor(blk(hres, r * 2 + s), blk(hres, r * 2 + s), rstd_post[:, :], ALU.mult
                                            ).then_inc(ln_ready, 1)
                        for s in range(2):
                            j = r * 2 + s
                            t = tmp[:, s, :]
                            dve.wait_ge(ln_ready, r * 2 + (s + 1))
                            did(v.tensor_scalar(t, blk(hres, j), prm_col("cf_ln_g", j), prm_col("cf_ln_b", j),
                                                ALU.mult, ALU.add))
                            dve.wait_ge(act_done, r * 4 + (A0[name] + s + 1))
                            did(v.tensor_tensor(t, t, (mean, std)[s][:, :], ALU.mult))
                            v.tensor_tensor(t, t, blk(gate_c, j), ALU.mult).then_inc(val_ready, 1)
                    for s in range(2):
                        j = r * 2 + s
                        multiplied(name, 2 * s + 1, r, 4)
                        product = (bank_of(name, 2 * s + 1), sig[:, s, :], ALU.mult)
                        if i == 0:
                            dve.wait_ge(act_done, r * 4 + (A0[name] + 2 + s + 1))
                        else:
                            dve.wait_ge(act_done, r * 2 + (A0[name] + s + 1))
                        if i == 1:
                            v.tensor_tensor(blk(acc, j), *product).then_inc(freed, 2)
                        if i == 0:
                            did(v.tensor_tensor(sig[:, s, :], *product))
                            v.tensor_tensor(blk(acc, j), blk(acc, j), sig[:, s, :], ALU.add).then_inc(freed, 2)
                            lo(blk(yb_lo, j), tmp[:, s, :], blk(yb_hi, j), "yc", j)
                        if i == 2:
                            v.tensor_tensor(sig[:, s, :], *product).then_inc(freed, 2)
                            dve.wait_ge(freed, r * 4 + (U0[name] + 2 * s + 2))
                            v.tensor_tensor(blk(acc, j), blk(acc, j), sig[:, s, :], ALU.add).then_inc(val_ready, 1)
                            lo(blk(ya_lo, j), blk(acc, j), blk(ya_hi, j), "m", j)

            merge(1)
            recip("ln_c", rstd_post[:, :])
            merge(0)
            spread_c()
            merge(2)
            columns_of("adag", 7, 0, 16)
            dve.wait_ge(x_in, 32)
            v.memset(std[:, :], 0.0).then_inc(r_ready, 1)
            with chain.loop(2, 4) as r:
                for i in range(4):
                    j = r * 4 + i
                    multiplied("wout", i, r, 4)
                    t = (tmp, sig)[i // 2][:, i % 2, :]
                    v.tensor_scalar(t, bank_of("wout", i), mod[:, bass.ds(j + 16, 1)], None, ALU.mult
                                    ).then_inc(freed, 1)
                    dve.wait_ge(freed, r * 4 + (U0["wout"] + i + 1))
                    did(v.scalar_tensor_tensor(blk(hres, j), blk(hres, j), ALPHA, t, ALU.mult, ALU.add))
                    dve.wait_ge(r_ready, j + 1)
                    v.tensor_tensor(std[:, :], std[:, :], blk(hres, j), ALU.add).then_inc(r_ready, 1)
            centre(hres, hres, 2)
            recip("ln_out", rstd_post[:, :])

            def two(r):
                for s in range(2):
                    j = r * 2 + s
                    v.scalar_tensor_tensor(tmp[:, s, :], blk(hres, j), prm_col("ln_g", j), rstd_post[:, :],
                                           ALU.mult, ALU.mult).then_inc(ln_ready, 1)
                for s in range(2):
                    j = r * 2 + s
                    dve.wait_ge(hi_ready, r * 2 + (K0["mix0"] + s + 1))
                    v.scalar_tensor_tensor(blk(x_lo, j), blk(hres, j), prm_col("pre_mix", j), blk(x_hi, j).bitcast(F32),
                                           ALU.mult, ALU.subtract).then_inc(lo_ready, 1)
                for s in range(2):
                    add_square("mix0", r, s, 2)

            two(0)
            with dve.Fori(1, 4) as r:
                two(r)
            recip("mix0", rstd_pre[:, :])

            v.memset(attn[:, 0, :], 0.0).then_inc(o_read, 1)
            did(v.memset(attn[:, 1, :], 0.0))
            dve.wait_ge(gla_in, 32)

            def head_query(h):
                multiplied("hg", 0, h, 4)
                v.scalar_tensor_tensor(hq[:, :], bank_of("hg", 0), float(P) ** -0.5, rstd_pre[:, :], ALU.mult, ALU.mult
                                       ).then_inc(freed, 1)

            def head(h):
                b = [bank_of("hg", i) for i in range(4)]
                for d in range(2):
                    multiplied("hg", 1 + d, h, 4)
                    v.tensor_tensor(hf[:, d, :], b[1 + d], rstd_pre[:, :], ALU.mult).then_inc(freed, 1)
                multiplied("hg", 3, h, 4)
                v.tensor_tensor(hvT[:, :], b[3], rstd_pre[:, :], ALU.mult).then_inc(freed, 1)
                at = lambda first: lbt[:, bass.ds(h + first, 1)] if not isinstance(h, int) else lbt[:, first + h:first + h + 1]
                for d in range(2):
                    dve.wait_ge(gla_act, h * 10 + (d + 1))
                    v.tensor_scalar(hf[:, d, :], hf[:, d, :], at(32), at(24), ALU.mult, ALU.add).then_inc(gla_dve, 1)
                    dve.wait_ge(gla_dve, h * 6 + (d + 1))
                    chain.did(v.tensor_scalar(hk[:, d, :], hf[:, d, :], -1.0, 1.0, ALU.mult, ALU.add))
                for d in range(2):
                    way = (slice(None), d, slice(None, None, -1) if d else slice(None))
                    dve.wait_ge(gla_act, h * 10 + (2 + d + 1))
                    v.tensor_tensor_scan(hG[way], reset[:, :], hg[way], 0.0, ALU.mult, ALU.add).then_inc(gla_dve, 1)
                for d in range(2):
                    dve.wait_ge(gla_dve, h * 6 + (2 + d + 1))
                    G = hG[:, d, :].rearrange("p (c t) -> p c t", t=CH)
                    end = G[:, :, 0:1] if d else G[:, :, CH - 1:CH]
                    v.tensor_tensor(hg[:, d, :].rearrange("p (c t) -> p c t", t=CH), end.to_broadcast([P, NCH, CH]), G,
                                    ALU.subtract).then_inc(gla_dve, 1)
                for d in range(2):
                    dve.wait_ge(gla_act, h * 10 + (4 + 3 * d + 2))
                    chain.did(v.tensor_tensor(hf[:, d, :], hq[:, :], hE[:, d, :], ALU.mult))
                    chain.wait()
                    v.tensor_tensor(hI[:, d, :], hk[:, d, :], hI[:, d, :], ALU.mult).then_inc(decayed, 1)
                    dve.wait_ge(gla_act, h * 10 + (4 + 3 * d + 3))
                    v.tensor_tensor(hg[:, d, :], hk[:, d, :], hg[:, d, :], ALU.mult).then_inc(kend_ready, 1)

            def scans(c, beside):
                for d in range(2):
                    dve.wait_ge(attn_mm, c * 2 - 1 + d)
                    v.memset(small[:, d:d + 1], 0.0)
                    v.copy_predicated(attn[:, d, :], mask[:, d, :], bank[7 - d][:, :]).then_inc(masked, 1)
                for d in range(2):
                    dve.wait_ge(kv_mm, c * 2 - 1 + d)
                    kv = lambda n: bank[4 + 2 * d + n % 2][:, n // 2 * P:(n // 2 + 1) * P]
                    order = list(range(NCH)) if d == 0 else list(range(NCH - 1, -1, -1))
                    for i in range(NCH - 1):
                        n, to = order[i], order[i + 1]
                        if i == 0:
                            ins_ = v.tensor_copy(state[:, d, to, :], kv(n))
                        else:
                            e = n * CH if d else n * CH + CH - 1
                            ins_ = v.scalar_tensor_tensor(state[:, d, to, :], state[:, d, n, :], hE[:, d, e:e + 1],
                                                          kv(n), ALU.mult, ALU.add)
                        if i == NCH - 2:
                            ins_.then_inc(states_done, 1)
                        else:
                            did(ins_)
                beside()
                dve.wait_ge(o_mm, c)
                v.tensor_copy(blk(acc, c - 1), bank[4][:, :]).then_inc(o_read, 1)

            GLA_HEAD, GLA_SCAN = 4, 12
            head_query(0)
            head(0)
            with chain.loop(HEADS - 1, GLA_HEAD + GLA_SCAN) as r:
                h = r + 1
                scans(h, lambda: head_query(h))
                head(h)

            def gate_out(i):
                multiplied("hggate", i)
                v.tensor_tensor(gate_o[i], bank_of("hggate", i), rstd_pre[:, :], ALU.mult).then_inc(freed, 1)

            def silu_gate(i):
                dve.wait_ge(gate_sig, i + 1)
                v.tensor_tensor(gate_o[i], gate_o[i], gate_s[i % 4], ALU.mult).then_inc(gate_ready, 1)

            def norm_o(h):
                dve.wait_ge(o_rstd, h + 1)
                v.scalar_tensor_tensor(acc[:, h, :], acc[:, h, :], prm_col("o_norm", h), o_scale[h],
                                       ALU.mult, ALU.mult).then_inc(o_normed, 1)

            def gated_o(h):
                dve.wait_ge(o_normed, h + 1)
                dve.wait_ge(gate_ready, h + 1)
                v.tensor_tensor(acc[:, h, :], acc[:, h, :], gate_o[h], ALU.mult).then_inc(val_ready, 1)

            def lo_o(h):
                lo(y_lo[:, h, :], acc[:, h, :], y_hi[:, h, :], "o", h)

            dve.wait_ge(kend_ready, 2 * HEADS)
            gate_out(0)
            gate_out(1)
            scans(HEADS, lambda: (gate_out(2), gate_out(3)))
            for i in range(4):
                silu_gate(i)
            for i in range(3):
                norm_o(2 * i)
                norm_o(2 * i + 1)
                if i:
                    gated_o(2 * i - 2)
                    gated_o(2 * i - 1)
                gate_out(4 + i)
                if i:
                    lo_o(2 * i - 2)
                    lo_o(2 * i - 1)
            norm_o(6)
            norm_o(7)
            for i in (4, 5, 6):
                silu_gate(i)
                gated_o(i)
            for h in (4, 5, 6):
                lo_o(h)
            gate_out(7)
            silu_gate(7)
            gated_o(7)
            lo_o(7)
            did(v.memset(std[:, :], 0.0))
            with dve.Fori(0, 2) as r:
                for i in range(4):
                    multiplied("hgout", i, r, 4)
                    v.tensor_copy(blk(acc, r * 4 + i), bank_of("hgout", i)).then_inc(freed, 1)
                    add_square("post_mix0", r, i)

            hblocks = {"mlp0": 1, "ple0": 2, "mix1": 3, "mlp1": 4, "ple1": 5, "end": 6}

            def residual(norm, gain, layer, name, next_gain, next_layer, first=lambda: None, beside=lambda: None):
                recip(norm, rstd_post[:, :])
                first()
                if name != "end":
                    dve.wait_ge(lo_ready, K0[name])

                def normed(r, s):
                    j = r * 2 + s
                    did(v.scalar_tensor_tensor(tmp[:, s, :], blk(acc, j), prm_col(gain, j + 8 * layer),
                                               rstd_post[:, :], ALU.mult, ALU.mult))

                def added(r, s):
                    j = r * 2 + s
                    v.tensor_tensor(blk(hres, j), blk(hres, j), tmp[:, s, :], ALU.add).then_inc(h_ready, 1)

                def rest_of(r, s):
                    j = r * 2 + s
                    if name == "end":
                        return
                    dve.wait_ge(hi_ready, j + (K0[name] + 1))
                    if next_gain:
                        v.scalar_tensor_tensor(blk(x_lo, j), blk(hres, j), prm_col(next_gain, j + 8 * next_layer),
                                               blk(x_hi, j).bitcast(F32), ALU.mult, ALU.subtract).then_inc(lo_ready, 1)
                    else:
                        v.tensor_tensor(blk(x_lo, j), blk(hres, j), blk(x_hi, j).bitcast(F32), ALU.subtract
                                        ).then_inc(lo_ready, 1)

                def two(r):
                    dve.wait_ge(h_ready, r * 2 + 8 * hblocks[name])
                    normed(r, 0)
                    added(r, 0)
                    normed(r, 1)
                    rest_of(r, 0)
                    added(r, 1)
                    rest_of(r, 1)
                    if name in TOTALS:
                        for s in range(2):
                            add_square(name, r, s, 2)

                two(0)
                beside()
                with chain.loop(3, 2) as r:
                    two(r + 1)

            def mlp(i):
                name = f"mlp{i}"
                residual(f"post_mix{i}", "post_mix", i, name, "pre_mlp", i)
                recip(name, rstd_pre[:, :])

                def quarter(q):
                    last = q == 3 if isinstance(q, int) else False
                    for u in range(8):
                        s = u % 2
                        dve.wait_ge(lo_ready, q * 8 + (K0[f"f{i}"] + u))
                        multiplied(name, u, q, 16)
                        v.scalar_tensor_tensor(tmp[:, s, :], bank_of(name, u), 0.0, rstd_pre[:, :], ALU.max, ALU.mult
                                               ).then_inc(freed, 1)
                        lo(y_lo[:, u, :], tmp[:, s, :], y_hi[:, u, :], f"f{i}", q * 8 + u)
                    if last:
                        dve.wait_ge(p_arrived, 16 * (i + 1))
                        for k in range(2):
                            lo(p_lo[:, k, :], p_in[:, k, :], p_hi[:, k, :], f"p{i}", k)
                    for u in range(8):
                        multiplied(name, 8 + u, q, 16)
                        if isinstance(q, int) and q == 0:
                            v.tensor_copy(acc[:, u, :], bank_of(name, 8 + u)).then_inc(freed, 1)
                            continue
                        v.tensor_tensor(acc[:, u, :], acc[:, u, :], bank_of(name, 8 + u), ALU.add).then_inc(freed, 1)
                        if last:
                            add_square(f"post_mlp{i}", 0, u)

                quarter(0)
                with dve.Fori(1, 3) as q:
                    quarter(q)
                quarter(3)

            def ple(i, nxt):
                def embedded(e):
                    multiplied(f"plee{i}", e)
                    for o in range(4):
                        last = v.tensor_copy(e_buf[:, 4 * e + o, :], bank[4 + o][:, :])
                    last.then_inc(freed, 1)

                residual(f"post_mlp{i}", "post_mlp", i, f"ple{i}", None, 0, lambda: embedded(0), lambda: embedded(1))
                name = f"pleg{i}"
                did(v.memset(std[:, :], 0.0))
                with dve.Fori(0, 2) as r:
                    for u in range(4):
                        j = r * 4 + u
                        dve.wait_ge(ple_sig, j + (8 * i + 1))
                        v.tensor_tensor(blk(acc, j), sig[:, u % 2, :], blk(e_buf, j), ALU.mult).then_inc(freed, 1)
                        add_square(f"post_ple{i}", r, u)
                residual(f"post_ple{i}", "ple_norm", i, nxt, "pre_mix", 1)

            mlp(0)
            ple(0, "mix1")
            recip("mix1", rstd_pre[:, :])

            def latent_out(i):
                multiplied("mlain", i)
                v.tensor_tensor(acc[:, i, :], bank_of("mlain", i), rstd_pre[:, :], ALU.mult).then_inc(freed, 1)

            for i in range(4):
                latent_out(i)
            dve.wait_ge(pos_in, 16)
            ang, n_turns = tmp[:, 0, :], tmp[:, 1, :]
            did(v.tensor_copy(ang, pos_i[:, :]))
            did(v.tensor_scalar(ang, ang, prm_col("inv_freq"), None, ALU.mult))
            for i, shift in enumerate((0.0, TWO_PI / 4)):
                o = (sin, cos)[i][:, :]
                did(v.tensor_scalar(n_turns, ang, 1.0 / TWO_PI, shift / TWO_PI, ALU.mult, ALU.add))
                did(v.tensor_scalar(n_turns, n_turns, ROUNDER, None, ALU.add))
                did(v.tensor_scalar(n_turns, n_turns, -ROUNDER, None, ALU.add))
                did(v.scalar_tensor_tensor(o, n_turns, -TWO_PI_PARTS[0], ang, ALU.mult, ALU.add))
                for part in TWO_PI_PARTS[1:]:
                    did(v.scalar_tensor_tensor(o, n_turns, -part, o, ALU.mult, ALU.add))
                did(v.tensor_scalar(o, o, shift, None, ALU.add))
                v.tensor_scalar(o, o, PI_LO, -PI_LO, ALU.min, ALU.max).then_inc(trig_arg, 1)
            latent_out(4)

            def latent_norm(ks, r):
                for k in ks:
                    gain = prm_col("q_norm", k) if k < 3 else prm_col("kv_norm", k - 3)
                    v.scalar_tensor_tensor(acc[:, k, :], acc[:, k, :], gain, r, ALU.mult, ALU.mult
                                           ).then_inc(val_ready, 1)

            dve.wait_ge(std_ready, STD0["cqkv"] + 1)
            did(v.reciprocal(tmp[:, 0, :], std[:, :]))
            latent_out(5)
            latent_norm(range(3), tmp[:, 0, :])
            for k in range(3):
                lo(cq_lo[:, k, :], acc[:, k, :], cq_hi[:, k, :], "cqkv", k)
            dve.wait_ge(std_ready, STD0["cqkv"] + 2)
            did(v.reciprocal(tmp[:, 1, :], sig[:, 0, :]))
            latent_norm(range(3, 5), tmp[:, 1, :])
            latent_out(6)
            for k in range(2):
                lo(ckv_lo[:, k, :], acc[:, 3 + k, :], ckv_hi[:, k, :], "cqkv", 3 + k)
            def rest(dst, value, hi, k):
                dve.wait_ge(hi_ready, k + 1)
                v.tensor_tensor(dst, value, hi.bitcast(F32), ALU.subtract).then_inc(lo_ready, 1)
            dve.wait_ge(trig, 2)
            did(v.tensor_scalar(sin[:, :], sin[:, :], prm_col("rope_sign"), None, ALU.mult))
            did(v.tensor_tensor(tmp[:, 0, :], acc[:, 5, :], cos[:, :], ALU.mult))
            did(v.tensor_tensor(tmp[:, 1, :], acc[:, 6, :], sin[:, :], ALU.mult))
            v.tensor_tensor(sig[:, 1, :], tmp[:, 0, :], tmp[:, 1, :], ALU.add).then_inc(val_ready, 1)
            lo(kr_lo[:, :], sig[:, 1, :], kr_hi[:, :], "kr", 0)

            def rope(done):
                dve.wait_ge(mm_done, done)
                chain.did(v.tensor_tensor(tmp[:, 0, :], bank[2][:, :], cos[:, :], ALU.mult))
                did(v.tensor_tensor(tmp[:, 1, :], bank[3][:, :], sin[:, :], ALU.mult))
                v.tensor_tensor(sig[:, 0, :], tmp[:, 0, :], tmp[:, 1, :], ALU.add).then_inc(val_ready, 1)

            def top(hp, i):
                s = i % 2
                dve.wait_ge(sc_mm, hp * 8 + (i + 1))
                did(v.tensor_reduce(small[:, 4 * s:4 * s + 1], bank[4 + s][:, :], AX_X, ALU.max))
                v.tensor_scalar(small[:, 4 * s + 1:4 * s + 2], small[:, 4 * s:4 * s + 1], -MLA_SCALE, None,
                                ALU.mult).then_inc(mx_ready, 1)

            def normed(hp, i):
                s = i % 2
                dve.wait_ge(exp_done, hp * 8 + (i + 1))
                did(v.reciprocal(small[:, 4 * s + 3:4 * s + 4], small[:, 4 * s + 2:4 * s + 3]))
                v.tensor_scalar(probs[:, s, :], probs[:, s, :], small[:, 4 * s + 3:4 * s + 4], None,
                                ALU.mult).then_inc(p_ready, 1)

            def queries(k, query_banks, key_banks):
                def one(name):
                    if name == "qr":
                        rest(qr_lo[:, :], sig[:, 0, :], qr_hi[:, :], k(name))
                    elif name[0] == "K":
                        e = int(name[1])
                        rest(K_lo[:, e, :], bank[key_banks[e]][:, :], K_hi[:, e, :], k(name))
                    else:
                        e = int(name[2])
                        rest(qn_lo[:, e, :], bank[query_banks[e]][:, :], qn_hi[:, e, :], k(name))
                return one

            def first_queries(n):
                one = queries(lambda name: K0[f"pairs{n}"] + AHEAD.index(name), (0, 1), (4, 5))
                for name in AHEAD:
                    if name == "qr":
                        rope(U0[f"heads{n}"] + 1)
                    one(name)
                for i in range(2):
                    top(4 * n, i)
                normed(4 * n, 0)

            def head_pair(j, n, last_pair=False):
                hp = j + 4 * n
                nxt = not last_pair
                order = CUTS_LAST if last_pair else CUTS

                def k(name):
                    return j * PAIR + (K0[f"pairs{n}"] + len(AHEAD) + order.index(name))

                query = queries(lambda name: k(name + "n"), (2, 1), (3, 0))

                def pt(i):
                    part = slice(i % 4 * P, (i % 4 + 1) * P)
                    rest(pt_lo[:, :, part], bank[6 + i % 2][:, :].rearrange("p (k n) -> p k n", n=P),
                         pt_hi[:, :, part], k(f"P{i}"))

                def o(e):
                    rest(blk(x_lo, j * 2 + e), bank[2 * e][:, :], blk(x_hi, j * 2 + e), k(f"o{e}"))

                def V(half):
                    rest(V_lo[:, 2 * half:2 * half + 2, :], bank[half][:, :].rearrange("p (k n) -> p k n", n=2 * P),
                         V_hi[:, 2 * half:2 * half + 2, :], k("V" + "ab"[half]))

                top(hp, 2)
                normed(hp, 1)
                pt(0)
                V(0)
                top(hp, 3)
                normed(hp, 2)
                pt(1)
                V(1)
                top(hp, 4)
                normed(hp, 3)
                pt(2)
                if nxt:
                    query("qn0")
                top(hp, 5)
                normed(hp, 4)
                pt(3)
                if nxt:
                    query("K0")
                top(hp, 6)
                normed(hp, 5)
                top(hp, 7)
                normed(hp, 6)
                o(0)
                pt(4)
                pt(5)
                normed(hp, 7)
                if nxt:
                    rope(j * 4 + (U0[f"heads{n}"] + 5))
                pt(6)
                if nxt:
                    query("qn1")
                    query("qr")
                pt(7)
                if nxt:
                    query("K1")
                o(1)
                if nxt:
                    top(hp + 1, 0)
                    top(hp + 1, 1)
                    normed(hp + 1, 0)

            for n in range(2):
                first_queries(n)
                with chain.loop(3, 18) as j:
                    head_pair(j, n)
                head_pair(3, n, last_pair=True)
                dve.wait_ge(lo_ready, K0[f"pairs{n}"] + 4 * PAIR)
                dve.sem_inc(freed, 16)
                if n == 0:
                    with dve.Fori(0, 2) as r:
                        for i in range(4):
                            multiplied("wo0", i, r, 4)
                            v.tensor_copy(blk(acc, r * 4 + i), bank_of("wo0", i)).then_inc(freed, 1)
                else:
                    did(v.memset(std[:, :], 0.0))
                    with dve.Fori(0, 2) as r:
                        for i in range(4):
                            multiplied("wo1", i, r, 4)
                            v.tensor_tensor(blk(acc, r * 4 + i), blk(acc, r * 4 + i), bank_of("wo1", i), ALU.add
                                            ).then_inc(freed, 1)
                            add_square("post_mix1", r, i)
            mlp(1)
            ple(1, "end")


def blocks(w):
    k, n = w.shape
    return w.reshape(k // P, P, n // P, P).transpose(2, 1, 0, 3)


def as_units(w):
    b = blocks(w)
    return b.reshape(b.shape[0], P, UNIT)


def weight_stream(a):
    w_in = as_units(a["w_in"][0]).reshape(12, NB, P, UNIT)
    ada = a["w_ada"][0].reshape(NB, P, 3, D).transpose(2, 0, 1, 3).reshape(24, P, UNIT)
    parts = [ada[:16], np.stack([w_in[p] for p in BRANCH_UNITS], 1).reshape(64, P, UNIT)]
    pool = blocks(a["pool_w"][0].reshape(4 * 256, 256))
    pool = pool.reshape(2, P, 4, 2, P).transpose(2, 1, 3, 0, 4)
    parts += [w_in[0]] + [pool[g:g + 2].transpose(1, 0, 2, 3, 4).reshape(1, P, UNIT) for g in (0, 2)]
    for i in (1, 0, 2):
        parts.append(np.stack([w_in[9 + i], as_units(a["w_branch"][0, i])], 1).reshape(16, P, UNIT))
    parts += [ada[16:], as_units(a["w_out"][0])]
    hg = as_units(a["hg_w_in_2"][0]).reshape(5, NB, P, UNIT)
    parts += [np.stack([hg[p] for p in range(4)], 1).reshape(32, P, UNIT), hg[4], as_units(a["hg_w_out_2"][0])]

    def mlp(i):
        w1 = as_units(a["w_mlp_in_2"][i]).reshape(4, 8, P, UNIT)
        w2 = np.stack([as_units(a["w_mlp_out_2"][i][q * D:(q + 1) * D]) for q in range(4)])
        e = blocks(a["w_ple_proj_2"][i]).reshape(2, 4, P, 2, P).transpose(0, 2, 1, 3, 4).reshape(2, P, UNIT)
        return [np.stack([w1, w2], 1).reshape(64, P, UNIT), e, as_units(a["w_ple_gate_2"][i])]

    parts += mlp(0)
    w = a["mla_w_in_2"][0]
    kr = w[:, 640:704]
    ks = np.concatenate([kr[:, 32:], kr[:, :32]], 1)
    parts.append(as_units(np.concatenate([w[:, :640], kr, kr, ks, ks], 1)))
    uq = a["mla_w_uq_2"][0].reshape(384, MH, 192)
    ukv = a["mla_w_ukv_2"][0].reshape(256, MH, 256)
    swap = np.concatenate([uq[:, :, 160:192], uq[:, :, 128:160]], 2)
    pad = np.zeros((P, 4, P), np.float32)
    wo = a["mla_w_o_2"][0]
    for half in range(2):
        a_b_d, c_ = [], []
        for h in range(8 * half, 8 * half + 8, 2):
            nope = [blocks(uq[:, h + e, :128])[0] for e in range(2)]
            rope = [blocks(x.reshape(384, P))[0] for x in (uq[:, h:h + 2, 128:], swap[:, h:h + 2])]
            uk = [blocks(ukv[:, h + e, :128])[0] for e in range(2)]
            uv = blocks(ukv[:, h:h + 2, 128:].reshape(256, 2 * P)).transpose(1, 2, 0, 3).reshape(P, 4, P)
            unit = [np.concatenate([*x, pad[:, :8 - sum(y.shape[1] for y in x)]], 1) for x in (rope, nope, uk, [uv])]
            a_b_d.append(unit[:3])
            c_.append(unit[3])
        order = a_b_d[0] + [x for j in range(3) for x in (c_[j], *a_b_d[j + 1])] + [c_[3]]
        parts.append(np.stack(order).reshape(16, P, UNIT))
        parts.append(as_units(wo[half * D:(half + 1) * D]))
    parts += mlp(1)
    return np.ascontiguousarray(np.concatenate(parts))


def columns(v):
    return v.reshape(-1, P).T


def lay_out(a):
    t = np.arange(16)
    inv = (1.0 / (np.float32(10000.0) ** (np.arange(0, 64, 2, dtype=np.float32) / np.float32(64)))).astype(np.float32)
    by_name = {
        "b_ada": columns(a["b_ada"]), "b_in": columns(a["b_in"]), "pool_scale": columns(a["pool_scale"]),
        "sc_w": a["sc_w"][0].reshape(3, NB, P).transpose(2, 1, 0).reshape(P, -1), "sc_b": columns(a["sc_b"]),
        "cf_w": a["cf_w"][0].reshape(TAPS, NB, P).transpose(2, 1, 0).reshape(P, -1), "cf_b": columns(a["cf_b"]),
        "cf_ln_g": columns(a["cf_ln_g"]), "cf_ln_b": columns(a["cf_ln_b"]), "ln_g": columns(a["ln_g"]),
        "ln_b": columns(a["ln_b"]), "pre_mix": columns(a["pre_mix_norm_2"]), "post_mix": columns(a["post_mix_norm_2"]),
        "pre_mlp": columns(a["pre_mlp_norm_2"]), "post_mlp": columns(a["post_mlp_norm_2"]),
        "ple_norm": columns(a["ple_norm_2"]), "hg_lb": columns(a["hg_lb_logits_2"]),
        "o_norm": columns(a["hg_o_norm_2"]), "q_norm": columns(a["mla_q_norm_2"]), "kv_norm": columns(a["mla_kv_norm_2"]),
        "inv_freq": np.tile(inv, 4)[:, None], "rope_sign": np.tile(np.repeat([-1.0, 1.0], 32), 2)[:, None],
        "c": columns(a["c"]),
        "inv_count": np.tile(np.concatenate([1.0 / np.minimum(t + 1, w) for w in POOLS]), (P, 1)),
    }
    params = np.concatenate([by_name[n].astype(np.float32) for n, _ in PARAMS], 1)
    assert params.shape == (P, NCOL)

    def turned(x):
        return np.ascontiguousarray(x.T.reshape(-1, P, T).transpose(1, 0, 2))

    tok = np.arange(P)
    same = tok[:, None] // CH == tok[None, :] // CH
    fwd = same & (tok[:, None] <= tok[None, :])
    bwd = same & (tok[:, None] >= tok[None, :])
    mask = np.stack([np.tile(fwd, (1, 4)), np.tile(bwd, (1, 4))], 1).astype(np.int32)
    return {
        "weights": weight_stream(a), "x": turned(a["x"][0]), "params": np.ascontiguousarray(params),
        "ident": np.eye(P, dtype=np.float32), "mask": mask,
        "reset": np.tile((np.arange(T) % CH != 0).astype(np.float32), (P, 1)),
        "p0": turned(a["p_2"][0, 0]), "p1": turned(a["p_2"][1, 0]), "positions": a["positions_2"].reshape(T),
    }


def kernel(**inputs):
    import concourse.bacc as _bacc
    from concourse.bass_utils import run_bass_kernel_spmd as _run

    arrays = lay_out({n: np.asarray(v) for n, v in inputs.items()})
    nc = _bacc.Bacc("TRN2", target_bir_lowering=False, num_devices=1, dynamic_dma_scratch_size=1024)
    ins = {n: nc.dram_tensor(f"{n}_dram", v.shape, mybir.dt.from_np(v.dtype), kind="ExternalInput").ap()
           for n, v in arrays.items()}
    out = nc.dram_tensor("out", (NB, P, T), F32, kind="ExternalOutput").ap()
    build(nc, ins, out)
    r = _run(nc, [{f"{n}_dram": v for n, v in arrays.items()}], core_ids=[0])
    return r.results[0]["out"].reshape(D, T).T.reshape(1, T, D)
```
